# Optimizing a Trainium2 kernel written in Bass

```python
import math
import jax
import jax.numpy as jnp
from jax import lax
import numpy as np

D_MODEL = 2048
BATCH = 1
SEQ = 512
DEPTH = 1

ATTN_HEAD_DIM = 128
ATTN_WIDTH = D_MODEL // 2
N_ATTN_HEADS = ATTN_WIDTH // ATTN_HEAD_DIM
POOL_WIDTH = D_MODEL // 4
POOL_WINDOWS = (2, 4, 8, 16)
POOL_GROUP = POOL_WIDTH // len(POOL_WINDOWS)
LRU_WIDTH = D_MODEL // 4
N_LRU_BLOCKS = 4
LRU_BLOCK = LRU_WIDTH // N_LRU_BLOCKS
LRU_C = 8.0
CONV_WIDTH = 4
N_IDX_HEADS = 16
IDX_DIM = 64
TOPK_MAX = 256
QUERY_BLOCK = 128
N_BUCKETS = 32
MAX_DISTANCE = 128
MLP_HIDDEN = 4 * D_MODEL
NORM_EPS = 1e-6
COLUMN_SIZES = (ATTN_WIDTH, ATTN_WIDTH, ATTN_WIDTH, N_IDX_HEADS * IDX_DIM, IDX_DIM,
                N_IDX_HEADS, POOL_WIDTH, LRU_WIDTH, LRU_WIDTH)
IN_WIDTH = 3 * ATTN_WIDTH + N_IDX_HEADS * IDX_DIM + IDX_DIM + N_IDX_HEADS + POOL_WIDTH + 2 * LRU_WIDTH

kernel_name = 'hybrid_dsa_pool_rglru_block'

def rms_norm(x, g):
    xf = x.astype(jnp.float32)
    y = xf * lax.rsqrt(jnp.mean(xf * xf, axis=-1, keepdims=True) + NORM_EPS)
    return (y * g.astype(jnp.float32)).astype(x.dtype)

def split_columns(proj):
    out = []
    start = 0
    for size in COLUMN_SIZES:
        out.append(proj[..., start:start + size])
        start += size
    return out

def t5_bucket(rel):
    max_exact = N_BUCKETS // 2
    rel = jnp.maximum(rel, 0)
    relf = jnp.maximum(rel.astype(jnp.float32), 1.0)
    large = max_exact + (jnp.log(relf / max_exact) / math.log(MAX_DISTANCE / max_exact)
                         * (N_BUCKETS - max_exact)).astype(jnp.int32)
    large = jnp.minimum(large, N_BUCKETS - 1)
    return jnp.where(rel < max_exact, rel, large)

def dsa_attention(q, k, v, q_idx, k_idx, w_idx, positions, rel_bias):
    B, L = q.shape[0], q.shape[1]
    top_k = min(TOPK_MAX, L // 4)
    qb = min(QUERY_BLOCK, L)
    n_blocks = L // qb
    scale = ATTN_HEAD_DIM ** -0.5
    idx_scale = (N_IDX_HEADS * IDX_DIM) ** -0.5
    k_idx_f = k_idx.astype(jnp.float32)
    gather = jax.vmap(lambda arr, ids: arr[ids])

    def block(start):
        qs = lax.dynamic_slice_in_dim(q, start, qb, axis=1)
        qi = lax.dynamic_slice_in_dim(q_idx, start, qb, axis=1)
        wi = lax.dynamic_slice_in_dim(w_idx, start, qb, axis=1)
        pq = lax.dynamic_slice_in_dim(positions, start, qb, axis=1)
        dots = jnp.einsum('bqhd,bsd->bqhs', qi.astype(jnp.float32), k_idx_f)
        score = jnp.einsum('bqh,bqhs->bqs', wi.astype(jnp.float32), jax.nn.relu(dots)) * idx_scale
        admissible = positions[:, None, :] <= pq[:, :, None]
        score = jnp.where(admissible, score, -jnp.inf)
        _, sel = lax.top_k(score, top_k)
        valid = jnp.take_along_axis(admissible, sel, axis=-1)
        k_sel = gather(k, sel)
        v_sel = gather(v, sel)
        pos_sel = gather(positions, sel)
        bias = rel_bias[t5_bucket(pq[:, :, None] - pos_sel)]
        logits = (jnp.einsum('bqhd,bqkhd->bhqk', qs, k_sel).astype(jnp.float32) * scale
                  + jnp.transpose(bias.astype(jnp.float32), (0, 3, 1, 2)))
        logits = jnp.where(valid[:, None, :, :], logits, -jnp.inf)
        p = jax.nn.softmax(logits, axis=-1).astype(v.dtype)
        out = jnp.einsum('bhqk,bqkhd->bqhd', p, v_sel)
        return out.reshape(B, qb, -1)

    outs = lax.map(block, jnp.arange(n_blocks, dtype=jnp.int32) * qb)
    return jnp.transpose(outs, (1, 0, 2, 3)).reshape(B, L, -1)

def pool_mixer(u, pool_w, pool_scale):
    B, L, C = u.shape
    uf = u.astype(jnp.float32)
    cs = jnp.concatenate([jnp.zeros((B, 1, C), jnp.float32), jnp.cumsum(uf, axis=1)], axis=1)
    t = jnp.arange(L)
    diffs = []
    for g, win in enumerate(POOL_WINDOWS):
        sl = slice(g * POOL_GROUP, (g + 1) * POOL_GROUP)
        csg = cs[:, :, sl]
        lo = jnp.maximum(t + 1 - win, 0)
        count = jnp.minimum(t + 1, win).astype(jnp.float32)
        diffs.append((csg[:, 1:] - csg[:, lo]) / count[None, :, None] - uf[:, :, sl])
    d = jnp.stack(diffs, axis=2)
    y = jnp.einsum('blgc,gcd->blgd', d, pool_w.astype(jnp.float32)).reshape(B, L, C)
    return (y * pool_scale.astype(jnp.float32)).astype(u.dtype)

def rglru_mixer(u, gate, conv_w, conv_b, r_w, r_b, i_w, i_b, lam):
    B, L, C = u.shape
    xc = lax.conv_general_dilated(u, conv_w[:, None, :], window_strides=(1,),
                                  padding=[(CONV_WIDTH - 1, 0)],
                                  dimension_numbers=('NWC', 'WIO', 'NWC'),
                                  feature_group_count=C) + conv_b
    xb = xc.reshape(B, L, N_LRU_BLOCKS, LRU_BLOCK)
    r = jax.nn.sigmoid(jnp.einsum('blgc,gcd->blgd', xb, r_w).reshape(B, L, C) + r_b)
    i = jax.nn.sigmoid(jnp.einsum('blgc,gcd->blgd', xb, i_w).reshape(B, L, C) + i_b)
    log_a = -LRU_C * r.astype(jnp.float32) * jax.nn.softplus(-lam.astype(jnp.float32))
    a = jnp.exp(log_a)
    b = jnp.sqrt(-jnp.expm1(2.0 * log_a)) * (i * xc).astype(jnp.float32)

    def combine(left, right):
        a1, b1 = left
        a2, b2 = right
        return a1 * a2, a2 * b1 + b2

    _, h = lax.associative_scan(combine, (a, b), axis=1)
    return (h * jax.nn.gelu(gate.astype(jnp.float32))).astype(u.dtype)

def setup_inputs(seed: int = 0) -> dict:
    key = jax.random.key(seed)
    ks = jax.random.split(key, 28)
    f32 = jnp.float32
    D = D_MODEL

    def nrm(k, shape, s):
        return jax.random.normal(k, shape, f32) * s

    def gain(k, n):
        return 1.0 + nrm(k, (DEPTH, n), 0.05)

    x = nrm(ks[0], (BATCH, SEQ, D), 1.0)
    c = nrm(ks[1], (BATCH, D), 1.0)
    offset = jax.random.randint(ks[2], (BATCH, 1), 0, 4096, dtype=jnp.int32)
    positions = offset + jnp.arange(SEQ, dtype=jnp.int32)[None, :]
    rel_bias = nrm(ks[3], (N_BUCKETS, N_ATTN_HEADS), 0.5)
    w_mod = nrm(ks[4], (DEPTH, D, 6 * D), 0.5 * D ** -0.5)
    b_mod = nrm(ks[5], (DEPTH, 6 * D), 0.01)
    g_pre_mix = gain(ks[6], D)
    g_post_mix = gain(ks[7], D)
    g_pre_mlp = gain(ks[8], D)
    g_post_mlp = gain(ks[9], D)
    w_in = nrm(ks[10], (DEPTH, D, IN_WIDTH), D ** -0.5)
    pool_w = nrm(ks[11], (DEPTH, len(POOL_WINDOWS), POOL_GROUP, POOL_GROUP), POOL_GROUP ** -0.5)
    pool_scale = 1.0 + nrm(ks[12], (DEPTH, POOL_WIDTH), 0.1)
    conv_w = nrm(ks[13], (DEPTH, CONV_WIDTH, LRU_WIDTH), CONV_WIDTH ** -0.5)
    conv_b = nrm(ks[14], (DEPTH, LRU_WIDTH), 0.01)
    gate_r_w = nrm(ks[15], (DEPTH, N_LRU_BLOCKS, LRU_BLOCK, LRU_BLOCK), LRU_BLOCK ** -0.5)
    gate_r_b = nrm(ks[16], (DEPTH, LRU_WIDTH), 0.1)
    gate_i_w = nrm(ks[17], (DEPTH, N_LRU_BLOCKS, LRU_BLOCK, LRU_BLOCK), LRU_BLOCK ** -0.5)
    gate_i_b = nrm(ks[18], (DEPTH, LRU_WIDTH), 0.1)
    a_c = jax.random.uniform(ks[19], (DEPTH, LRU_WIDTH), f32, 0.9, 0.999)
    s = a_c ** (1.0 / LRU_C)
    lru_lambda = jnp.log(s) - jnp.log1p(-s)
    g_attn_out = gain(ks[20], ATTN_WIDTH)
    g_pool_out = gain(ks[21], POOL_WIDTH)
    g_lru_out = gain(ks[22], LRU_WIDTH)
    w_out = nrm(ks[23], (DEPTH, D, D), D ** -0.5)
    w_mlp_up = nrm(ks[24], (DEPTH, D, MLP_HIDDEN), D ** -0.5)
    w_mlp_down = nrm(ks[25], (DEPTH, MLP_HIDDEN, D), MLP_HIDDEN ** -0.5)
    return {'x': x, 'c': c, 'positions': positions, 'rel_bias': rel_bias,
            'w_mod': w_mod, 'b_mod': b_mod,
            'g_pre_mix': g_pre_mix, 'g_post_mix': g_post_mix,
            'g_pre_mlp': g_pre_mlp, 'g_post_mlp': g_post_mlp,
            'w_in': w_in, 'pool_w': pool_w, 'pool_scale': pool_scale,
            'conv_w': conv_w, 'conv_b': conv_b,
            'gate_r_w': gate_r_w, 'gate_r_b': gate_r_b,
            'gate_i_w': gate_i_w, 'gate_i_b': gate_i_b, 'lru_lambda': lru_lambda,
            'g_attn_out': g_attn_out, 'g_pool_out': g_pool_out, 'g_lru_out': g_lru_out,
            'w_out': w_out, 'w_mlp_up': w_mlp_up, 'w_mlp_down': w_mlp_down}

def reference(x, c, positions, rel_bias, w_mod, b_mod, g_pre_mix, g_post_mix, g_pre_mlp,
              g_post_mlp, w_in, pool_w, pool_scale, conv_w, conv_b, gate_r_w, gate_r_b,
              gate_i_w, gate_i_b, lru_lambda, g_attn_out, g_pool_out, g_lru_out, w_out,
              w_mlp_up, w_mlp_down):
    B, L, _ = x.shape
    c_act = jax.nn.silu(c)
    for l in range(DEPTH):
        mod = c_act @ w_mod[l] + b_mod[l]
        shift1, scale1, gate1, shift2, scale2, gate2 = [m[:, None, :] for m in jnp.split(mod, 6, axis=-1)]

        h = rms_norm(x, g_pre_mix[l]) * (1.0 + scale1) + shift1
        proj = h @ w_in[l]
        q, k, v, q_idx, k_idx, w_idx, pool_in, lru_in, lru_gate = split_columns(proj)
        attn = dsa_attention(q.reshape(B, L, N_ATTN_HEADS, ATTN_HEAD_DIM),
                             k.reshape(B, L, N_ATTN_HEADS, ATTN_HEAD_DIM),
                             v.reshape(B, L, N_ATTN_HEADS, ATTN_HEAD_DIM),
                             q_idx.reshape(B, L, N_IDX_HEADS, IDX_DIM), k_idx, w_idx,
                             positions, rel_bias)
        pool = pool_mixer(pool_in, pool_w[l], pool_scale[l])
        lru = rglru_mixer(lru_in, lru_gate, conv_w[l], conv_b[l], gate_r_w[l], gate_r_b[l],
                          gate_i_w[l], gate_i_b[l], lru_lambda[l])
        mixed = jnp.concatenate([rms_norm(attn, g_attn_out[l]),
                                 rms_norm(pool, g_pool_out[l]),
                                 rms_norm(lru, g_lru_out[l])], axis=-1)
        y = mixed @ w_out[l]
        x = x + gate1 * rms_norm(y, g_post_mix[l])

        h = rms_norm(x, g_pre_mlp[l]) * (1.0 + scale2) + shift2
        u = jax.nn.relu(h @ w_mlp_up[l])
        y = (u * u) @ w_mlp_down[l]
        x = x + gate2 * rms_norm(y, g_post_mlp[l])
    return x


_drawn_inputs = setup_inputs


def setup_inputs(seed=0):
    import zlib

    import numpy as np

    out = dict(_drawn_inputs(seed))
    spreads = {}
    factors = {'b_mod': 2.963,
     'g_post_mix': 3.571,
     'g_pre_mlp': 3.557,
     'g_post_mlp': 3.785,
     'pool_scale': 3.887,
     'conv_b': 8.0,
     'gate_r_w': 2.711,
     'gate_r_b': 8.0,
     'gate_i_b': 8.0,
     'g_attn_out': 5.53,
     'g_pool_out': 7.835,
     'g_lru_out': 8.0}
    for name, (base, spread) in spreads.items():
        noise = np.random.default_rng([zlib.crc32(name.encode()), seed]).standard_normal(out[name].shape)
        drawn = base * np.exp(spread * noise) if base else spread * noise
        out[name] = jnp.asarray(drawn.astype(out[name].dtype))
    for name, factor in factors.items():
        out[name] = (out[name] * factor).astype(out[name].dtype)
    return out
```

```python
from contextlib import ExitStack

import numpy as np
import concourse.bass as bass
from concourse import mybir

F32 = mybir.dt.float32
F32R = mybir.dt.float32r
BF16 = mybir.dt.bfloat16
I32 = mybir.dt.int32
ALU = mybir.AluOpType
ACT = mybir.ActivationFunctionType
AXX = mybir.AxisListType.X

P = 128
D = 2048
T = 512
KD = D // P
TT = T // P
HEADS, HD = 8, 128
AW = HEADS * HD
IH, ID = 16, 64
GW = 512
CT = GW // P
TOPK = min(256, T // 4)
ROUNDS = TOPK // 8
HIDDEN = 4 * D
NBUCKET, MAXDIST = 32, 128
EPS = 1e-6
LRU_C = 8.0
NEG = -1e30
TAKEN = -3e38

C_Q, C_K, C_V, C_QI = 0, AW, 2 * AW, 3 * AW
C_KI = C_QI + IH * ID
C_WI = C_KI + ID
C_POOL = C_WI + IH
C_LRU = C_POOL + GW
C_GATE = C_LRU + GW

RING = 4
KS = 2
SG = KD // KS
G_KW, G_QI, G_LRU, G_GATE, G_POOL, G_K, G_Q, G_V = 0, 1, 3, 4, 5, 6, 8, 10
PROJ_GROUPS = 12
PROJ_SLABS = PROJ_GROUPS * SG
OUT_SLABS = TT * SG
MLP0 = PROJ_SLABS + OUT_SLABS
CHUNK = 1024
STEPS = HIDDEN // CHUNK
HT = CHUNK // P
UPG, DNG = CHUNK // 512, D // 512
DS = HT // KS
STEP_SLABS = UPG * SG + DNG * DS

SHIFT1, SCALE1, GATE1, SHIFT2, SCALE2, GATE2 = range(6)
MOD_ORDER = [SCALE1, SHIFT1, GATE1, SCALE2, SHIFT2, GATE2]
MOD_EARLY = 2 * KD
MOD_PROJ = 3 * KD

STAGES = (
    [("vec", "D")] + [(f"bias{n}", "A") for n in range(8)] + [("mod0", "D"), ("mod1", "D")]
    + [(f"ht{n}", "AD") for n in range(KD // 4)]
    + [("g0", "AD"), ("g1", "AD"), ("g2", "AD"), ("widx", "D"), ("mod2", "D")]
    + [(f"dots{n}", "A") for n in range(TT * IH // 4)]
    + [("g3", "A"), ("g4", "A"), ("mod3", "D"), ("rgate", "A"), ("igate", "A"), ("g5", "A"), ("g6", "A"),
       ("mod4", "D"), ("g7", "A"), ("poolmm", "A"), ("g8", "A"), ("ssq", "A"), ("g9", "A"), ("g10", "AD"),
       ("g11", "AD")]
    + [(f"out{n}", "AD") for n in range(TT)] + [("mod5", "D")]
    + [(f"h2t{n}", "AD") for n in range(KD // 4)]
)
STAGE = {name: n for n, (name, _) in enumerate(STAGES)}


GROUP_OF = {f"g{g}": g for g in range(PROJ_GROUPS)} | {f"out{d}": PROJ_GROUPS + d for d in range(TT)}

CONV_DONE, U_ARG, SCANNED, GELU_ARG, LRU_DONE, POOL_DIFF = range(1, 7)
BRANCH_SQ = 10
TOPK_AT = 34
UP0 = 2


def freed(who, n):
    return sum(who in by for _, by in STAGES[:n])


def bucket_starts():
    exact = NBUCKET // 2
    return [b if b < exact else int(np.ceil(exact * (MAXDIST / exact) ** ((b - exact) / (NBUCKET - exact)) - 1e-9))
            for b in range(NBUCKET)]


def build(nc, x, c, positions, rel_bias, w_mod, b_mod, g_pre_mix, g_post_mix, g_pre_mlp, g_post_mlp, w_in,
          pool_w, pool_scale, conv_w, conv_b, gate_r_w, gate_r_b, gate_i_w, gate_i_b, lru_lambda,
          g_attn_out, g_pool_out, g_lru_out, w_out, w_mlp_up, w_mlp_down, out):
    def rows(w):
        return w.rearrange("a (t p) n -> p (a t) n", p=P)

    def vec_rows(v):
        return v.rearrange("a (r p) -> (a r) p", p=P)

    x_d, out_d = rows(x), rows(out)
    w_mod_d, w_in_d, w_out_d = rows(w_mod), rows(w_in), rows(w_out)
    w_up_d, w_down_d = rows(w_mlp_up), rows(w_mlp_down)
    bias_s = nc.dram_tensor("bias_s", (T * HEADS, T), F32, kind="Internal").ap()
    gate_s = nc.dram_tensor("gate_s", (2, D), F32, kind="Internal").ap()
    x1_s = nc.dram_tensor("x1_s", (P, TT, D), F32, kind="Internal").ap()
    bias_h = bias_s.rearrange("(q t h) k -> h q t k", q=P, t=TT)

    b_rows = vec_rows(b_mod)
    vec_a_rows = [("g_pre1", vec_rows(g_pre_mix)), ("g_pre2", vec_rows(g_pre_mlp)),
                  ("b_mod0", b_rows[SCALE1 * KD:(SCALE1 + 1) * KD]), ("b_mod1", b_rows[SHIFT1 * KD:(SHIFT1 + 1) * KD]),
                  ("b_mod3", b_rows[SCALE2 * KD:(SCALE2 + 1) * KD]), ("b_mod4", b_rows[SHIFT2 * KD:(SHIFT2 + 1) * KD]),
                  ("c", vec_rows(c))]
    vec_b_rows = [("conv_w", conv_w.rearrange("a j (r p) -> (a j r) p", p=P)), ("conv_b", vec_rows(conv_b)),
                  ("r_b", vec_rows(gate_r_b)), ("i_b", vec_rows(gate_i_b)), ("lam", vec_rows(lru_lambda)),
                  ("pool_scale", vec_rows(pool_scale)), ("g_attn", vec_rows(g_attn_out)),
                  ("g_pool", vec_rows(g_pool_out)), ("g_lru", vec_rows(g_lru_out)),
                  ("b_mod2", b_rows[GATE1 * KD:(GATE1 + 1) * KD]), ("b_mod5", b_rows[GATE2 * KD:(GATE2 + 1) * KD]),
                  ("g_post1", vec_rows(g_post_mix)), ("g_post2", vec_rows(g_post_mlp))]
    at_a, at_b = {}, {}
    for at, table in ((at_a, vec_a_rows), (at_b, vec_b_rows)):
        n = 0
        for name, v in table:
            at[name] = n
            n += v.shape[0]
        assert n <= P
    n_small = len(vec_a_rows) + len(vec_b_rows)

    with ExitStack() as ctx:
        def sb(name, shape, dt):
            return ctx.enter_context(nc.sbuf_tensor(name, shape, dt))

        def sem(name):
            return ctx.enter_context(nc.semaphore(name))

        raw = sb("raw", [P, RING, KS, 512], F32)
        w_hi = sb("w_hi", [P, RING, KS, 512], F32R)
        w_lo = sb("w_lo", [P, RING, KS, 512], F32R)
        ident = sb("ident", [P, P], F32)
        ones = sb("ones", [P, P], F32)
        col_a = sb("col_a", [P, P], F32)
        col_b = sb("col_b", [P, P], F32)
        pos_k = sb("pos_k", [P, T], F32)
        pos_q = sb("pos_q", [P, TT], F32)
        start_col = sb("start_col", [P, 1], F32)
        rb = sb("rb", [P, HEADS], F32)
        rb_prev = sb("rb_prev", [P, HEADS], F32)
        rb_step = sb("rb_step", [P, HEADS], F32)
        c_act = sb("c_act", [P, KD], F32)
        c_tmp = sb("c_tmp", [P, KD], F32)
        mod = sb("mod", [P, 6, KD], F32)
        mul = sb("mul", [P, 2, KD], F32)
        w_idx = sb("w_idx", [P, TT, IH], F32)
        lam_t = sb("lam_t", [P, 8, CT], F32)
        half_b = sb("half_b", [P, 2, CT], F32)
        stat = sb("stat", [P, 8, 16], F32)
        eps_c = sb("eps_c", [P, 1], F32)
        inv_n = sb("inv_n", [P, 16], F32)
        pool_fix = sb("pool_fix", [P, CT, 16], F32)
        top8 = sb("top8", [P, 8], F32)
        amax = sb("amax", [P, 3], F32)
        nmax = sb("nmax", [P, 3], F32)
        asum = sb("asum", [P, 3], F32)
        arec = sb("arec", [P, 3], F32)

        def at(kb, name, shape, dt):
            with ExitStack() as e:
                if kb:
                    e.enter_context(nc.sbuf_tensor(f"below_{name}", [P, int(kb * 256)], F32))
                return e.enter_context(nc.sbuf_tensor(name, shape, dt))

        bias_out = at(0, "bias_out", [P, 2, T], F32)
        steps = at(4, "steps", [P, 4, T], F32R)
        junk = at(20, "junk", [P, D], F32)
        vec_a = at(28, "vec_a", [P, P], F32)
        vec_b = at(28.5, "vec_b", [P, P], F32)
        pos_qi = at(29, "pos_qi", [P, P], I32)
        pos_qf = at(29.5, "pos_qf", [P, P], F32)
        start_row = at(30, "start_row", [P, P], F32)
        reach = at(30.5, "reach", [P, P], F32)
        x_tok = at(84, "x_tok", [P, TT, D], F32)
        blk = at(116, "blk", [P, 4, P], F32)
        blk_hi = at(118, "blk_hi", [P, 4, P], F32R)
        blk_lo = at(120, "blk_lo", [P, 4, P], F32R)
        pos_ki = at(148, "pos_ki", [P, T], I32)
        acc_a = at(124, "acc_a", [P, D], F32)
        acc_b = at(12, "acc_b", [P, D], F32)
        mod_slab = at(132, "mod_slab", [P, 2, D], F32)
        h_full = at(0, "h_full", [P, 2, T], F32)
        h_hi = at(20, "h_hi", [P, KD, T], F32R)
        h_lo = at(52, "h_lo", [P, KD, T], F32R)
        score = at(4, "score", [P, TT, T], F32)
        qi_hi = at(84, "qi_hi", [P, IH // 2, T], F32R)
        qi_lo = at(100, "qi_lo", [P, IH // 2, T], F32R)
        ki_hi = at(116, "ki_hi", [P, T], F32R)
        ki_lo = at(118, "ki_lo", [P, T], F32R)
        relu = at(120, "relu", [P, 2, T], F32)
        widx_t = at(148, "widx_t", [P, T], F32)
        late = at(150, "late", [P, T], F32)
        gates_w = at(0, "gates_w", [P, 2, CT, P], F32)
        gate_in = at(84, "gate_in", [P, CT, T], F32)
        xc = at(92, "xc", [P, CT, T], F32)
        lru_in = at(100, "lru_in", [P, CT, T], F32)
        r_t = at(108, "r_t", [P, CT, T], F32)
        i_t = at(116, "i_t", [P, CT, T], F32)
        PAD = 8
        pool_u = at(84, "pool_u", [P, CT, PAD + T], F32)
        pool_b = at(93, "pool_b", [P, CT, PAD + T], F32)
        pool_c = at(102, "pool_c", [P, CT, PAD + T], F32)
        pool_ws = at(122, "pool_ws", [P, CT, P], F32)
        pool_sq = at(111, "pool_sq", [P, CT, T], F32)
        lru_sq = at(84, "lru_sq", [P, CT, T], F32)
        rnorm = at(148, "rnorm", [P, 2, T], F32)
        mask = at(0, "mask", [P, TT, T], BF16)
        pool_o = at(4, "pool_o", [P, CT, T], F32)
        lru_o = at(12, "lru_o", [P, CT, T], F32)
        v_hi = at(84, "v_hi", [P, TT, AW], F32R)
        v_lo = at(100, "v_lo", [P, TT, AW], F32R)
        q_t = at(116, "q_t", [P, HEADS, T], F32)
        k_t = at(132, "k_t", [P, HEADS, T], F32)
        attn = at(20, "attn", [P, HEADS, T], F32)
        bm = at(36, "bm", [P, 2, TT, T], F32)
        q_hi = at(52, "q_hi", [P, 2, T], F32R)
        q_lo = at(56, "q_lo", [P, 2, T], F32R)
        k_hi = at(60, "k_hi", [P, 2, T], F32R)
        k_lo = at(64, "k_lo", [P, 2, T], F32R)
        probs = at(68, "probs", [P, 3, T], F32)
        pt_hi = at(74, "pt_hi", [P, 2, TT, P], F32R)
        pt_lo = at(78, "pt_lo", [P, 2, TT, P], F32R)
        attn_sq = at(82, "attn_sq", [P, T], F32)
        m_hi = at(84, "m_hi", [P, KD, T], F32R)
        m_lo = at(116, "m_lo", [P, KD, T], F32R)
        x_in = at(20, "x_in", [P, 2, D], F32)
        y1 = at(36, "y1", [P, TT, D], F32)
        g1_bc = at(68, "g1_bc", [P, D], F32)
        slab_0 = at(4, "slab_0", [P, D], F32)
        slab_1 = at(76, "slab_1", [P, D], F32)
        sq_out = at(148, "sq_out", [P, T], F32)
        h2_hi = at(84, "h2_hi", [P, KD, T], F32R)
        h2_lo = at(116, "h2_lo", [P, KD, T], F32R)
        y2 = at(20, "y2", [P, TT, D], F32)
        u2_hi = at(52, "u2_hi", [P, HT, T], F32R)
        u2_lo = at(68, "u2_lo", [P, HT, T], F32R)
        u_relu = at(0, "u_relu", [P, 2, T], F32)
        u_sq = at(4, "u_sq", [P, 2, T], F32)
        g2_bc = at(12, "g2_bc", [P, D], F32)
        x1_in = at(84, "x1_in", [P, TT, D], F32)
        junk2 = at(116, "junk2", [P, D], F32)

        psum = ctx.enter_context(nc.psum_tensor("psum", [P, 8, 512], F32))

        def bank(stage, b):
            return psum[:, 4 * (stage % 2) + b, :]

        raw_landed = [sem(f"raw_landed{i}") for i in range(RING)]
        hi_ready, lo_pool, lo_dve, slab_used = sem("hi_ready"), sem("lo_pool"), sem("lo_dve"), sem("slab_used")
        stage_done, act_freed, dve_freed = sem("stage_done"), sem("act_freed"), sem("dve_freed")
        dve_chain, act_chain, pool_chain = sem("dve_chain"), sem("act_chain"), sem("pool_chain")
        small_in, pos_in, x_landed = sem("small_in"), sem("pos_in"), [sem(f"x_landed{t}") for t in range(TT)]
        mod_landed, mod_step = [sem("mod_landed0"), sem("mod_landed1")], sem("mod_step")
        consts, rb_in, blk_ready, reach_ready = sem("consts"), sem("rb_in"), sem("blk_ready"), sem("reach_ready")
        step_dve, step_pool, step_used = sem("step_dve"), sem("step_pool"), sem("step_used")
        bias_stored = [sem("bias_stored0"), sem("bias_stored1")]
        vec_ready, c_tanh, c_ready = sem("vec_ready"), sem("c_tanh"), sem("c_ready")
        ssq_ready, root_ready, rinv_ready, xn_ready = sem("ssq_ready"), sem("root_ready"), sem("rinv_ready"), sem("xn_ready")
        mul_ready, h_hi_ready, h_ready = sem("mul_ready"), sem("h_hi_ready"), sem("h_ready")
        act_hi = sem("act_hi")
        idx_ready, widx_copied = sem("idx_ready"), sem("widx_copied")
        relu_ready, relu_used, score_done = sem("relu_ready"), sem("relu_used"), sem("score_done")
        gates_in, pool_in = sem("gates_in"), sem("pool_in")
        branch_act, branch_dve = sem("branch_act"), sem("branch_dve")
        mask_done, gate_col, gate_stored, g_landed = sem("mask_done"), sem("gate_col"), sem("gate_stored"), sem("g_landed")
        pool_fixed = sem("pool_fixed")
        bias_landed = [sem("bias_landed0"), sem("bias_landed1")]
        bm_ready, bm_used = sem("bm_ready"), sem("bm_used")
        qk_hi, qk_lo = sem("qk_hi"), sem("qk_lo")
        s_done, max_ready, exp_ready, probs_ready, pt_done, pt_hi_ready, pt_lo_ready = (
            sem("s_done"), sem("max_ready"), sem("exp_ready"), sem("probs_ready"), sem("pt_done"),
            sem("pt_hi_ready"), sem("pt_lo_ready"))
        pv_done, o_ready, sq_ready, sq_used = sem("pv_done"), sem("o_ready"), sem("sq_ready"), sem("sq_used")
        mixed_full, mixed_hi, mixed_ready = sem("mixed_full"), sem("mixed_hi"), sem("mixed_ready")
        x_again, x1_ready, x1_stored = [sem("x_again0"), sem("x_again1")], sem("x1_ready"), [sem(f"x1_stored{t}") for t in range(TT)]
        up_relu, up_used, u2_ready = sem("up_relu"), sem("up_used"), sem("u2_ready")
        x1_back, final_ready, out_stored = sem("x1_back"), sem("final_ready"), sem("out_stored")

        class Chain:

            def __init__(self, eng, counter):
                self.eng, self.counter, self.n = eng, counter, 0

            def put(self, instruction):
                instruction.then_inc(self.counter, 1)
                self.n += 1
                return self.n

            def wait(self, n=None):
                self.eng.wait_ge(self.counter, self.n if n is None else n)

            def link(self, instruction):
                self.put(instruction)
                self.wait()

        def slab_source(s):
            g, j = divmod(s, SG)
            k = slice(KS * j, KS * j + KS)
            if g == G_KW:
                return w_in_d[:, k, C_KI:C_KI + 192], 192
            if g < PROJ_GROUPS:
                col = {G_QI: C_QI, G_QI + 1: C_QI + 512, G_LRU: C_LRU, G_GATE: C_GATE, G_POOL: C_POOL, G_K: C_K,
                       G_K + 1: C_K + 512, G_Q: C_Q, G_Q + 1: C_Q + 512, G_V: C_V, G_V + 1: C_V + 512}[g]
                return w_in_d[:, k, col:col + 512], 512
            col = 512 * (g - PROJ_GROUPS)
            return w_out_d[:, k, col:col + 512], 512

        def wait_lo(eng, s):
            if s < PROJ_SLABS:
                eng.wait_ge(lo_pool, s + 1)
            else:
                eng.wait_ge(lo_dve, s - PROJ_SLABS + 1)

        def wait_stage(eng, name):
            if name in GROUP_OF:
                eng.wait_ge(slab_used, SG * (GROUP_OF[name] + 1))
            elif name.startswith("bias"):
                eng.wait_ge(step_used, 16 * (int(name[4:]) + 1))
            else:
                counted = [k for k, _ in STAGES if k not in GROUP_OF and not k.startswith("bias")]
                eng.wait_ge(stage_done, counted.index(name) + 1)

        def store_gate(eng, k):
            with nc.allow_non_contiguous_dma(reason="2048 elements"):
                eng.dma_start(gate_s[k:k + 1, :].rearrange("a (r p) -> p (a r)", p=P),
                              mod[:, (2, 5)[k], :]).then_inc(gate_stored, 16)

        block = ctx.enter_context(nc.Block())

        @block.sync
        def _(sp):
            def load_slab(s):
                if s >= RING:
                    wait_lo(sp, s - RING)
                src, n = slab_source(s)
                sp.dma_start(raw[:, s % RING, :, 0:n], src).then_inc(raw_landed[s % RING], 16)

            def load_mod(g):
                j, k = divmod(g, KD)
                if g >= 2:
                    sp.wait_ge(mod_step, g - 1)
                m = MOD_ORDER[j]
                if j == 5:
                    dst = (slab_0, slab_1)[g % 2][:]
                else:
                    dst = mod_slab[:, g % 2, :]
                sp.dma_start(dst, w_mod_d[:, k, D * m:D * (m + 1)]).then_inc(mod_landed[g % 2], 16)

            n = 0
            for v, table in ((vec_a, vec_a_rows), (vec_b, vec_b_rows)):
                n = 0
                for _, src in table:
                    sp.dma_start(v[n:n + src.shape[0], :], src).then_inc(small_in, 16)
                    n += src.shape[0]
            sp.dma_start(pos_ki[:], positions[0:1, :].to_broadcast([P, T])).then_inc(pos_in, 16)
            sp.dma_start(pos_qi[0:TT, :], positions.rearrange("a (r p) -> (a r) p", p=P)).then_inc(pos_in, 16)
            sp.wait_ge(consts, 1)
            for q in range(4):
                sp.dma_start(rb[32 * q:32 * q + NBUCKET, :], rel_bias).then_inc(rb_in, 16)
                sp.dma_start(rb_prev[32 * q + 1:32 * q + NBUCKET, :], rel_bias[0:NBUCKET - 1, :]).then_inc(rb_in, 16)
            for g in range(MOD_EARLY):
                load_mod(g)
                if g in (8, 11, 14, 17):
                    t = (g - 8) // 3
                    sp.dma_start(x_tok[:, t, :], x_d[:, t, :]).then_inc(x_landed[t], 16)
            for s in range(2):
                load_slab(s)
            for s in range(PROJ_SLABS):
                if s < MOD_PROJ:
                    load_mod(MOD_EARLY + s)
                load_slab(s + 2)
                if s == 24:
                    sp.wait_ge(h_ready, KD)
                    for k, w in enumerate((gate_r_w, gate_i_w)):
                        sp.dma_start(gates_w[:, k, :, :], w.rearrange("a g c d -> c (a g) d")).then_inc(gates_in, 16)
                if s == 34:
                    sp.wait_ge(gate_col, 1)
                    store_gate(sp, 0)
                if s == 50:
                    sp.wait_ge(branch_dve, LRU_DONE)
                    sp.dma_start(pool_ws[:], pool_w.rearrange("a g c d -> c (a g) d")).then_inc(pool_in, 16)

            load_slab(PROJ_SLABS + 2)
            load_slab(PROJ_SLABS + 3)
            for h in range(HEADS):
                if h == 0:
                    wait_stage(sp, "g11")
                if h >= 2:
                    sp.wait_ge(bm_used, TT * (h - 1))
                sp.dma_start(bm[:, h % 2, :, :], bias_h[h]).then_inc(bias_landed[h % 2], 16)

            for s in range(PROJ_SLABS, MLP0):
                k = s - PROJ_SLABS
                if s + RING < MLP0:
                    load_slab(s + RING)
                if k == 0:
                    sp.wait_ge(gate_stored, 16)
                    sp.wait_ge(pt_lo_ready, HEADS * TT)
                    sp.wait_ge(pv_done, HEADS * TT)
                    sp.dma_start(g1_bc[:], gate_s[0:1, :].to_broadcast([P, D])).then_inc(g_landed, 16)
                    sp.wait_ge(mixed_ready, KD)
                if k % 2 == 0:
                    load_mod(5 * KD + k // 2)
                if k in (1, 3):
                    t = k // 2
                    sp.dma_start(x_in[:, t, :], x_d[:, t, :]).then_inc(x_again[t], 16)
            for t in range(TT):
                sp.wait_ge(x1_ready, t + 1)
                sp.dma_start(x1_s[:, t, :], y1[:, t, :]).then_inc(x1_stored[t], 16)
                if t + 2 < TT:
                    sp.dma_start(x_in[:, t % 2, :], x_d[:, t + 2, :]).then_inc(x_again[t % 2], 16)
                if t == 1:
                    sp.wait_ge(gate_col, 2)
                    store_gate(sp, 1)

            def load_mlp(s, i, local):
                wait_count = MLP0 - PROJ_SLABS - RING + 1 + local
                sp.wait_ge(lo_dve, i * STEP_SLABS + wait_count)
                if local < UPG * SG:
                    g, j = divmod(local, SG)
                    src = w_up_d[:, KS * j:KS * j + KS, bass.ds(i * CHUNK + 512 * g, 512)]
                else:
                    g, j = divmod(local - UPG * SG, DS)
                    src = w_down_d[:, bass.ds(i * HT + KS * j, KS), 512 * g:512 * g + 512]
                sp.dma_start(raw[:, s % RING, :, :], src).then_inc(raw_landed[s % RING], 16)

            with sp.Fori(0, STEPS) as i:
                for local in range(STEP_SLABS):
                    load_mlp(MLP0 + local, i, local)
            sp.wait_ge(gate_stored, 32)
            sp.dma_start(g2_bc[:], gate_s[1:2, :].to_broadcast([P, D])).then_inc(g_landed, 16)
            for t in range(TT):
                sp.wait_ge(x1_stored[t], 16)
            sp.wait_ge(slab_used, MLP0 + STEP_SLABS * (STEPS - 1) + UPG * SG)
            sp.dma_start(x1_in[:], x1_s).then_inc(x1_back, 16)
            for t in range(TT):
                sp.wait_ge(final_ready, t + 1)
                sp.dma_start(out_d[:, t, :], x1_in[:, t, :]).then_inc(out_stored, 16)
            sp.wait_ge(out_stored, 16 * TT)
            sp.wait_ge(bias_stored[0], 16 * T // 32)
            sp.wait_ge(bias_stored[1], 16 * T // 32)

        @block.gpsimd
        def _(pool):
            ch = Chain(pool, pool_chain)
            nc.gpsimd.memset(rb_prev[:], 0.0).then_inc(consts, 1)
            ch.put(nc.gpsimd.memset(ident[:], 0.0))
            ch.put(nc.gpsimd.memset(blk[:], 0.0))
            starts = bucket_starts()
            row = start_row[0:1, :].rearrange("a (q b) -> a b q", q=4)
            for b in range(NBUCKET):
                ch.put(nc.gpsimd.memset(row[:, b, :], float(starts[b])))
            for n in range(16):
                ch.put(nc.gpsimd.memset(inv_n[:, n:n + 1], 1.0 / (n + 1)))
            ch.put(nc.gpsimd.memset(eps_c[:], EPS))
            ch.put(nc.gpsimd.memset(ones[:], 1.0))
            ch.wait()
            ch.link(nc.gpsimd.affine_select(out=ident[:], in_=ident[:], compare_op=ALU.not_equal, fill=1.0, base=0,
                                            pattern=[[-1, P]], channel_multiplier=1))
            pool.wait_ge(rb_in, 16 * 8)
            ch.link(nc.gpsimd.tensor_tensor(rb_step[:], rb[:], rb_prev[:], ALU.subtract))
            for q in range(4):
                for j in range(4):
                    o = 32 * j + 8 * q
                    ch.put(nc.gpsimd.tensor_copy(blk[32 * q:32 * q + 32, j, o:o + 8], rb_step[32 * q:32 * q + 32, :]))
            ch.wait()
            ch.link(nc.gpsimd.tensor_copy(blk_hi[:], blk[:]))
            nc.gpsimd.tensor_tensor(blk_lo[:], blk[:], blk_hi[:].bitcast(F32), ALU.subtract).then_inc(blk_ready, 1)
            pool.wait_ge(blk_ready, 1)
            nc.gpsimd.memset(stat[:], 0.0).then_inc(consts, 1)
            pool.wait_ge(reach_ready, 1)
            for n in range(3, P, 4):
                if n >= 4:
                    pool.wait_ge(step_used, n - 3)
                nc.gpsimd.tensor_scalar(steps[:, n % 4, :], pos_k[:], reach[:, n:n + 1], None,
                                        ALU.is_le).then_inc(step_pool, 1)
            for s in range(PROJ_SLABS):
                pool.wait_ge(hi_ready, s + 1)
                r, hi, lo = raw[:, s % RING, :, :], w_hi[:, s % RING, :, :], w_lo[:, s % RING, :, :]
                if s < SG:
                    ch.put(nc.gpsimd.tensor_tensor(lo[:, :, 0:64], r[:, :, 0:64], hi[:, :, 0:64].bitcast(F32), ALU.subtract))
                    ch.wait()
                    r, hi, lo = r[:, :, 0:192], hi[:, :, 64:256], lo[:, :, 64:256]
                nc.gpsimd.tensor_tensor(lo, r, hi.bitcast(F32), ALU.subtract).then_inc(lo_pool, 1)
            pool.wait_ge(mask_done, TT)
            for h in range(HEADS + 1):
                if h < HEADS:
                    pool.wait_ge(bias_landed[h % 2], 16 * (h // 2 + 1))
                    nc.gpsimd.tensor_tensor(bm[:, h % 2, :, :], bm[:, h % 2, :, :], mask[:], ALU.add).then_inc(bm_ready, 1)
                if h >= 1:
                    pool.wait_ge(o_ready, h)
                    if h >= 2:
                        pool.wait_ge(sq_used, h - 1)
                    nc.gpsimd.tensor_tensor(attn_sq[:], attn[:, h - 1, :], attn[:, h - 1, :], ALU.mult).then_inc(sq_ready, 1)

        @block.tensor
        def _(pe):
            def begin(n):
                if n >= 2:
                    if freed("A", n - 1):
                        pe.wait_ge(act_freed, freed("A", n - 1))
                    if freed("D", n - 1):
                        pe.wait_ge(dve_freed, freed("D", n - 1))

            def three(o, a_hi, a_lo, b_hi, b_lo, first, last):
                nc.tensor.matmul(o, a_hi, b_hi, start=first, stop=False)
                nc.tensor.matmul(o, a_hi, b_lo, start=False, stop=False)
                return nc.tensor.matmul(o, a_lo, b_hi, start=False, stop=last)

            def weights(slot, j, cols):
                return w_hi[:, slot, j, cols], w_lo[:, slot, j, cols]

            def features_out(stage, slot, j, act, kt, nk, tiles=4):
                for b in range(tiles):
                    last = three(bank(stage, b), *weights(slot, j, slice(P * b, P * b + P)),
                                 act[0][:, kt, :], act[1][:, kt, :], kt == 0, kt == nk - 1)
                return last

            def tokens_out(stage, slot, j, act, kt, nk):
                for b in range(TT):
                    tok = slice(P * b, P * b + P)
                    last = three(bank(stage, b), act[0][:, kt, tok], act[1][:, kt, tok],
                                 *weights(slot, j, slice(0, 512)), kt == 0, kt == nk - 1)
                return last

            def group(g, stage, emit, act, ready=None, **how):
                begin(stage)
                for j in range(SG):
                    s = g * SG + j
                    wait_lo(pe, s)
                    for k in range(KS):
                        if ready is not None:
                            pe.wait_ge(ready, KS * j + k + 1)
                        last = emit(stage, s % RING, k, act, KS * j + k, KD, **how)
                    last.then_inc(slab_used, 1)

            def mod_sum(j):
                n = STAGE[f"mod{j}"]
                begin(n)
                pe.wait_ge(mod_step, KD * (j + 1))
                acc = acc_b if j % 2 else acc_a
                for k in range(KD):
                    last = nc.tensor.matmul(bank(n, 0)[:, k:k + 1], acc[:, P * k:P * k + P], ones[:, 0:1],
                                            start=True, stop=True)
                last.then_inc(stage_done, 1)

            def transposed(n, src, k0):
                begin(n)
                for b in range(4):
                    for t in range(TT):
                        last = nc.tensor.transpose(bank(n, b)[:, P * t:P * t + P],
                                                   src[:, t, P * (k0 + b):P * (k0 + b) + P], ident[:])
                last.then_inc(stage_done, 1)

            pe.wait_ge(small_in, 16 * n_small)
            pe.wait_ge(pos_in, 32)
            pe.wait_ge(blk_ready, 1)
            pe.wait_ge(vec_ready, 1)
            n = STAGE["vec"]
            na, nb = sum(v.shape[0] for _, v in vec_a_rows), sum(v.shape[0] for _, v in vec_b_rows)
            nc.tensor.transpose(bank(n, 0)[:, 0:na], vec_a[0:na, :], ident[0:na, 0:na])
            nc.tensor.transpose(bank(n, 1)[:, 0:nb], vec_b[0:nb, :], ident[0:nb, 0:nb])
            nc.tensor.transpose(bank(n, 2)[:, 0:TT], pos_qf[0:TT, :], ident[0:TT, 0:TT])
            nc.tensor.matmul(bank(n, 3)[:, 0:1], start_row[0:1, :], ones[0:1, 0:1], start=True,
                             stop=True).then_inc(stage_done, 1)

            for m in range(8):
                n = STAGE[f"bias{m}"]
                begin(n)
                for b in range(4):
                    for j in range(4):
                        k = 16 * m + 4 * b + j
                        if j < 3:
                            pe.wait_ge(step_dve, 3 * (k // 4) + j + 1)
                        else:
                            pe.wait_ge(step_pool, k // 4 + 1)
                        nc.tensor.matmul(bank(n, b), blk_hi[:, j, :], steps[:, k % 4, :], start=j == 0, stop=False)
                        last = nc.tensor.matmul(bank(n, b), blk_lo[:, j, :], steps[:, k % 4, :], start=False, stop=j == 3)
                        last.then_inc(step_used, 1)

            mod_sum(0)
            mod_sum(1)
            pe.wait_ge(xn_ready, TT)
            for k in range(KD // 4):
                transposed(STAGE[f"ht{k}"], x_tok, 4 * k)

            h = (h_hi, h_lo)
            group(G_KW, STAGE["g0"], features_out, h, ready=h_ready, tiles=2)
            group(G_QI, STAGE["g1"], features_out, h)
            group(G_QI + 1, STAGE["g2"], features_out, h)
            n = STAGE["widx"]
            begin(n)
            pe.wait_ge(widx_copied, 1)
            for t in range(TT):
                last = nc.tensor.transpose(bank(n, 0)[:, IH * t:IH * t + IH], widx_t[0:IH, P * t:P * t + P],
                                           ident[0:IH, 0:IH])
            last.then_inc(stage_done, 1)
            mod_sum(2)
            pe.wait_ge(idx_ready, 1 + IH // 2)
            for m in range(TT * IH // 4):
                n = STAGE[f"dots{m}"]
                begin(n)
                t = m // (IH // 4)
                for b in range(4):
                    hd = 4 * (m % (IH // 4)) + b
                    rows_ = slice(64 * (hd % 2), 64 * (hd % 2) + 64)
                    tok = slice(P * t, P * t + P)
                    last = three(bank(n, b), qi_hi[rows_, hd // 2, tok], qi_lo[rows_, hd // 2, tok],
                                 ki_hi[rows_, :], ki_lo[rows_, :], True, True)
                last.then_inc(stage_done, 1)
            group(G_LRU, STAGE["g3"], features_out, h)
            group(G_GATE, STAGE["g4"], features_out, h)
            mod_sum(3)
            pe.wait_ge(gates_in, 32)
            pe.wait_ge(branch_dve, CONV_DONE)
            for k, name in enumerate(("rgate", "igate")):
                n = STAGE[name]
                begin(n)
                for b in range(CT):
                    last = nc.tensor.matmul(bank(n, b), gates_w[:, k, b, :], xc[:, b, :], start=True, stop=True)
                last.then_inc(stage_done, 1)
            group(G_POOL, STAGE["g5"], features_out, h)
            group(G_K, STAGE["g6"], features_out, h)
            mod_sum(4)
            group(G_K + 1, STAGE["g7"], features_out, h)
            n = STAGE["poolmm"]
            begin(n)
            pe.wait_ge(pool_in, 16)
            pe.wait_ge(branch_dve, POOL_DIFF)
            for b in range(CT):
                last = nc.tensor.matmul(bank(n, b), pool_ws[:, b, :], (pool_b, pool_c)[b % 2][:, b, PAD:], start=True,
                                        stop=True)
            last.then_inc(stage_done, 1)
            group(G_Q, STAGE["g8"], features_out, h)
            n = STAGE["ssq"]
            begin(n)
            pe.wait_ge(branch_act, BRANCH_SQ)
            for b, sq in enumerate((pool_sq, lru_sq)):
                for t in range(CT):
                    last = nc.tensor.matmul(bank(n, b), ones[:], sq[:, t, :], start=t == 0, stop=t == CT - 1)
            last.then_inc(stage_done, 1)
            group(G_Q + 1, STAGE["g9"], features_out, h)
            group(G_V, STAGE["g10"], tokens_out, h)
            group(G_V + 1, STAGE["g11"], tokens_out, h)

            pe.wait_ge(act_freed, freed("A", STAGE["g11"] + 1))
            pe.wait_ge(dve_freed, freed("D", STAGE["g11"] + 1))

            def scores_of(it):
                hd, t = divmod(it, TT)
                if t == 0:
                    pe.wait_ge(qk_lo, hd + 1)
                if it >= 3:
                    pe.wait_ge(max_ready, it - 2)
                tok = slice(P * t, P * t + P)
                three(psum[:, it % 3, :], q_hi[:, hd % 2, tok], q_lo[:, hd % 2, tok], k_hi[:, hd % 2, :],
                      k_lo[:, hd % 2, :], True, True).then_inc(s_done, 1)

            def transpose_of(it):
                pe.wait_ge(probs_ready, it + 1)
                if it >= 2:
                    pe.wait_ge(pt_lo_ready, it - 1)
                for k in range(TT):
                    last = nc.tensor.transpose(psum[:, 3 + it % 2, P * k:P * k + P],
                                               probs[:, it % 3, P * k:P * k + P], ident[:])
                last.then_inc(pt_done, 1)

            def values_of(it):
                hd, t = divmod(it, TT)
                if t == 0 and hd >= 2:
                    pe.wait_ge(o_ready, hd - 1)
                pe.wait_ge(pt_lo_ready, it + 1)
                cols = slice(HD * hd, HD * hd + HD)
                o = psum[:, 5 + hd % 2, P * t:P * t + P]
                for k in range(TT):
                    last = three(o, v_hi[:, k, cols], v_lo[:, k, cols], pt_hi[:, it % 2, k, :], pt_lo[:, it % 2, k, :],
                                 k == 0, k == TT - 1)
                last.then_inc(pv_done, 1)

            def square_sum(hd):
                pe.wait_ge(sq_ready, hd + 1)
                nc.tensor.matmul(psum[:, 7, :], ones[:], attn_sq[:], start=hd == 0, stop=hd == HEADS - 1).then_inc(sq_used, 1)

            n_it = HEADS * TT
            for it in range(n_it + 4):
                if it < n_it:
                    scores_of(it)
                if 0 <= it - 2 < n_it:
                    transpose_of(it - 2)
                if 0 <= it - 3 < n_it:
                    values_of(it - 3)
                    if (it - 3) % TT == 2 and it - 3 > TT:
                        square_sum((it - 3) // TT - 1)
            square_sum(HEADS - 1)

            pe.wait_ge(o_ready, HEADS)
            for d in range(TT):
                if d == 0:
                    pe.wait_ge(root_ready, 3)
                group(PROJ_GROUPS + d, STAGE[f"out{d}"], tokens_out, (m_hi, m_lo), ready=mixed_ready if d == 0 else None)
            mod_sum(5)
            pe.wait_ge(xn_ready, 2 * TT)
            for k in range(KD // 4):
                transposed(STAGE[f"h2t{k}"], y1, 4 * k)

            n0, a0, d0 = len(STAGES), freed("A", len(STAGES)), freed("D", len(STAGES))
            pe.wait_ge(act_freed, a0)
            pe.wait_ge(dve_freed, d0)
            pe.wait_ge(h_ready, 2 * KD)
            with pe.Fori(0, STEPS) as i:
                for u in range(UPG + DNG):
                    if u < UPG:
                        pe.wait_ge(dve_freed, i * DNG + (d0 - UPG + 1 + u))
                    elif u < 2 * UPG:
                        pe.wait_ge(act_freed, i * UPG + (a0 + 1 + u - UPG))
                    else:
                        pe.wait_ge(dve_freed, i * DNG + (d0 + u - 2 * UPG + 1))
                    slabs, nk = (SG, KD) if u < UPG else (DS, HT)
                    first = SG * u if u < UPG else UPG * SG + DS * (u - UPG)
                    for j in range(slabs):
                        local = first + j
                        pe.wait_ge(lo_dve, i * STEP_SLABS + (MLP0 - PROJ_SLABS + local + 1))
                        for k in range(KS):
                            kt = KS * j + k
                            if u < UPG:
                                last = features_out(n0 + u, local % RING, k, (h2_hi, h2_lo), kt, nk)
                            else:
                                if u == UPG:
                                    pe.wait_ge(u2_ready, i * HT + (kt + 1))
                                last = tokens_out(n0 + u, local % RING, k, (u2_hi, u2_lo), kt, nk)
                        last.then_inc(slab_used, 1)

        @block.scalar
        def _(act):
            ch = Chain(act, act_chain)

            def split(s):
                act.wait_ge(raw_landed[s % RING], 16 * (s // RING + 1))
                if s >= RING:
                    act.wait_ge(slab_used, s - RING + 1)
                r, hi = raw[:, s % RING, :, :], w_hi[:, s % RING, :, :]
                if s < SG:
                    ch.link(nc.scalar.activation(hi[:, :, 0:64], r[:, :, 0:64], ACT.Copy))
                    r, hi = r[:, :, 0:192], hi[:, :, 64:256]
                nc.scalar.activation(hi, r, ACT.Copy).then_inc(hi_ready, 1)

            def done(name):
                wait_stage(act, name)

            def squares(src, dst, col, after=None):
                return nc.scalar.activation(dst, src, ACT.Square, accum_out=col)

            def h_stage(name, m, dst, sub, k0):
                done(name)
                shift = mod[:, (1, 4)[sub], :]
                for b in range(4):
                    k = k0 + b
                    nc.scalar.activation(dst[:, k, :], bank(STAGE[name], b), ACT.Identity, bias=shift[:, k:k + 1],
                                         scale=mul[:, sub, k:k + 1]).then_inc(h_hi_ready, 1)
                act.wait_ge(h_hi_ready, sub * KD + k0 + 4)
                act.sem_inc(act_freed, 1)

            act.wait_ge(vec_ready, 2)
            nc.scalar.activation(c_tmp[:], col_a[:, at_a["c"]:at_a["c"] + KD], ACT.Tanh, scale=0.5).then_inc(c_tanh, 1)
            act.wait_ge(vec_ready, 3)
            nc.scalar.activation(lam_t[:, 1, :], lam_t[:, 0, :], ACT.Exp, scale=-1.0).then_inc(c_tanh, 1)
            act.wait_ge(consts, 2)

            def bias_store(k):
                act.wait_ge(act_chain, bias_at[k])
                act.dma_start(bias_s[P * k:P * k + P, :], bias_out[:, k % 2, :]).then_inc(bias_stored[k % 2], 16)

            bias_at = []
            xs = 0
            for m in range(8):
                done(f"bias{m}")
                for b in range(4):
                    k = 4 * m + b
                    if k >= 2:
                        act.wait_ge(bias_stored[k % 2], 16 * (k // 2))
                    bias_at.append(ch.put(nc.scalar.activation(bias_out[:, k % 2, :], bank(STAGE[f"bias{m}"], b), ACT.Copy)))
                    if b == 3:
                        ch.wait()
                        act.sem_inc(act_freed, 1)
                    bias_store(k)
                if m >= 4:
                    t = m - 4
                    act.wait_ge(x_landed[t], 16)
                    if t:
                        act.wait_ge(ssq_ready, t)
                    squares(x_tok[:, t, :], junk[:], stat[:, 0, t:t + 1]).then_inc(ssq_ready, 1)
            act.wait_ge(ssq_ready, TT)
            nc.scalar.activation(stat[:, 1, 0:TT], stat[:, 0, 0:TT], ACT.Sqrt, bias=eps_c[:], scale=1.0 / D).then_inc(root_ready, 1)
            act.wait_ge(rinv_ready, 1)
            for t in range(TT):
                nc.scalar.activation(x_tok[:, t, :], x_tok[:, t, :], ACT.Copy, scale=stat[:, 2, t:t + 1]).then_inc(xn_ready, 1)
            act.wait_ge(mul_ready, 1)
            for k in range(KD // 4):
                h_stage(f"ht{k}", k, h_hi, 0, 4 * k)

            def split_to(s, upto):
                while s < upto:
                    split(s)
                    s += 1
                return s

            s = split_to(0, SG + 3)
            done("g0")
            n = STAGE["g0"]
            act.wait_ge(dve_freed, freed("D", STAGE["ht3"] + 1))
            nc.scalar.activation(ki_hi[:], bank(n, 0), ACT.Copy).then_inc(act_hi, 1)
            nc.scalar.activation(widx_t[0:IH, :], bank(n, 1)[0:IH, :], ACT.Copy).then_inc(widx_copied, 1)
            act.wait_ge(widx_copied, 1)
            act.wait_ge(act_hi, 1)
            act.sem_inc(act_freed, 1)
            for g in (1, 2):
                s = split_to(s, SG * (g + 1) + 3)
                done(f"g{g}")
                for b in range(4):
                    nc.scalar.activation(qi_hi[:, 4 * (g - 1) + b, :], bank(STAGE[f"g{g}"], b), ACT.Copy).then_inc(act_hi, 1)
                act.wait_ge(act_hi, 1 + 4 * g)
                act.sem_inc(act_freed, 1)
            for m in range(TT * IH // 4):
                done(f"dots{m}")
                for b in range(4):
                    k = 4 * m + b
                    if k >= 2:
                        act.wait_ge(relu_used, k - 1)
                    nc.scalar.activation(relu[:, k % 2, :], bank(STAGE[f"dots{m}"], b), ACT.Relu).then_inc(relu_ready, 1)
                act.wait_ge(relu_ready, 4 * m + 4)
                act.sem_inc(act_freed, 1)

            def copy_out(name, dst, scale=1.0, after=None):
                done(name)
                for b in range(4):
                    ch.put(nc.scalar.activation(dst(b), bank(STAGE[name], b), ACT.Copy, scale=scale))
                ch.wait()
                act.sem_inc(act_freed, 1)

            s = split_to(s, SG * 4 + 3)
            act.wait_ge(score_done, TT)
            copy_out("g3", lambda b: lru_in[:, b, :])
            act.sem_inc(branch_act, 1)
            s = split_to(s, SG * 5 + 3)
            copy_out("g4", lambda b: gate_in[:, b, :])
            act.sem_inc(branch_act, 1)
            for k, (name, dst) in enumerate((("rgate", r_t), ("igate", i_t))):
                done(name)
                for b in range(CT):
                    ch.put(nc.scalar.activation(dst[:, b, :], bank(STAGE[name], b), ACT.Tanh, bias=half_b[:, k, b:b + 1],
                                                scale=0.5))
                ch.wait()
                act.sem_inc(act_freed, 1)
            act.sem_inc(branch_act, 1)
            act.wait_ge(branch_dve, U_ARG)
            ch.link(nc.scalar.activation(r_t[:], r_t[:], ACT.Tanh))
            act.sem_inc(branch_act, 1)
            s = split_to(s, SG * 5 + 5)
            ch.link(nc.scalar.activation(lru_in[:], r_t[:], ACT.Sqrt, scale=-1.0))
            act.sem_inc(branch_act, 1)
            act.wait_ge(branch_dve, SCANNED)
            ch.link(nc.scalar.activation(r_t[:], gate_in[:], ACT.Square))
            act.sem_inc(branch_act, 1)
            s = split_to(s, SG * 6 + 3)
            act.wait_ge(branch_dve, GELU_ARG)
            ch.link(nc.scalar.activation(lru_in[:], r_t[:], ACT.Tanh, scale=float(np.sqrt(2 / np.pi))))
            act.sem_inc(branch_act, 1)
            act.wait_ge(branch_dve, LRU_DONE)
            copy_out("g5", lambda b: pool_u[:, b, PAD:])
            act.sem_inc(branch_act, 1)
            s = split_to(s, SG * 7 + 3)
            act.wait_ge(mod_step, MOD_EARLY + MOD_PROJ)
            copy_out("g6", lambda b: k_t[:, b, :])
            s = split_to(s, SG * 8 + 3)
            copy_out("g7", lambda b: k_t[:, 4 + b, :])
            act.wait_ge(mask_done, TT)
            done("poolmm")
            n = STAGE["poolmm"]
            for b in range(CT):
                o = at_b["pool_scale"] + b
                ch.put(nc.scalar.activation(pool_o[:, b, :], bank(n, b), ACT.Copy, scale=col_b[:, o:o + 1]))
            ch.wait()
            act.sem_inc(act_freed, 1)
            nc.scalar.activation(pool_sq[:], pool_o[:], ACT.Square).then_inc(branch_act, 1)
            nc.scalar.activation(lru_sq[:], lru_o[:], ACT.Square).then_inc(branch_act, 1)
            act.wait_ge(dve_freed, freed("D", STAGE["mod4"] + 1))
            s = split_to(s, SG * 9 + 3)
            done("ssq")
            copy_out("g8", lambda b: q_t[:, b, :], scale=HD ** -0.5)
            for b in range(2):
                ch.put(nc.scalar.activation(rnorm[:, b, :], bank(STAGE["ssq"], b), ACT.Sqrt, bias=eps_c[:], scale=1.0 / GW))
            ch.wait()
            act.sem_inc(act_freed, 1)
            act.sem_inc(root_ready, 1)
            s = split_to(s, SG * 10 + 3)
            copy_out("g9", lambda b: q_t[:, 4 + b, :], scale=HD ** -0.5)
            for g in (10, 11):
                s = split_to(s, SG * (g + 1) + 3)
                done(f"g{g}")
                for b in range(TT):
                    c0 = 512 * (g - 10)
                    nc.scalar.activation(v_hi[:, b, c0:c0 + 512], bank(STAGE[f"g{g}"], b), ACT.Copy).then_inc(act_hi, 1)
                act.wait_ge(act_hi, 9 + 4 * (g - 9))
                act.sem_inc(act_freed, 1)

            def head_split(hd):
                if hd >= 2:
                    act.wait_ge(s_done, TT * (hd - 1))
                nc.scalar.activation(q_hi[:, hd % 2, :], q_t[:, hd, :], ACT.Copy).then_inc(qk_hi, 1)
                nc.scalar.activation(k_hi[:, hd % 2, :], k_t[:, hd, :], ACT.Copy).then_inc(qk_hi, 1)

            def exps(it):
                act.wait_ge(max_ready, it + 1)
                nc.scalar.activation(probs[:, it % 3, :], probs[:, it % 3, :], ACT.Exp, bias=nmax[:, it % 3:it % 3 + 1],
                                     accum_out=asum[:, it % 3:it % 3 + 1]).then_inc(exp_ready, 1)

            def pt_split(it):
                act.wait_ge(pt_done, it + 1)
                if it >= 2:
                    act.wait_ge(pv_done, it - 1)
                nc.scalar.activation(pt_hi[:, it % 2, :, :].rearrange("p k q -> p (k q)"), psum[:, 3 + it % 2, :],
                                     ACT.Copy).then_inc(pt_hi_ready, 1)

            def head_out(hd):
                act.wait_ge(pv_done, TT * (hd + 1))
                nc.scalar.activation(attn[:, hd, :], psum[:, 5 + hd % 2, :], ACT.Copy).then_inc(o_ready, 1)

            head_split(0)
            head_split(1)
            n_it = HEADS * TT
            for it in range(n_it + 5):
                if it < n_it:
                    exps(it)
                if 0 <= it - 1 < n_it:
                    pt_split(it - 1)
                if it % TT == 1 and 2 <= it // TT + 1 < HEADS:
                    head_split(it // TT + 1)
                if it >= TT + 2 and (it - 3) % TT == TT - 1:
                    head_out((it - 3) // TT)

            act.wait_ge(sq_used, HEADS)
            nc.scalar.activation(rnorm[:, 0, :], psum[:, 7, :], ACT.Sqrt, bias=eps_c[:], scale=1.0 / AW).then_inc(root_ready, 1)
            for k in range(KD):
                if k < HEADS:
                    act.wait_ge(mixed_full, k + 1)
                    src = h_full[:, k % 2, :]
                else:
                    src = pool_o[:, k - HEADS, :] if k < HEADS + CT else lru_o[:, k - HEADS - CT, :]
                    if k == HEADS:
                        act.wait_ge(rinv_ready, 2)
                nc.scalar.activation(m_hi[:, k, :], src, ACT.Copy).then_inc(mixed_hi, 1)
            for d in range(TT):
                s = split_to(s, min(SG * (PROJ_GROUPS + d + 1) + 3, MLP0))
                done(f"out{d}")
                for t in range(TT):
                    ch.link(squares(bank(STAGE[f"out{d}"], t), sq_out[:], stat[:, 3 + d, t:t + 1]))
                act.sem_inc(act_freed, 1)
            act.sem_inc(ssq_ready, 1)
            act.wait_ge(rinv_ready, 3)
            nc.scalar.activation(stat[:, 1, 0:TT], stat[:, 0, 0:TT], ACT.Sqrt, bias=eps_c[:], scale=1.0 / D).then_inc(root_ready, 1)
            for t in range(TT):
                act.wait_ge(x1_ready, t + 1)
                if t:
                    act.wait_ge(ssq_ready, TT + 1 + t)
                squares(y1[:, t, :], slab_1[:], stat[:, 0, 4 + t:5 + t]).then_inc(ssq_ready, 1)
            act.wait_ge(ssq_ready, 2 * TT + 1)
            nc.scalar.activation(stat[:, 1, 0:TT], stat[:, 0, 4:4 + TT], ACT.Sqrt, bias=eps_c[:], scale=1.0 / D).then_inc(root_ready, 1)
            act.wait_ge(rinv_ready, 5)
            for t in range(TT):
                act.wait_ge(x1_stored[t], 16)
                nc.scalar.activation(y1[:, t, :], y1[:, t, :], ACT.Copy, scale=stat[:, 2, t:t + 1]).then_inc(xn_ready, 1)
            act.wait_ge(mul_ready, 2)
            for k in range(KD // 4):
                h_stage(f"h2t{k}", k, h2_hi, 1, 4 * k)

            n0 = len(STAGES)

            def split_mlp(i, local):
                act.wait_ge(raw_landed[local % RING], i * (16 * STEP_SLABS // RING) + 16 * ((MLP0 + local) // RING + 1))
                act.wait_ge(slab_used, i * STEP_SLABS + (MLP0 + local - RING + 1))
                nc.scalar.activation(w_hi[:, local % RING, :, :], raw[:, local % RING, :, :], ACT.Copy).then_inc(hi_ready, 1)

            def up_stage(i, u):
                act.wait_ge(slab_used, i * STEP_SLABS + (MLP0 + SG * (u + 1)))
                for b in range(4):
                    act.wait_ge(up_used, i * HT + (UP0 + 4 * u + b - 1))
                    nc.scalar.activation(u_relu[:, b % 2, :], bank(n0 + u, b), ACT.Relu).then_inc(up_relu, 1)
                act.wait_ge(up_relu, i * HT + (4 * u + 4))
                act.sem_inc(act_freed, 1)

            with act.Fori(0, STEPS) as i:
                for local in range(STEP_SLABS):
                    split_mlp(i, local)
                    if local in (SG + 2, 2 * SG + 2):
                        up_stage(i, (local - 2) // SG - 1)
            act.wait_ge(ssq_ready, 2 * TT + 1)
            act.wait_ge(dve_freed, freed("D", n0) + DNG * STEPS)
            for t in range(TT):
                ch.link(squares(y2[:, t, :], junk2[:], stat[:, 0, 8 + t:9 + t]))
            nc.scalar.activation(stat[:, 1, 0:TT], stat[:, 0, 8:8 + TT], ACT.Sqrt, bias=eps_c[:], scale=1.0 / D).then_inc(root_ready, 1)

        @block.vector
        def _(dve):
            ch = Chain(dve, dve_chain)
            V = nc.vector

            def done(name):
                wait_stage(dve, name)

            def free():
                ch.wait()
                dve.sem_inc(dve_freed, 1)

            def cols(table, name, n):
                tile, at_ = (col_a, at_a) if table == "a" else (col_b, at_b)
                return tile[:, at_[name]:at_[name] + n]

            def rsqrt(v_src, n, dst, scale, tmp):
                root = stat[:, 1, 0:n]
                v = stat[:, 7, 0:n]
                ch.link(V.tensor_scalar(v, v_src, scale, EPS, ALU.mult, ALU.add))
                ch.link(V.reciprocal(dst, root))
                ch.link(V.tensor_tensor(tmp, dst, dst, ALU.mult))
                ch.link(V.tensor_tensor(tmp, tmp, v, ALU.mult))
                ch.link(V.tensor_scalar(tmp, tmp, -0.5, 1.5, ALU.mult, ALU.add))
                ch.link(V.tensor_tensor(dst, dst, tmp, ALU.mult))

            dve.wait_ge(pos_in, 32)
            ch.put(V.tensor_copy(pos_k[:], pos_ki[:]))
            V.tensor_copy(pos_qf[0:TT, :], pos_qi[0:TT, :]).then_inc(vec_ready, 1)
            done("vec")
            n = STAGE["vec"]
            na, nb = sum(v.shape[0] for _, v in vec_a_rows), sum(v.shape[0] for _, v in vec_b_rows)
            ch.put(V.tensor_copy(col_a[:, 0:na], bank(n, 0)[:, 0:na]))
            ch.put(V.tensor_copy(col_b[:, 0:nb], bank(n, 1)[:, 0:nb]))
            ch.put(V.tensor_copy(pos_q[:], bank(n, 2)[:, 0:TT]))
            ch.put(V.tensor_copy(start_col[:], bank(n, 3)[:, 0:1]))
            free()
            dve.sem_inc(vec_ready, 1)
            for q in range(4):
                r32 = slice(32 * q, 32 * q + 32)
                ch.put(V.tensor_scalar(reach[r32, :], pos_k[r32, P * q:P * q + P], start_col[r32, :], None, ALU.subtract))
            ch.wait()
            dve.sem_inc(reach_ready, 1)
            lam = cols("b", "lam", CT)
            ch.link(V.tensor_scalar(lam_t[:, 2, :], lam, -1.0, None, ALU.mult))
            ch.link(V.tensor_tensor(lam_t[:, 0, :], lam_t[:, 2, :], lam, ALU.max))
            ch.link(V.tensor_scalar(lam_t[:, 2, :], lam_t[:, 2, :], 0.0, None, ALU.max))
            for k, name in enumerate(("r_b", "i_b")):
                ch.put(V.tensor_scalar(half_b[:, k, :], cols("b", name, CT), 0.5, None, ALU.mult))
            ch.wait()
            dve.sem_inc(vec_ready, 1)
            dve.wait_ge(c_tanh, 2)
            ch.link(V.scalar_tensor_tensor(c_act[:], c_tmp[:], 1.0, cols("a", "c", KD), ALU.add, ALU.mult))
            ch.link(V.tensor_scalar(c_act[:], c_act[:], 0.5, None, ALU.mult))
            e_, z, z2, sp_ = lam_t[:, 1, :], lam_t[:, 3, :], lam_t[:, 4, :], lam_t[:, 5, :]
            ch.link(V.tensor_scalar(z, e_, 2.0, None, ALU.add))
            ch.link(V.reciprocal(z, z))
            ch.link(V.tensor_tensor(z, z, e_, ALU.mult))
            ch.link(V.tensor_tensor(z2, z, z, ALU.mult))
            ch.link(V.tensor_scalar(sp_, z2, 1.0 / 17, 1.0 / 15, ALU.mult, ALU.add))
            for odd in (13, 11, 9, 7, 5, 3, 1):
                ch.link(V.tensor_tensor(sp_, sp_, z2, ALU.mult))
                ch.link(V.tensor_scalar(sp_, sp_, 1.0 / odd, None, ALU.add))
            ch.link(V.tensor_tensor(sp_, sp_, z, ALU.mult))
            ch.link(V.scalar_tensor_tensor(sp_, sp_, 2.0, lam_t[:, 2, :], ALU.mult, ALU.add))
            ch.link(V.tensor_scalar(sp_, sp_, -LRU_C / 4, None, ALU.mult))

            def mod_add(g):
                j, k = divmod(g, KD)
                acc = acc_b if j % 2 else acc_a
                slab = (slab_0, slab_1)[g % 2][:] if j == 5 else mod_slab[:, g % 2, :]
                dve.wait_ge(mod_landed[g % 2], 16 * (g // 2 + 1))
                if k == 0:
                    if j >= 2:
                        wait_stage(dve, f"mod{j - 2}")
                    V.tensor_scalar(acc[:], slab, c_act[:, k:k + 1], None, ALU.mult).then_inc(mod_step, 1)
                else:
                    dve.wait_ge(mod_step, g)
                    V.scalar_tensor_tensor(acc[:], slab, c_act[:, k:k + 1], acc[:], ALU.mult, ALU.add).then_inc(mod_step, 1)

            def mod_out(j):
                done(f"mod{j}")
                table = "a" if f"b_mod{j}" in at_a else "b"
                ch.link(V.tensor_tensor(mod[:, j, :], bank(STAGE[f"mod{j}"], 0)[:, 0:KD], cols(table, f"b_mod{j}", KD), ALU.add))
                dve.sem_inc(dve_freed, 1)
                if j in (2, 5):
                    ch.link(V.tensor_tensor(mod[:, j, :], mod[:, j, :], cols("b", "g_post1" if j == 2 else "g_post2", KD), ALU.mult))
                    dve.sem_inc(gate_col, 1)
                if j in (0, 3):
                    k = j // 3
                    ch.link(V.scalar_tensor_tensor(mul[:, k, :], mod[:, j, :], 1.0, cols("a", f"g_pre{k + 1}", KD), ALU.add, ALU.mult))
                if j in (1, 4):
                    dve.sem_inc(mul_ready, 1)

            for g in range(MOD_EARLY):
                mod_add(g)
                for j in range(3):
                    k = 4 * g + j
                    if k >= 4:
                        dve.wait_ge(step_used, k - 3)
                    V.tensor_scalar(steps[:, k % 4, :], pos_k[:], reach[:, k:k + 1], None, ALU.is_le).then_inc(step_dve, 1)
            dve.wait_ge(root_ready, 1)
            rsqrt(stat[:, 0, 0:TT], TT, stat[:, 2, 0:TT], 1.0 / D, stat[:, 2, 8:8 + TT])
            dve.sem_inc(rinv_ready, 1)
            mod_out(0)
            mod_out(1)

            def h_stage(name, sub, hi, lo, k0):
                done(name)
                for b in range(4):
                    k = k0 + b
                    n = sub * KD + k
                    dve.wait_ge(h_hi_ready, n + 1)
                    ch.link(V.tensor_scalar(h_full[:, b % 2, :], bank(STAGE[name], b), mul[:, sub, k:k + 1],
                                            mod[:, (1, 4)[sub], k:k + 1], ALU.mult, ALU.add))
                    V.tensor_tensor(lo[:, k, :], h_full[:, b % 2, :], hi[:, k, :].bitcast(F32), ALU.subtract).then_inc(h_ready, 1)
                free()

            dve.wait_ge(bias_stored[0], 16 * T // 32)
            dve.wait_ge(bias_stored[1], 16 * T // 32)
            for k in range(KD // 4):
                h_stage(f"ht{k}", 0, h_hi, h_lo, 4 * k)

            def beside(s):
                if s < MOD_PROJ:
                    mod_add(MOD_EARLY + s)
                if TOPK_AT <= s < TOPK_AT + TT * ROUNDS // 2:
                    for r in (2 * (s - TOPK_AT), 2 * (s - TOPK_AT) + 1):
                        topk_round(*divmod(r, ROUNDS))

            def is_late(t):
                ch.link(V.tensor_scalar(late[:], pos_k[:], pos_q[:, t:t + 1], None, ALU.is_gt))

            def topk_round(t, r):
                ch.link(V.max(top8[:], score[:, t, :]))
                ch.link(V.match_replace(score[:, t, :], top8[:], score[:, t, :], TAKEN))
                if r == ROUNDS - 1:
                    is_late(t)
                    ch.link(V.scalar_tensor_tensor(score[:, t, :], score[:, t, :], TAKEN / 2, late[:], ALU.is_gt, ALU.max))
                    if t == 0:
                        wait_stage(dve, "igate")
                    V.tensor_scalar(mask[:, t, :], score[:, t, :], NEG, None, ALU.mult).then_inc(mask_done, 1)

            def beside_to(s, upto):
                while s < upto:
                    beside(s)
                    s += 1
                return s

            def low(dst, stage, b, hi, signal, n_hi):
                dve.wait_ge(act_hi, n_hi)
                V.tensor_tensor(dst, bank(stage, b), hi.bitcast(F32), ALU.subtract).then_inc(signal, 1)

            s = beside_to(0, SG + 3)
            done("g0")
            low(ki_lo[:], STAGE["g0"], 0, ki_hi[:], idx_ready, 1)
            dve.wait_ge(idx_ready, 1)
            dve.sem_inc(dve_freed, 1)
            for g in (1, 2):
                s = beside_to(s, SG * (g + 1) + 3)
                done(f"g{g}")
                for b in range(4):
                    k = 4 * (g - 1) + b
                    low(qi_lo[:, k, :], STAGE[f"g{g}"], b, qi_hi[:, k, :], idx_ready, 2 + k)
                dve.wait_ge(idx_ready, 1 + 4 * g)
                dve.sem_inc(dve_freed, 1)
            done("widx")
            for t in range(TT):
                ch.put(V.tensor_scalar(w_idx[:, t, :], bank(STAGE["widx"], 0)[:, IH * t:IH * t + IH], (IH * ID) ** -0.5, None,
                                       ALU.mult))
            free()
            mod_out(2)
            for k in range(TT * IH):
                t, hd = divmod(k, IH)
                if hd == 0:
                    ch.link(V.tensor_scalar(score[:, t, :], pos_k[:], pos_q[:, t:t + 1], NEG, ALU.is_gt, ALU.mult))
                dve.wait_ge(relu_ready, k + 1)
                if hd:
                    dve.wait_ge(relu_used, k)
                V.scalar_tensor_tensor(score[:, t, :], relu[:, k % 2, :], w_idx[:, t, hd:hd + 1], score[:, t, :], ALU.mult,
                                       ALU.add).then_inc(relu_used, 1)
                if hd == IH - 1:
                    dve.wait_ge(relu_used, k + 1)
                    dve.sem_inc(score_done, 1)

            s = beside_to(s, SG * 4 + 3)
            dve.wait_ge(branch_act, 1)
            taps = cols("b", "conv_w", 4 * CT)
            for b in range(CT):
                tap = [taps[:, CT * j + b:CT * j + b + 1] for j in range(4)]
                ch.link(V.tensor_scalar(xc[:, b, :], lru_in[:, b, :], tap[3], cols("b", "conv_b", CT)[:, b:b + 1], ALU.mult, ALU.add))
                for j in (2, 1, 0):
                    w = 3 - j
                    ch.link(V.scalar_tensor_tensor(xc[:, b, w:], lru_in[:, b, :T - w], tap[j], xc[:, b, w:], ALU.mult, ALU.add))
            dve.sem_inc(branch_dve, 1)
            s = beside_to(s, SG * 5)
            mod_out(3)
            s = beside_to(s, SG * 5 + 3)
            dve.wait_ge(branch_act, 3)
            for b in range(CT):
                ch.put(V.tensor_scalar(r_t[:, b, :], r_t[:, b, :], 1.0, sp_[:, b:b + 1], ALU.add, ALU.mult))
            ch.wait()
            dve.sem_inc(branch_dve, 1)
            ch.link(V.scalar_tensor_tensor(xc[:], i_t[:], 1.0, xc[:], ALU.add, ALU.mult))
            dve.wait_ge(branch_act, 4)
            ch.link(V.tensor_scalar(i_t[:], r_t[:], -1.0, 1.0, ALU.mult, ALU.add))
            ch.link(V.reciprocal(i_t[:], i_t[:]))
            ch.link(V.tensor_tensor(xc[:], xc[:], i_t[:], ALU.mult))
            dve.wait_ge(branch_act, 5)
            ch.link(V.tensor_tensor(xc[:], xc[:], lru_in[:], ALU.mult))
            ch.link(V.scalar_tensor_tensor(r_t[:], r_t[:], 1.0, i_t[:], ALU.add, ALU.mult))
            for b in range(CT):
                ch.put(V.tensor_tensor_scan(i_t[:, b, :], r_t[:, b, :], xc[:, b, :], 0.0, ALU.mult, ALU.add))
            ch.wait()
            dve.sem_inc(branch_dve, 1)
            s = beside_to(s, SG * 5 + 6)
            dve.wait_ge(branch_act, 6)
            ch.link(V.tensor_scalar(r_t[:], r_t[:], 0.044715, 1.0, ALU.mult, ALU.add))
            ch.link(V.tensor_tensor(r_t[:], r_t[:], gate_in[:], ALU.mult))
            dve.sem_inc(branch_dve, 1)
            dve.wait_ge(branch_act, 7)
            ch.link(V.scalar_tensor_tensor(gate_in[:], lru_in[:], 1.0, gate_in[:], ALU.add, ALU.mult))
            wait_stage(dve, "mod3")
            ch.link(V.scalar_tensor_tensor(lru_o[:], i_t[:], 0.5, gate_in[:], ALU.mult, ALU.mult))
            dve.sem_inc(branch_dve, 1)
            s = beside_to(s, SG * 6 + 5)
            for t_ in (pool_u, pool_b, pool_c):
                ch.put(V.memset(t_[:, :, 0:PAD], 0.0))
            ch.wait()
            dve.wait_ge(branch_act, 8)
            src, dst, w = pool_u, pool_b, 1
            for b in range(CT):
                ch.link(V.tensor_tensor(dst[:, b:, PAD:], src[:, b:, PAD:], src[:, b:, PAD - w:PAD - w + T], ALU.add))
                src, dst, w = dst, (pool_c if dst is pool_b else pool_b), 2 * w
            for b in range(CT):
                win = 2 ** (b + 1)
                o = (pool_b, pool_c)[b % 2]
                ch.link(V.tensor_tensor(pool_fix[:, b, 0:win], o[:, b, PAD:PAD + win], inv_n[:, 0:win], ALU.mult))
                ch.link(V.scalar_tensor_tensor(o[:, b, PAD:], o[:, b, PAD:], 1.0 / win, pool_u[:, b, PAD:], ALU.mult, ALU.subtract))
                ch.link(V.tensor_tensor(o[:, b, PAD:PAD + win], pool_fix[:, b, 0:win], pool_u[:, b, PAD:PAD + win], ALU.subtract))
            dve.sem_inc(branch_dve, 1)
            s = beside_to(s, SG * 7 + 3)
            mod_out(4)
            s = beside_to(s, TOPK_AT + TT * ROUNDS // 2)
            dve.wait_ge(root_ready, 2)
            for k, (o, g) in enumerate(((pool_o, "g_pool"), (lru_o, "g_lru"))):
                ch.link(V.reciprocal(rnorm[:, k, :], rnorm[:, k, :]))
                for b in range(CT):
                    ch.put(V.scalar_tensor_tensor(o[:, b, :], o[:, b, :], cols("b", g, CT)[:, b:b + 1], rnorm[:, k, :],
                                                  ALU.mult, ALU.mult))
            ch.wait()
            dve.sem_inc(rinv_ready, 1)
            for g in (10, 11):
                done(f"g{g}")
                for b in range(TT):
                    c0 = 512 * (g - 10)
                    k = 4 * (g - 10) + b
                    low(v_lo[:, b, c0:c0 + 512], STAGE[f"g{g}"], b, v_hi[:, b, c0:c0 + 512], idx_ready, 10 + k)
                dve.wait_ge(idx_ready, 9 + 4 * (g - 9))
                dve.sem_inc(dve_freed, 1)

            def split(s):
                dve.wait_ge(hi_ready, s + 1)
                V.tensor_tensor(w_lo[:, s % RING, :, :], raw[:, s % RING, :, :], w_hi[:, s % RING, :, :].bitcast(F32),
                                ALU.subtract).then_inc(lo_dve, 1)

            for s in range(PROJ_SLABS, PROJ_SLABS + 3):
                split(s)

            def head_split(hd):
                dve.wait_ge(qk_hi, 2 * hd + 2)
                ch.put(V.tensor_tensor(q_lo[:, hd % 2, :], q_t[:, hd, :], q_hi[:, hd % 2, :].bitcast(F32), ALU.subtract))
                ch.wait()
                V.tensor_tensor(k_lo[:, hd % 2, :], k_t[:, hd, :], k_hi[:, hd % 2, :].bitcast(F32), ALU.subtract).then_inc(qk_lo, 1)

            def logits(it):
                hd, t = divmod(it, TT)
                if t == 0:
                    dve.wait_ge(bm_ready, hd + 1)
                dve.wait_ge(s_done, it + 1)
                if it >= 3:
                    dve.wait_ge(pt_done, it - 2)
                j = it % 3
                V.tensor_tensor_reduce(out=probs[:, j, :], in0=psum[:, j, :], in1=bm[:, hd % 2, t, :], scale=1.0,
                                       scalar=-3e38, op0=ALU.add, op1=ALU.max, accum_out=amax[:, j:j + 1]).then_inc(bm_used, 1)
                dve.wait_ge(bm_used, it + 1)
                V.tensor_scalar(nmax[:, j:j + 1], amax[:, j:j + 1], -1.0, None, ALU.mult).then_inc(max_ready, 1)

            def normalise(it):
                j = it % 3
                dve.wait_ge(exp_ready, it + 1)
                ch.link(V.reciprocal(arec[:, j:j + 1], asum[:, j:j + 1]))
                V.tensor_scalar(probs[:, j, :], probs[:, j, :], arec[:, j:j + 1], None, ALU.mult).then_inc(probs_ready, 1)

            def pt_split(it):
                dve.wait_ge(pt_hi_ready, it + 1)
                V.tensor_tensor(pt_lo[:, it % 2, :, :].rearrange("p k q -> p (k q)"), psum[:, 3 + it % 2, :],
                                pt_hi[:, it % 2, :, :].rearrange("p k q -> p (k q)").bitcast(F32),
                                ALU.subtract).then_inc(pt_lo_ready, 1)

            head_split(0)
            head_split(1)
            n_it = HEADS * TT
            for it in range(n_it + 2):
                if it < n_it:
                    logits(it)
                if 0 <= it - 1 < n_it:
                    normalise(it - 1)
                if 0 <= it - 2 < n_it:
                    pt_split(it - 2)
                if it % TT == 2 and 2 <= it // TT + 1 < HEADS:
                    head_split(it // TT + 1)

            dve.wait_ge(root_ready, 3)
            ch.link(V.reciprocal(rnorm[:, 0, :], rnorm[:, 0, :]))
            for k in range(KD):
                if k < HEADS:
                    if k >= 2:
                        dve.wait_ge(mixed_hi, k - 1)
                    src = h_full[:, k % 2, :]
                    V.scalar_tensor_tensor(src, attn[:, k, :], cols("b", "g_attn", HEADS)[:, k:k + 1], rnorm[:, 0, :],
                                           ALU.mult, ALU.mult).then_inc(mixed_full, 1)
                    dve.wait_ge(mixed_full, k + 1)
                else:
                    src = pool_o[:, k - HEADS, :] if k < HEADS + CT else lru_o[:, k - HEADS - CT, :]
                dve.wait_ge(mixed_hi, k + 1)
                V.tensor_tensor(m_lo[:, k, :], src, m_hi[:, k, :].bitcast(F32), ALU.subtract).then_inc(mixed_ready, 1)

            s = PROJ_SLABS + 3
            g = 5 * KD
            for d in range(TT):
                upto = min(SG * (PROJ_GROUPS + d + 1) + 3, MLP0)
                while s < upto:
                    split(s)
                    if s % 2 and g < 6 * KD:
                        mod_add(g)
                        g += 1
                    s += 1
                if d == TT - 1:
                    while g < 6 * KD:
                        mod_add(g)
                        g += 1
                done(f"out{d}")
                for t in range(TT):
                    dve.wait_ge(act_freed, freed("A", STAGE[f"out{d}"] + 1))
                    ch.put(V.tensor_copy(y1[:, t, 512 * d:512 * d + 512], bank(STAGE[f"out{d}"], t)))
                free()
            mod_out(5)
            dve.wait_ge(ssq_ready, TT + 1)
            ch.link(V.tensor_reduce(stat[:, 0, 0:TT], stat[:, 3:7, 0:TT].rearrange("p d t -> p t d"), AXX, ALU.add))
            dve.sem_inc(rinv_ready, 1)
            dve.wait_ge(root_ready, 4)
            rsqrt(stat[:, 0, 0:TT], TT, stat[:, 2, 0:TT], 1.0 / D, stat[:, 2, 8:8 + TT])
            dve.sem_inc(rinv_ready, 1)
            dve.wait_ge(g_landed, 16)
            for t in range(TT):
                ch.link(V.scalar_tensor_tensor(y1[:, t, :], y1[:, t, :], stat[:, 2, t:t + 1], g1_bc[:], ALU.mult, ALU.mult))
                dve.wait_ge(x_again[t % 2], 16 * (t // 2 + 1))
                V.tensor_tensor(y1[:, t, :], y1[:, t, :], x_in[:, t % 2, :], ALU.add).then_inc(x1_ready, 1)
            dve.wait_ge(root_ready, 5)
            rsqrt(stat[:, 0, 4:4 + TT], TT, stat[:, 2, 0:TT], 1.0 / D, stat[:, 2, 8:8 + TT])
            dve.sem_inc(rinv_ready, 1)
            for k in range(KD // 4):
                h_stage(f"h2t{k}", 1, h2_hi, h2_lo, 4 * k)
            for t in (0, 2):
                V.memset(y2[:, t:t + 2, :], 0.0).then_inc(up_used, 1)

            n0, d0 = len(STAGES), freed("D", len(STAGES))
            MC = 2 * HT

            def split_mlp(i, local):
                dve.wait_ge(hi_ready, i * STEP_SLABS + (MLP0 + local + 1))
                V.tensor_tensor(w_lo[:, local % RING, :, :], raw[:, local % RING, :, :],
                                w_hi[:, local % RING, :, :].bitcast(F32), ALU.subtract).then_inc(lo_dve, 1)

            c0 = ch.n

            def square_stage(i, u):
                for b in range(4):
                    k = 4 * u + b
                    dve.wait_ge(up_relu, i * HT + (k + 1))
                    if not isinstance(i, int) or k >= 2:
                        dve.wait_ge(u2_ready, i * HT + (k - 1))
                    V.tensor_tensor(u_sq[:, b % 2, :], u_relu[:, b % 2, :], u_relu[:, b % 2, :], ALU.mult).then_inc(up_used, 1)
                    dve.wait_ge(up_used, i * HT + (UP0 + k + 1))
                    V.tensor_copy(u2_hi[:, k, :], u_sq[:, b % 2, :]).then_inc(dve_chain, 1)
                    dve.wait_ge(dve_chain, i * HT + (c0 + k + 1))
                    V.tensor_tensor(u2_lo[:, k, :], u_sq[:, b % 2, :], u2_hi[:, k, :].bitcast(F32), ALU.subtract).then_inc(u2_ready, 1)

            def add_stage(i, d):
                dve.wait_ge(slab_used, i * STEP_SLABS + (MLP0 + UPG * SG + DS * (d + 1)))
                for t in range(TT):
                    y = y2[:, t, 512 * d:512 * d + 512]
                    last = V.tensor_tensor(y, y, bank(n0 + UPG + d, t), ALU.add)
                    if t == TT - 1:
                        last.then_inc(dve_freed, 1)

            def step(i, before):
                for local in range(STEP_SLABS):
                    split_mlp(i, local)
                    if local == 2 and before is not None:
                        add_stage(before, DNG - 1)
                    if local in (SG + 2, 2 * SG + 2):
                        square_stage(i, (local - 2) // SG - 1)
                    d, r = divmod(local - UPG * SG - DS - 2, DS)
                    if r == 0 and 0 <= d < DNG - 1:
                        add_stage(i, d)

            step(0, None)
            with dve.Fori(1, STEPS) as i:
                step(i, i - 1)
            add_stage(STEPS - 1, DNG - 1)
            ch.n = c0 + HT * STEPS
            dve.wait_ge(root_ready, 6)
            rsqrt(stat[:, 0, 8:8 + TT], TT, stat[:, 2, 0:TT], 1.0 / D, stat[:, 2, 8:8 + TT])
            dve.wait_ge(g_landed, 32)
            dve.wait_ge(x1_back, 16)
            for t in range(TT):
                ch.link(V.scalar_tensor_tensor(y2[:, t, :], y2[:, t, :], stat[:, 2, t:t + 1], g2_bc[:], ALU.mult, ALU.mult))
                V.tensor_tensor(x1_in[:, t, :], x1_in[:, t, :], y2[:, t, :], ALU.add).then_inc(final_ready, 1)


INPUTS = ["x", "c", "positions", "rel_bias", "w_mod", "b_mod", "g_pre_mix", "g_post_mix", "g_pre_mlp", "g_post_mlp",
          "w_in", "pool_w", "pool_scale", "conv_w", "conv_b", "gate_r_w", "gate_r_b", "gate_i_w", "gate_i_b",
          "lru_lambda", "g_attn_out", "g_pool_out", "g_lru_out", "w_out", "w_mlp_up", "w_mlp_down"]


def kernel(**inputs):
    import concourse.bacc as bacc
    from concourse.bass_utils import run_bass_kernel_spmd

    nc = bacc.Bacc("TRN2", target_bir_lowering=False, num_devices=1)
    arrays, args = {}, []
    for name in INPUTS:
        a = np.ascontiguousarray(inputs[name])
        arrays[f"in_{name}"] = a
        args.append(nc.dram_tensor(f"in_{name}", a.shape, mybir.dt.from_np(a.dtype), kind="ExternalInput").ap())
    args.append(nc.dram_tensor("out_x", (1, T, D), F32, kind="ExternalOutput").ap())
    build(nc, *args)
    r = run_bass_kernel_spmd(nc, [arrays], core_ids=[0])
    return r.results[0]["out_x"]
```

```python
from contextlib import ExitStack

import numpy as np
import concourse.bass as bass
from concourse import mybir

F32 = mybir.dt.float32
F32R = mybir.dt.float32r
BF16 = mybir.dt.bfloat16
I32 = mybir.dt.int32
ALU = mybir.AluOpType
ACT = mybir.ActivationFunctionType
AXX = mybir.AxisListType.X

P = 128
D = 2048
T = 512
KD = D // P
TT = T // P
HEADS, HD = 8, 128
AW = HEADS * HD
IH, ID = 16, 64
GW = 512
CT = GW // P
TOPK = min(256, T // 4)
ROUNDS = TOPK // 8
HIDDEN = 4 * D
NBUCKET, MAXDIST = 32, 128
EPS = 1e-6
LRU_C = 8.0
NEG = -1e30
TAKEN = -3e38

C_Q, C_K, C_V, C_QI = 0, AW, 2 * AW, 3 * AW
C_KI = C_QI + IH * ID
C_WI = C_KI + ID
C_POOL = C_WI + IH
C_LRU = C_POOL + GW
C_GATE = C_LRU + GW

RING = 4
KS = 2
SG = KD // KS
G_KW, G_QI, G_LRU, G_GATE, G_POOL, G_K, G_Q, G_V = 0, 1, 3, 4, 5, 6, 8, 10
PROJ_GROUPS = 12
PROJ_SLABS = PROJ_GROUPS * SG
OUT_SLABS = TT * SG
MLP0 = PROJ_SLABS + OUT_SLABS
CHUNK = 1024
STEPS = HIDDEN // CHUNK
HT = CHUNK // P
UPG, DNG = CHUNK // 512, D // 512
DS = HT // KS
STEP_SLABS = UPG * SG + DNG * DS

SHIFT1, SCALE1, GATE1, SHIFT2, SCALE2, GATE2 = range(6)
MOD_ORDER = [SCALE1, SHIFT1, GATE1, SCALE2, SHIFT2, GATE2]
MOD_EARLY = 2 * KD
MOD_PROJ = 3 * KD

STAGES = (
    [("c", "D"), ("vec", "D")] + [(f"bias{n}", "A") for n in range(8)] + [(f"xt{t}", "AD") for t in range(TT)] + [("mod0", "D"), ("mod1", "D")]
    + [("g0", "AD"), ("g1", "AD"), ("g2", "AD"), ("widx", "D"), ("mod2", "D")]
    + [(f"dots{n}", "A") for n in range(TT * IH // 4)]
    + [("g3", "A"), ("g4", "A"), ("mod3", "D"), ("rgate", "A"), ("igate", "A"), ("g5", "A"), ("g6", "A"),
       ("mod4", "D"), ("g7", "A"), ("poolmm", "A"), ("g8", "A"), ("ssq", "A"), ("g9", "A"), ("g10", "AD"),
       ("g11", "AD")]
    + [(f"out{n}", "AD") for n in range(TT)] + [("mod5", "D")]
)
STAGE = {name: n for n, (name, _) in enumerate(STAGES)}
TURN_HALF = (len(STAGES) + 1) % 2


GROUP_OF = {f"g{g}": g for g in range(PROJ_GROUPS)} | {f"out{d}": PROJ_GROUPS + d for d in range(TT)}

CONV_DONE, U_ARG, SCANNED, GELU_ARG, LRU_DONE, POOL_DIFF = range(1, 7)
BRANCH_SQ = 10
X_AT = (5, 7, 9, 11)
TOPK_AT = 34
PROB_SLOTS, BM_SLOTS = 4, 8
S_BANK, SQ_BANK = 4 * (STAGE["out0"] % 2), 4 * ((STAGE["out0"] + 1) % 2)
O_BANK = SQ_BANK + 1
PT_BANK = (S_BANK + 3, SQ_BANK + 3)
LAG_EXP, LAG_NORM, LAG_TURN, LAG_HI, LAG_LO, LAG_PV = 0, 1, 3, 2, 3, 5
EARLY_SPLITS = RING + (KD - 4) // KS + 1
assert EARLY_SPLITS <= SG + 3


def freed(who, n):
    return sum(who in by for _, by in STAGES[:n])


def out_tile(n):
    return (n + HEADS) % KD


def bucket_starts():
    exact = NBUCKET // 2
    return [b if b < exact else int(np.ceil(exact * (MAXDIST / exact) ** ((b - exact) / (NBUCKET - exact)) - 1e-9))
            for b in range(NBUCKET)]


def build(nc, x, c, positions, rel_bias, w_mod, b_mod, g_pre_mix, g_post_mix, g_pre_mlp, g_post_mlp, w_in,
          pool_w, pool_scale, conv_w, conv_b, gate_r_w, gate_r_b, gate_i_w, gate_i_b, lru_lambda,
          g_attn_out, g_pool_out, g_lru_out, w_out, w_mlp_up, w_mlp_down, out):
    def rows(w):
        return w.rearrange("a (t p) n -> p (a t) n", p=P)

    def vec_rows(v):
        return v.rearrange("a (r p) -> (a r) p", p=P)

    x_d, out_d = rows(x), rows(out)
    w_mod_d, w_in_d, w_out_d = rows(w_mod), rows(w_in), rows(w_out)
    w_up_d, w_down_d = rows(w_mlp_up), rows(w_mlp_down)
    bias_s = nc.dram_tensor("bias_s", (T * HEADS, T), F32, kind="Internal").ap()
    gate_s = nc.dram_tensor("gate_s", (2, D), F32, kind="Internal").ap()
    x1_s = nc.dram_tensor("x1_s", (P, TT, D), F32, kind="Internal").ap()
    bias_h = bias_s.rearrange("(q t h) k -> h q t k", q=P, t=TT)

    b_rows = vec_rows(b_mod)
    vec_a_rows = [("g_pre1", vec_rows(g_pre_mix)), ("g_pre2", vec_rows(g_pre_mlp)),
                  ("b_mod0", b_rows[SCALE1 * KD:(SCALE1 + 1) * KD]), ("b_mod1", b_rows[SHIFT1 * KD:(SHIFT1 + 1) * KD]),
                  ("b_mod3", b_rows[SCALE2 * KD:(SCALE2 + 1) * KD]), ("b_mod4", b_rows[SHIFT2 * KD:(SHIFT2 + 1) * KD])]
    vec_b_rows = [("conv_w", conv_w.rearrange("a j (r p) -> (a j r) p", p=P)), ("conv_b", vec_rows(conv_b)),
                  ("r_b", vec_rows(gate_r_b)), ("i_b", vec_rows(gate_i_b)), ("lam", vec_rows(lru_lambda)),
                  ("pool_scale", vec_rows(pool_scale)), ("g_attn", vec_rows(g_attn_out)),
                  ("g_pool", vec_rows(g_pool_out)), ("g_lru", vec_rows(g_lru_out)),
                  ("b_mod2", b_rows[GATE1 * KD:(GATE1 + 1) * KD]), ("b_mod5", b_rows[GATE2 * KD:(GATE2 + 1) * KD]),
                  ("g_post1", vec_rows(g_post_mix)), ("g_post2", vec_rows(g_post_mlp))]
    at_a, at_b = {}, {}
    for at, table in ((at_a, vec_a_rows), (at_b, vec_b_rows)):
        n = 0
        for name, v in table:
            at[name] = n
            n += v.shape[0]
        assert n <= P
    n_small = len(vec_a_rows) + len(vec_b_rows)

    with ExitStack() as ctx:
        def sb(name, shape, dt):
            return ctx.enter_context(nc.sbuf_tensor(name, shape, dt))

        def sem(name):
            return ctx.enter_context(nc.semaphore(name))

        raw = sb("raw", [P, RING, KS, 512], F32)
        w_hi = sb("w_hi", [P, RING, KS, 512], F32R)
        w_lo = sb("w_lo", [P, RING, KS, 512], F32R)
        ident = sb("ident", [P, P], F32)
        ones = sb("ones", [P, P], F32)
        col_a = sb("col_a", [P, P], F32)
        col_b = sb("col_b", [P, P], F32)
        pos_k = sb("pos_k", [P, T], F32)
        pos_q = sb("pos_q", [P, TT], F32)
        start_col = sb("start_col", [P, 1], F32)
        rb = sb("rb", [P, HEADS], F32)
        rb_prev = sb("rb_prev", [P, HEADS], F32)
        rb_step = sb("rb_step", [P, HEADS], F32)
        c_col = sb("c_col", [P, KD], F32)
        c_act = sb("c_act", [P, KD], F32)
        c_tmp = sb("c_tmp", [P, KD], F32)
        mod = sb("mod", [P, 6, KD], F32)
        mul = sb("mul", [P, 2, KD], F32)
        w_idx = sb("w_idx", [P, TT, IH], F32)
        lam_t = sb("lam_t", [P, 8, CT], F32)
        half_b = sb("half_b", [P, 2, CT], F32)
        stat = sb("stat", [P, 8, 16], F32)
        eps_c = sb("eps_c", [P, 1], F32)
        inv_n = sb("inv_n", [P, 16], F32)
        pool_fix = sb("pool_fix", [P, CT, 16], F32)
        top8 = sb("top8", [P, 8], F32)
        nmax = sb("nmax", [P, PROB_SLOTS], F32)
        asum = sb("asum", [P, PROB_SLOTS], F32)
        arec = sb("arec", [P, PROB_SLOTS], F32)

        def at(kb, name, shape, dt):
            with ExitStack() as e:
                if kb:
                    e.enter_context(nc.sbuf_tensor(f"below_{name}", [P, int(kb * 256)], F32))
                return e.enter_context(nc.sbuf_tensor(name, shape, dt))

        bias_out = at(32, "bias_out", [P, 4, T], F32)
        steps = at(4, "steps", [P, 4, T], F32R)
        junk = at(20, "junk", [P, D], F32)
        vec_a = at(28, "vec_a", [P, P], F32)
        vec_b = at(28.5, "vec_b", [P, P], F32)
        c_row = at(31, "c_row", [P, P], F32)
        pos_qi = at(29, "pos_qi", [P, P], I32)
        pos_qf = at(29.5, "pos_qf", [P, P], F32)
        start_row = at(30, "start_row", [P, P], F32)
        reach = at(30.5, "reach", [P, P], F32)
        x_tok = at(84, "x_tok", [P, TT, D], F32)
        blk = at(116, "blk", [P, 4, P], F32)
        blk_hi = at(118, "blk_hi", [P, 4, P], F32R)
        blk_lo = at(120, "blk_lo", [P, 4, P], F32R)
        diag = at(150, "diag", [P, TT, P], F32)
        pos_ki = at(148, "pos_ki", [P, T], I32)
        acc_a = at(124, "acc_a", [P, D], F32)
        acc_b = at(12, "acc_b", [P, D], F32)
        mod_slab = at(132, "mod_slab", [P, 2, D], F32)
        h_full = at(0, "h_full", [P, 2, T], F32)
        h_hi = at(20, "h_hi", [P, KD, T], F32R)
        h_lo = at(52, "h_lo", [P, KD, T], F32R)
        x_t = at(52, "x_t", [P, KD, T], F32)
        score = at(4, "score", [P, TT, T], F32)
        qi_hi = at(84, "qi_hi", [P, IH // 2, T], F32R)
        qi_lo = at(100, "qi_lo", [P, IH // 2, T], F32R)
        ki_hi = at(116, "ki_hi", [P, T], F32R)
        ki_lo = at(118, "ki_lo", [P, T], F32R)
        relu = at(120, "relu", [P, 2, T], F32)
        widx_t = at(148, "widx_t", [P, T], F32)
        late = at(150, "late", [P, T], F32)
        gates_w = at(0, "gates_w", [P, 2, CT, P], F32)
        gate_in = at(84, "gate_in", [P, CT, T], F32)
        xc = at(92, "xc", [P, CT, T], F32)
        lru_in = at(100, "lru_in", [P, CT, T], F32)
        r_t = at(108, "r_t", [P, CT, T], F32)
        i_t = at(116, "i_t", [P, CT, T], F32)
        PAD = 8
        pool_u = at(84, "pool_u", [P, CT, PAD + T], F32)
        pool_b = at(93, "pool_b", [P, CT, PAD + T], F32)
        pool_c = at(102, "pool_c", [P, CT, PAD + T], F32)
        pool_ws = at(122, "pool_ws", [P, CT, P], F32)
        pool_sq = at(111, "pool_sq", [P, CT, T], F32)
        lru_sq = at(84, "lru_sq", [P, CT, T], F32)
        rnorm = at(148, "rnorm", [P, 2, T], F32)
        mask = at(0, "mask", [P, TT, T], BF16)
        pool_o = at(4, "pool_o", [P, CT, T], F32)
        lru_o = at(12, "lru_o", [P, CT, T], F32)
        v_hi = at(84, "v_hi", [P, TT, AW], F32R)
        v_lo = at(100, "v_lo", [P, TT, AW], F32R)
        q_t = at(116, "q_t", [P, HEADS, T], F32)
        k_t = at(132, "k_t", [P, HEADS, T], F32)
        attn = at(20, "attn", [P, HEADS, T], F32)
        bm = at(36, "bm", [P, BM_SLOTS, T], F32)
        q_hi = at(52, "q_hi", [P, 2, T], F32R)
        k_hi = at(56, "k_hi", [P, 2, T], F32R)
        q_lo = at(116, "q_lo", [P, HEADS, T], F32R)
        k_lo = at(132, "k_lo", [P, HEADS, T], F32R)
        probs = at(60, "probs", [P, PROB_SLOTS, T], F32)
        pt_hi = at(68, "pt_hi", [P, 2, TT, 2 * P], F32R)
        pt_lo = at(76, "pt_lo", [P, 2, TT, 2 * P], F32R)
        attn_sq = at(150, "attn_sq", [P, T], F32)
        m_hi = at(84, "m_hi", [P, KD, T], F32R)
        m_lo = at(116, "m_lo", [P, KD, T], F32R)
        mixed = at(20, "mixed", [P, HEADS, T], F32)
        x_in = [at(kb, f"x_in{t}", [P, D], F32) for t, kb in enumerate((20, 28, 84, 92))]
        y1 = at(36, "y1", [P, TT, D], F32)
        g1_bc = at(68, "g1_bc", [P, D], F32)
        slab_0 = at(4, "slab_0", [P, D], F32)
        slab_1 = at(76, "slab_1", [P, D], F32)
        sq_out = at(148, "sq_out", [P, T], F32)
        h2_hi = at(84, "h2_hi", [P, KD, T], F32R)
        h2_lo = at(116, "h2_lo", [P, KD, T], F32R)
        y2 = at(20, "y2", [P, TT, D], F32)
        u2_hi = at(52, "u2_hi", [P, HT, T], F32R)
        u2_lo = at(68, "u2_lo", [P, HT, T], F32R)
        u_relu = at(0, "u_relu", [P, 2, T], F32)
        u_sq = at(4, "u_sq", [P, 2, T], F32)
        g2_bc = at(12, "g2_bc", [P, D], F32)
        x1_in = at(84, "x1_in", [P, TT, D], F32)
        junk2 = at(116, "junk2", [P, D], F32)

        psum = ctx.enter_context(nc.psum_tensor("psum", [P, 8, 512], F32))

        def bank(stage, b):
            return psum[:, 4 * (stage % 2) + b, :]

        raw_landed = [sem(f"raw_landed{i}") for i in range(RING)]
        hi_ready, lo_pool, lo_dve, slab_used = sem("hi_ready"), sem("lo_pool"), sem("lo_dve"), sem("slab_used")
        stage_done, act_freed, dve_freed = sem("stage_done"), sem("act_freed"), sem("dve_freed")
        dve_chain, act_chain, pool_chain = sem("dve_chain"), sem("act_chain"), sem("pool_chain")
        c_in, ident_ready, small_in, pos_in, x_landed = sem("c_in"), sem("ident_ready"), sem("small_in"), sem("pos_in"), [sem(f"x_landed{t}") for t in range(TT)]
        mod_landed, mod_step = [sem("mod_landed0"), sem("mod_landed1")], sem("mod_step")
        consts, rb_in, blk_ready, reach_ready = sem("consts"), sem("rb_in"), sem("blk_ready"), sem("reach_ready")
        step_dve, step_pool, step_used = sem("step_dve"), sem("step_pool"), sem("step_used")
        bias_stored = [sem(f"bias_stored{i}") for i in range(4)]
        vec_ready, c_tanh, c_copied, diag_ready = sem("vec_ready"), sem("c_tanh"), sem("c_copied"), sem("diag_ready")
        ssq_ready, root_ready, rinv_ready, xn_ready = sem("ssq_ready"), sem("root_ready"), sem("rinv_ready"), sem("xn_ready")
        mul_ready, h_hi_ready, h_ready = sem("mul_ready"), sem("h_hi_ready"), sem("h_ready")
        turned, turned_used = sem("turned"), sem("turned_used")
        act_hi = sem("act_hi")
        idx_ready, widx_copied = sem("idx_ready"), sem("widx_copied")
        relu_ready, relu_used, score_done = sem("relu_ready"), sem("relu_used"), sem("score_done")
        gates_in, pool_in = sem("gates_in"), sem("pool_in")
        branch_act, branch_dve = sem("branch_act"), sem("branch_dve")
        out_squared = sem("out_squared")
        mask_done, gate_col, gate_stored, g_landed = sem("mask_done"), sem("gate_col"), sem("gate_stored"), sem("g_landed")
        pool_fixed = sem("pool_fixed")
        bias_landed = [sem(f"bias_landed{i}") for i in range(BM_SLOTS)]
        bm_ready = sem("bm_ready")
        qk_hi, q_lo_ready, k_lo_ready = sem("qk_hi"), sem("q_lo_ready"), sem("k_lo_ready")
        s_done, max_ready, exp_ready, probs_ready, pt_done, pt_hi_ready, pt_lo_ready = (
            sem("s_done"), sem("max_ready"), sem("exp_ready"), sem("probs_ready"), sem("pt_done"),
            sem("pt_hi_ready"), sem("pt_lo_ready"))
        pv_done, o_ready, sq_ready, sq_used = sem("pv_done"), sem("o_ready"), sem("sq_ready"), sem("sq_used")
        mixed_full, mixed_hi, mixed_ready = sem("mixed_full"), sem("mixed_hi"), sem("mixed_ready")
        x_again, x1_ready, x1_stored = [sem(f"x_again{t}") for t in range(TT)], sem("x1_ready"), [sem(f"x1_stored{t}") for t in range(TT)]
        y2_zero = sem("y2_zero")
        up_relu, up_used, u2_ready = sem("up_relu"), sem("up_used"), sem("u2_ready")
        x1_back, final_ready, out_stored = sem("x1_back"), sem("final_ready"), sem("out_stored")

        class Chain:

            def __init__(self, eng, counter):
                self.eng, self.counter, self.n = eng, counter, 0

            def put(self, instruction):
                instruction.then_inc(self.counter, 1)
                self.n += 1
                return self.n

            def wait(self, n=None):
                self.eng.wait_ge(self.counter, self.n if n is None else n)

            def link(self, instruction):
                self.put(instruction)
                self.wait()

        def slab_source(s):
            g, j = divmod(s, SG)
            k = slice(KS * j, KS * j + KS)
            if g == G_KW:
                return w_in_d[:, k, C_KI:C_KI + 192], 192
            if g < PROJ_GROUPS:
                col = {G_QI: C_QI, G_QI + 1: C_QI + 512, G_LRU: C_LRU, G_GATE: C_GATE, G_POOL: C_POOL, G_K: C_K,
                       G_K + 1: C_K + 512, G_Q: C_Q, G_Q + 1: C_Q + 512, G_V: C_V, G_V + 1: C_V + 512}[g]
                return w_in_d[:, k, col:col + 512], 512
            col = 512 * (g - PROJ_GROUPS)
            k = slice(out_tile(KS * j), out_tile(KS * j) + KS)
            return w_out_d[:, k, col:col + 512], 512

        def wait_lo(eng, s):
            if s < PROJ_SLABS:
                eng.wait_ge(lo_pool, s + 1)
            else:
                eng.wait_ge(lo_dve, s - PROJ_SLABS + 1)

        def wait_stage(eng, name):
            if name in GROUP_OF:
                eng.wait_ge(slab_used, SG * (GROUP_OF[name] + 1))
            elif name.startswith("bias"):
                eng.wait_ge(step_used, 16 * (int(name[4:]) + 1))
            else:
                counted = [k for k, _ in STAGES if k not in GROUP_OF and not k.startswith("bias")]
                eng.wait_ge(stage_done, counted.index(name) + 1)

        def store_gate(eng, k):
            with nc.allow_non_contiguous_dma(reason="2048 elements"):
                eng.dma_start(gate_s[k:k + 1, :].rearrange("a (r p) -> p (a r)", p=P),
                              mod[:, (2, 5)[k], :]).then_inc(gate_stored, 16)

        block = ctx.enter_context(nc.Block())

        @block.sync
        def _(sp):
            def load_slab(s):
                if s >= RING:
                    wait_lo(sp, s - RING)
                src, n = slab_source(s)
                sp.dma_start(raw[:, s % RING, :, 0:n], src).then_inc(raw_landed[s % RING], 16)

            def load_mod(g):
                j, k = divmod(g, KD)
                if g >= 2:
                    sp.wait_ge(mod_step, g - 1)
                m = MOD_ORDER[j]
                if j == 5:
                    dst = (slab_0, slab_1)[g % 2][:]
                else:
                    dst = mod_slab[:, g % 2, :]
                sp.dma_start(dst, w_mod_d[:, k, D * m:D * (m + 1)]).then_inc(mod_landed[g % 2], 16)

            sp.dma_start(c_row[0:KD, :], vec_rows(c)).then_inc(c_in, 16)
            for g in range(MOD_EARLY):
                load_mod(g)
                if g == 1:
                    for v, table in ((vec_a, vec_a_rows), (vec_b, vec_b_rows)):
                        n = 0
                        for _, src in table:
                            sp.dma_start(v[n:n + src.shape[0], :], src).then_inc(small_in, 16)
                            n += src.shape[0]
                if g in X_AT:
                    t = X_AT.index(g)
                    sp.dma_start(x_tok[:, t, :], x_d[:, t, :]).then_inc(x_landed[t], 16)
                if g == MOD_EARLY - 3:
                    load_slab(0)
                    load_slab(1)
            for s in range(PROJ_SLABS):
                if s < MOD_PROJ:
                    load_mod(MOD_EARLY + s)
                load_slab(s + 2)
                if s == 24:
                    sp.wait_ge(h_ready, KD)
                    for k, w in enumerate((gate_r_w, gate_i_w)):
                        sp.dma_start(gates_w[:, k, :, :], w.rearrange("a g c d -> c (a g) d")).then_inc(gates_in, 16)
                if s == 34:
                    sp.wait_ge(gate_col, 1)
                    store_gate(sp, 0)
                if s == 50:
                    sp.wait_ge(branch_dve, LRU_DONE)
                    sp.dma_start(pool_ws[:], pool_w.rearrange("a g c d -> c (a g) d")).then_inc(pool_in, 16)

            load_slab(PROJ_SLABS + 2)
            load_slab(PROJ_SLABS + 3)
            wait_stage(sp, "g11")
            for it in range(HEADS * TT):
                if it >= BM_SLOTS:
                    sp.wait_ge(max_ready, it - BM_SLOTS + 1)
                sp.dma_start(bm[:, it % BM_SLOTS, :], bias_h[it // TT][:, it % TT, :]).then_inc(bias_landed[it % BM_SLOTS], 16)

            for s in range(PROJ_SLABS, MLP0):
                k = s - PROJ_SLABS
                if s + RING < MLP0:
                    load_slab(s + RING)
                if k == 0:
                    sp.wait_ge(gate_stored, 16)
                    sp.wait_ge(pt_lo_ready, HEADS * TT)
                    sp.wait_ge(pv_done, HEADS * TT // 2)
                    sp.dma_start(g1_bc[:], gate_s[0:1, :].to_broadcast([P, D])).then_inc(g_landed, 16)
                    sp.wait_ge(mixed_ready, KD)
                if k % 2 == 0:
                    load_mod(5 * KD + k // 2)
                if k in (1, 3):
                    t = k // 2
                    sp.dma_start(x_in[t][:], x_d[:, t, :]).then_inc(x_again[t], 16)

            def load_mlp(s, i, local):
                wait_count = MLP0 - PROJ_SLABS - RING + 1 + local
                sp.wait_ge(lo_dve, i * STEP_SLABS + wait_count)
                if local < UPG * SG:
                    g, j = divmod(local, SG)
                    src = w_up_d[:, KS * j:KS * j + KS, bass.ds(i * CHUNK + 512 * g, 512)]
                else:
                    g, j = divmod(local - UPG * SG, DS)
                    src = w_down_d[:, bass.ds(i * HT + KS * j, KS), 512 * g:512 * g + 512]
                sp.dma_start(raw[:, s % RING, :, :], src).then_inc(raw_landed[s % RING], 16)

            for local in range(STEP_SLABS):
                load_mlp(MLP0 + local, 0, local)
                if local == RING - 1:
                    wait_stage(sp, "out3")
                    for t in (2, 3):
                        sp.dma_start(x_in[t][:], x_d[:, t, :]).then_inc(x_again[t], 16)
                    for t in range(TT):
                        sp.wait_ge(x1_ready, t + 1)
                        sp.dma_start(x1_s[:, t, :], y1[:, t, :]).then_inc(x1_stored[t], 16)
                    sp.wait_ge(gate_col, 2)
                    store_gate(sp, 1)
            with sp.Fori(1, STEPS) as i:
                for local in range(STEP_SLABS):
                    load_mlp(MLP0 + local, i, local)
            sp.wait_ge(gate_stored, 32)
            sp.dma_start(g2_bc[:], gate_s[1:2, :].to_broadcast([P, D])).then_inc(g_landed, 16)
            for t in range(TT):
                sp.wait_ge(x1_stored[t], 16)
            sp.wait_ge(slab_used, MLP0 + STEP_SLABS * (STEPS - 1) + UPG * SG)
            sp.dma_start(x1_in[:], x1_s).then_inc(x1_back, 16)
            for t in range(TT):
                sp.wait_ge(final_ready, t + 1)
                sp.dma_start(out_d[:, t, :], x1_in[:, t, :]).then_inc(out_stored, 16)
            sp.wait_ge(out_stored, 16 * TT)
            for stored in bias_stored:
                sp.wait_ge(stored, 16 * 8)

        @block.gpsimd
        def _(pool):
            ch = Chain(pool, pool_chain)
            ch.put(nc.gpsimd.memset(ones[:], 1.0))
            ch.link(nc.gpsimd.memset(ident[:], 0.0))
            nc.gpsimd.affine_select(out=ident[:], in_=ident[:], compare_op=ALU.not_equal, fill=1.0, base=0,
                                    pattern=[[-1, P]], channel_multiplier=1).then_inc(ident_ready, 1)
            nc.gpsimd.memset(rb_prev[:], 0.0).then_inc(consts, 1)
            ch.put(nc.gpsimd.memset(blk[:], 0.0))
            starts = bucket_starts()
            row = start_row[0:1, :].rearrange("a (q b) -> a b q", q=4)
            for b in range(NBUCKET):
                ch.put(nc.gpsimd.memset(row[:, b, :], float(starts[b])))
            for n in range(16):
                ch.put(nc.gpsimd.memset(inv_n[:, n:n + 1], 1.0 / (n + 1)))
            ch.put(nc.gpsimd.memset(eps_c[:], EPS))
            ch.wait()
            pool.wait_ge(rb_in, 16 * 8)
            ch.link(nc.gpsimd.tensor_tensor(rb_step[:], rb[:], rb_prev[:], ALU.subtract))
            for q in range(4):
                for j in range(4):
                    o = 32 * j + 8 * q
                    ch.put(nc.gpsimd.tensor_copy(blk[32 * q:32 * q + 32, j, o:o + 8], rb_step[32 * q:32 * q + 32, :]))
            ch.wait()
            ch.link(nc.gpsimd.tensor_copy(blk_hi[:], blk[:]))
            nc.gpsimd.tensor_tensor(blk_lo[:], blk[:], blk_hi[:].bitcast(F32), ALU.subtract).then_inc(blk_ready, 1)
            pool.wait_ge(blk_ready, 1)
            nc.gpsimd.memset(stat[:], 0.0).then_inc(consts, 1)
            pool.wait_ge(reach_ready, 1)
            for n in range(3, P, 4):
                if n >= 4:
                    pool.wait_ge(step_used, n - 3)
                nc.gpsimd.tensor_scalar(steps[:, n % 4, :], pos_k[:], reach[:, n:n + 1], None,
                                        ALU.is_le).then_inc(step_pool, 1)
            for s in range(PROJ_SLABS):
                pool.wait_ge(hi_ready, s + 1)
                r, hi, lo = raw[:, s % RING, :, :], w_hi[:, s % RING, :, :], w_lo[:, s % RING, :, :]
                if s < SG:
                    ch.put(nc.gpsimd.tensor_tensor(lo[:, :, 0:64], r[:, :, 0:64], hi[:, :, 0:64].bitcast(F32), ALU.subtract))
                    ch.wait()
                    r, hi, lo = r[:, :, 0:192], hi[:, :, 64:256], lo[:, :, 64:256]
                nc.gpsimd.tensor_tensor(lo, r, hi.bitcast(F32), ALU.subtract).then_inc(lo_pool, 1)
            pool.wait_ge(mask_done, TT)

            def k_low(hd):
                pool.wait_ge(qk_hi, 2 * hd + 2)
                nc.gpsimd.tensor_tensor(k_lo[:, hd, :], k_t[:, hd, :], k_hi[:, hd % 2, :].bitcast(F32),
                                        ALU.subtract).then_inc(k_lo_ready, 1)

            def squares_of(hd):
                pool.wait_ge(o_ready, hd + 1)
                if hd >= 1:
                    pool.wait_ge(sq_used, hd)
                nc.gpsimd.tensor_tensor(attn_sq[:], attn[:, hd, :], attn[:, hd, :], ALU.mult).then_inc(sq_ready, 1)

            k_low(0)
            for it in range(HEADS * TT):
                b = bm[:, it % BM_SLOTS, :]
                pool.wait_ge(bias_landed[it % BM_SLOTS], 16 * (it // BM_SLOTS + 1))
                nc.gpsimd.tensor_tensor(b, b, mask[:, it % TT, :], ALU.add).then_inc(bm_ready, 1)
                hd = it // TT
                if it == 1:
                    k_low(1)
                if it % TT == TT - 1 and 2 <= hd + 1 < HEADS:
                    k_low(hd + 1)
                if it % TT == 1 and hd >= 3:
                    squares_of(hd - 3)
            for hd in range(HEADS - 3, HEADS):
                squares_of(hd)
            pool.wait_ge(turned, KD)
            for stored in x1_stored:
                pool.wait_ge(stored, 16)
            nc.gpsimd.memset(y2[:, :, D - 512:D], 0.0).then_inc(y2_zero, 1)

        @block.tensor
        def _(pe):
            def begin(n):
                if n >= 2:
                    if freed("A", n - 1):
                        pe.wait_ge(act_freed, freed("A", n - 1))
                    if freed("D", n - 1):
                        pe.wait_ge(dve_freed, freed("D", n - 1))

            def three(o, a_hi, a_lo, b_hi, b_lo, first, last):
                nc.tensor.matmul(o, a_hi, b_hi, start=first, stop=False)
                nc.tensor.matmul(o, a_hi, b_lo, start=False, stop=False)
                return nc.tensor.matmul(o, a_lo, b_hi, start=False, stop=last)

            def weights(slot, j, cols):
                return w_hi[:, slot, j, cols], w_lo[:, slot, j, cols]

            def features_out(stage, slot, j, act, kt, first, last_, tiles=4):
                for b in range(tiles):
                    last = three(bank(stage, b), *weights(slot, j, slice(P * b, P * b + P)),
                                 act[0][:, kt, :], act[1][:, kt, :], first, last_)
                return last

            def tokens_out(stage, slot, j, act, kt, first, last_):
                for b in range(TT):
                    tok = slice(P * b, P * b + P)
                    last = three(bank(stage, b), act[0][:, kt, tok], act[1][:, kt, tok],
                                 *weights(slot, j, slice(0, 512)), first, last_)
                return last

            def group(g, stage, emit, act, ready=None, tile=lambda n: n, **how):
                begin(stage)
                for j in range(SG):
                    s = g * SG + j
                    wait_lo(pe, s)
                    for k in range(KS):
                        if ready is not None:
                            pe.wait_ge(ready, KS * j + k + 1)
                        n = KS * j + k
                        last = emit(stage, s % RING, k, act, tile(n), n == 0, n == KD - 1, **how)
                    last.then_inc(slab_used, 1)

            def mod_sum(j):
                n = STAGE[f"mod{j}"]
                begin(n)
                pe.wait_ge(mod_step, KD * (j + 1))
                acc = acc_b if j % 2 else acc_a
                for k in range(KD):
                    last = nc.tensor.matmul(bank(n, 0)[:, k:k + 1], acc[:, P * k:P * k + P], ones[:, 0:1],
                                            start=True, stop=True)
                last.then_inc(stage_done, 1)

            def transposed(o, src, kt):
                for t in range(TT):
                    last = nc.tensor.matmul(o[:, P * t:P * t + P], src[:, t, P * kt:P * kt + P], diag[:, t, :],
                                            start=True, stop=True)
                return last

            pe.wait_ge(c_in, 16)
            pe.wait_ge(ident_ready, 1)
            nc.tensor.transpose(bank(STAGE["c"], 0)[:, 0:KD], c_row[0:KD, :], ident[0:KD, 0:KD]).then_inc(stage_done, 1)
            pe.wait_ge(small_in, 16 * n_small)
            pe.wait_ge(pos_in, 32)
            pe.wait_ge(blk_ready, 1)
            pe.wait_ge(vec_ready, 1)
            n = STAGE["vec"]
            na, nb = sum(v.shape[0] for _, v in vec_a_rows), sum(v.shape[0] for _, v in vec_b_rows)
            nc.tensor.transpose(bank(n, 0)[:, 0:na], vec_a[0:na, :], ident[0:na, 0:na])
            nc.tensor.transpose(bank(n, 1)[:, 0:nb], vec_b[0:nb, :], ident[0:nb, 0:nb])
            nc.tensor.transpose(bank(n, 2)[:, 0:TT], pos_qf[0:TT, :], ident[0:TT, 0:TT])
            nc.tensor.matmul(bank(n, 3)[:, 0:1], start_row[0:1, :], ones[0:1, 0:1], start=True,
                             stop=True).then_inc(stage_done, 1)

            for m in range(8):
                n = STAGE[f"bias{m}"]
                begin(n)
                for b in range(4):
                    for j in range(4):
                        k = 16 * m + 4 * b + j
                        if j < 3:
                            pe.wait_ge(step_dve, 3 * (k // 4) + j + 1)
                        else:
                            pe.wait_ge(step_pool, k // 4 + 1)
                        nc.tensor.matmul(bank(n, b), blk_hi[:, j, :], steps[:, k % 4, :], start=j == 0, stop=False)
                        last = nc.tensor.matmul(bank(n, b), blk_lo[:, j, :], steps[:, k % 4, :], start=False, stop=j == 3)
                        last.then_inc(step_used, 1)

            pe.wait_ge(diag_ready, TT)
            for n in range(TT):
                begin(STAGE[f"xt{n}"])
                for b in range(4):
                    last = transposed(bank(STAGE[f"xt{n}"], b), x_tok, 4 * n + b)
                last.then_inc(stage_done, 1)
            mod_sum(0)
            mod_sum(1)

            h = (h_hi, h_lo)
            group(G_KW, STAGE["g0"], features_out, h, ready=h_ready, tiles=2)
            group(G_QI, STAGE["g1"], features_out, h)
            group(G_QI + 1, STAGE["g2"], features_out, h)
            n = STAGE["widx"]
            begin(n)
            pe.wait_ge(widx_copied, 1)
            for t in range(TT):
                last = nc.tensor.transpose(bank(n, 0)[:, IH * t:IH * t + IH], widx_t[0:IH, P * t:P * t + P],
                                           ident[0:IH, 0:IH])
            last.then_inc(stage_done, 1)
            mod_sum(2)
            pe.wait_ge(idx_ready, 1 + IH // 2)
            for m in range(TT * IH // 4):
                n = STAGE[f"dots{m}"]
                begin(n)
                t = m // (IH // 4)
                for b in range(4):
                    hd = 4 * (m % (IH // 4)) + b
                    rows_ = slice(64 * (hd % 2), 64 * (hd % 2) + 64)
                    tok = slice(P * t, P * t + P)
                    last = three(bank(n, b), qi_hi[rows_, hd // 2, tok], qi_lo[rows_, hd // 2, tok],
                                 ki_hi[rows_, :], ki_lo[rows_, :], True, True)
                last.then_inc(stage_done, 1)
            group(G_LRU, STAGE["g3"], features_out, h)
            group(G_GATE, STAGE["g4"], features_out, h)
            mod_sum(3)
            pe.wait_ge(gates_in, 32)
            pe.wait_ge(branch_dve, CONV_DONE)
            for k, name in enumerate(("rgate", "igate")):
                n = STAGE[name]
                begin(n)
                for b in range(CT):
                    last = nc.tensor.matmul(bank(n, b), gates_w[:, k, b, :], xc[:, b, :], start=True, stop=True)
                last.then_inc(stage_done, 1)
            group(G_POOL, STAGE["g5"], features_out, h)
            group(G_K, STAGE["g6"], features_out, h)
            mod_sum(4)
            group(G_K + 1, STAGE["g7"], features_out, h)
            n = STAGE["poolmm"]
            begin(n)
            pe.wait_ge(pool_in, 16)
            pe.wait_ge(branch_dve, POOL_DIFF)
            for b in range(CT):
                last = nc.tensor.matmul(bank(n, b), pool_ws[:, b, :], (pool_b, pool_c)[b % 2][:, b, PAD:], start=True,
                                        stop=True)
            last.then_inc(stage_done, 1)
            group(G_Q, STAGE["g8"], features_out, h)
            n = STAGE["ssq"]
            begin(n)
            pe.wait_ge(branch_act, BRANCH_SQ)
            for b, sq in enumerate((pool_sq, lru_sq)):
                for t in range(CT):
                    last = nc.tensor.matmul(bank(n, b), ones[:], sq[:, t, :], start=t == 0, stop=t == CT - 1)
            last.then_inc(stage_done, 1)
            group(G_Q + 1, STAGE["g9"], features_out, h)
            group(G_V, STAGE["g10"], tokens_out, h)
            group(G_V + 1, STAGE["g11"], tokens_out, h)

            pe.wait_ge(act_freed, freed("A", STAGE["g11"] + 1))
            pe.wait_ge(dve_freed, freed("D", STAGE["g11"] + 1))

            def scores_of(it):
                hd, t = divmod(it, TT)
                if t == 0:
                    pe.wait_ge(q_lo_ready, hd + 1)
                    pe.wait_ge(k_lo_ready, hd + 1)
                if it >= 3:
                    pe.wait_ge(max_ready, it - 2)
                tok = slice(P * t, P * t + P)
                three(psum[:, S_BANK + it % 3, :], q_hi[:, hd % 2, tok], q_lo[:, hd, tok], k_hi[:, hd % 2, :],
                      k_lo[:, hd, :], True, True).then_inc(s_done, 1)

            def transpose_of(it):
                pe.wait_ge(probs_ready, it + 1)
                if it >= 2:
                    pe.wait_ge(pt_lo_ready, it - 1)
                for k in range(TT):
                    last = nc.tensor.transpose(psum[:, PT_BANK[it % 2], P * k:P * k + P],
                                               probs[:, it % PROB_SLOTS, P * k:P * k + P], ident[:])
                last.then_inc(pt_done, 1)

            def values_of(pair):
                hd, half = divmod(pair, TT // 2)
                if half == 0 and hd >= 2:
                    pe.wait_ge(o_ready, hd - 1)
                pe.wait_ge(pt_lo_ready, 2 * pair + 2)
                cols = slice(HD * hd, HD * hd + HD)
                o = psum[:, O_BANK + hd % 2, 2 * P * half:2 * P * half + 2 * P]
                for k in range(TT):
                    last = three(o, v_hi[:, k, cols], v_lo[:, k, cols], pt_hi[:, pair % 2, k, :], pt_lo[:, pair % 2, k, :],
                                 k == 0, k == TT - 1)
                last.then_inc(pv_done, 1)

            def square_sum(hd):
                pe.wait_ge(sq_ready, hd + 1)
                nc.tensor.matmul(psum[:, SQ_BANK, :], ones[:], attn_sq[:], start=hd == 0, stop=hd == HEADS - 1).then_inc(sq_used, 1)

            n_it = HEADS * TT
            for it in range(n_it + LAG_PV):
                if it < n_it:
                    scores_of(it)
                if 0 <= it - LAG_TURN < n_it:
                    transpose_of(it - LAG_TURN)
                v = it - LAG_PV
                if v >= 0 and v % 2:
                    values_of(v // 2)
                    if v % TT == 1 and v // TT >= 2:
                        square_sum(v // TT - 2)
            square_sum(HEADS - 2)
            square_sum(HEADS - 1)

            pe.wait_ge(o_ready, HEADS)
            pe.wait_ge(pt_lo_ready, HEADS * TT)
            for d in range(TT):
                group(PROJ_GROUPS + d, STAGE[f"out{d}"], tokens_out, (m_hi, m_lo),
                      ready=mixed_ready if d == 0 else None, tile=out_tile)
            mod_sum(5)

            n0, a0, d0 = len(STAGES), freed("A", len(STAGES)), freed("D", len(STAGES))
            pe.wait_ge(act_freed, a0)
            pe.wait_ge(dve_freed, d0)

            def turn_x1(kt):
                if kt >= 4:
                    pe.wait_ge(turned_used, kt - 3)
                transposed(psum[:, 4 * TURN_HALF + kt % 4, :], y1, kt).then_inc(turned, 1)

            def mlp_step(i, first_step):
                for u in range(UPG + DNG):
                    if not first_step or u >= UPG:
                        if u < UPG:
                            pe.wait_ge(dve_freed, i * DNG + (d0 - UPG + 1 + u))
                        elif u < 2 * UPG:
                            pe.wait_ge(act_freed, i * UPG + (a0 + 1 + u - UPG))
                        else:
                            pe.wait_ge(dve_freed, i * DNG + (d0 + u - 2 * UPG + 1))
                    elif u == 0:
                        pe.wait_ge(diag_ready, 2 * TT)
                        for kt in range(4):
                            turn_x1(kt)
                    else:
                        pe.wait_ge(turned_used, KD)
                    slabs, nk = (SG, KD) if u < UPG else (DS, HT)
                    first = SG * u if u < UPG else UPG * SG + DS * (u - UPG)
                    for j in range(slabs):
                        local = first + j
                        pe.wait_ge(lo_dve, i * STEP_SLABS + (MLP0 - PROJ_SLABS + local + 1))
                        for k in range(KS):
                            kt = KS * j + k
                            if u < UPG:
                                if first_step and u == 0:
                                    pe.wait_ge(h_ready, KD + kt + 1)
                                last = features_out(n0 + u, local % RING, k, (h2_hi, h2_lo), kt, kt == 0, kt == nk - 1)
                            else:
                                if u == UPG:
                                    pe.wait_ge(u2_ready, i * HT + (kt + 1))
                                last = tokens_out(n0 + u, local % RING, k, (u2_hi, u2_lo), kt, kt == 0, kt == nk - 1)
                        last.then_inc(slab_used, 1)
                        if first_step and u == 0:
                            for kt in range(KS * j + 4, min(KS * j + 4 + KS, KD)):
                                turn_x1(kt)

            mlp_step(0, True)
            with pe.Fori(1, STEPS) as i:
                mlp_step(i, False)

        @block.scalar
        def _(act):
            ch = Chain(act, act_chain)

            def split(s):
                act.wait_ge(raw_landed[s % RING], 16 * (s // RING + 1))
                if s >= RING:
                    act.wait_ge(slab_used, s - RING + 1)
                r, hi = raw[:, s % RING, :, :], w_hi[:, s % RING, :, :]
                if s < SG:
                    ch.link(nc.scalar.activation(hi[:, :, 0:64], r[:, :, 0:64], ACT.Copy))
                    r, hi = r[:, :, 0:192], hi[:, :, 64:256]
                nc.scalar.activation(hi, r, ACT.Copy).then_inc(hi_ready, 1)

            def done(name):
                wait_stage(act, name)

            def squares(src, dst, col, after=None):
                return nc.scalar.activation(dst, src, ACT.Square, accum_out=col)

            def evacuate(name, dst, n, banks):
                done(name)
                for b in banks:
                    ch.put(nc.scalar.activation(dst[:, 4 * n + b, :], bank(STAGE[name], b), ACT.Copy))
                ch.wait()
                act.sem_inc(act_freed, 1)

            def h_high(sub, k, src, dst):
                nc.scalar.activation(dst[:, k, :], src, ACT.Identity, bias=mod[:, (1, 4)[sub], k:k + 1],
                                     scale=mul[:, sub, k:k + 1]).then_inc(h_hi_ready, 1)

            act.dma_start(pos_ki[:], positions[0:1, :].to_broadcast([P, T])).then_inc(pos_in, 16)
            act.dma_start(pos_qi[0:TT, :], positions.rearrange("a (r p) -> (a r) p", p=P)).then_inc(pos_in, 16)
            act.wait_ge(consts, 1)
            for q in range(4):
                act.dma_start(rb[32 * q:32 * q + NBUCKET, :], rel_bias).then_inc(rb_in, 16)
                act.dma_start(rb_prev[32 * q + 1:32 * q + NBUCKET, :], rel_bias[0:NBUCKET - 1, :]).then_inc(rb_in, 16)
            act.wait_ge(c_copied, 1)
            nc.scalar.activation(c_tmp[:], c_col[:], ACT.Tanh, scale=0.5).then_inc(c_tanh, 1)
            act.wait_ge(vec_ready, 3)
            nc.scalar.activation(lam_t[:, 1, :], lam_t[:, 0, :], ACT.Exp, scale=-1.0).then_inc(c_tanh, 1)
            act.wait_ge(consts, 2)

            def bias_store(k):
                act.wait_ge(act_chain, bias_at[k])
                act.dma_start(bias_s[P * k:P * k + P, :], bias_out[:, k % 4, :]).then_inc(bias_stored[k % 4], 16)

            bias_at = []
            xs = 0
            for m in range(8):
                done(f"bias{m}")
                for b in range(4):
                    k = 4 * m + b
                    if k >= 4:
                        act.wait_ge(bias_stored[k % 4], 16 * (k // 4))
                    bias_at.append(ch.put(nc.scalar.activation(bias_out[:, k % 4, :], bank(STAGE[f"bias{m}"], b), ACT.Copy)))
                    if b == 3:
                        ch.wait()
                        act.sem_inc(act_freed, 1)
                    bias_store(k)
                t = m - 2
                if 0 <= t < TT:
                    act.wait_ge(x_landed[t], 16)
                    if t:
                        act.wait_ge(ssq_ready, t)
                    squares(x_tok[:, t, :], junk[:], stat[:, 0, t:t + 1]).then_inc(ssq_ready, 1)
                if t == TT - 1:
                    act.wait_ge(ssq_ready, TT)
                    nc.scalar.activation(stat[:, 1, 0:TT], stat[:, 0, 0:TT], ACT.Sqrt, bias=eps_c[:],
                                         scale=1.0 / D).then_inc(root_ready, 1)
            for n in range(TT):
                evacuate(f"xt{n}", x_t, n, (0, 1))
            s = 0
            split(0)
            split(1)
            act.wait_ge(mul_ready, 1)
            act.wait_ge(dve_freed, freed("D", STAGE["xt3"] + 1))
            for stored in bias_stored:
                act.wait_ge(stored, 16 * 8)
            for k in range(KD):
                h_high(0, k, x_t[:, k, :], h_hi)

            def split_to(s, upto):
                while s < upto:
                    split(s)
                    s += 1
                return s

            s = split_to(2, SG + 3)
            done("g0")
            n = STAGE["g0"]
            nc.scalar.activation(ki_hi[:], bank(n, 0), ACT.Copy).then_inc(act_hi, 1)
            nc.scalar.activation(widx_t[0:IH, :], bank(n, 1)[0:IH, :], ACT.Copy).then_inc(widx_copied, 1)
            act.wait_ge(widx_copied, 1)
            act.wait_ge(act_hi, 1)
            act.sem_inc(act_freed, 1)
            for g in (1, 2):
                s = split_to(s, SG * (g + 1) + 3)
                done(f"g{g}")
                for b in range(4):
                    nc.scalar.activation(qi_hi[:, 4 * (g - 1) + b, :], bank(STAGE[f"g{g}"], b), ACT.Copy).then_inc(act_hi, 1)
                act.wait_ge(act_hi, 1 + 4 * g)
                act.sem_inc(act_freed, 1)
            for m in range(TT * IH // 4):
                done(f"dots{m}")
                for b in range(4):
                    k = 4 * m + b
                    if k >= 2:
                        act.wait_ge(relu_used, k - 1)
                    nc.scalar.activation(relu[:, k % 2, :], bank(STAGE[f"dots{m}"], b), ACT.Relu).then_inc(relu_ready, 1)
                act.wait_ge(relu_ready, 4 * m + 4)
                act.sem_inc(act_freed, 1)

            def copy_out(name, dst, scale=1.0, after=None):
                done(name)
                for b in range(4):
                    ch.put(nc.scalar.activation(dst(b), bank(STAGE[name], b), ACT.Copy, scale=scale))
                ch.wait()
                act.sem_inc(act_freed, 1)

            s = split_to(s, SG * 4 + 3)
            act.wait_ge(score_done, TT)
            copy_out("g3", lambda b: lru_in[:, b, :])
            act.sem_inc(branch_act, 1)
            s = split_to(s, SG * 5 + 3)
            copy_out("g4", lambda b: gate_in[:, b, :])
            act.sem_inc(branch_act, 1)
            for k, (name, dst) in enumerate((("rgate", r_t), ("igate", i_t))):
                done(name)
                for b in range(CT):
                    ch.put(nc.scalar.activation(dst[:, b, :], bank(STAGE[name], b), ACT.Tanh, bias=half_b[:, k, b:b + 1],
                                                scale=0.5))
                ch.wait()
                act.sem_inc(act_freed, 1)
            act.sem_inc(branch_act, 1)
            act.wait_ge(branch_dve, U_ARG)
            ch.link(nc.scalar.activation(r_t[:], r_t[:], ACT.Tanh))
            act.sem_inc(branch_act, 1)
            s = split_to(s, SG * 5 + 5)
            ch.link(nc.scalar.activation(lru_in[:], r_t[:], ACT.Sqrt, scale=-1.0))
            act.sem_inc(branch_act, 1)
            act.wait_ge(branch_dve, SCANNED)
            ch.link(nc.scalar.activation(r_t[:], gate_in[:], ACT.Square))
            act.sem_inc(branch_act, 1)
            s = split_to(s, SG * 6 + 3)
            act.wait_ge(branch_dve, GELU_ARG)
            ch.link(nc.scalar.activation(lru_in[:], r_t[:], ACT.Tanh, scale=float(np.sqrt(2 / np.pi))))
            act.sem_inc(branch_act, 1)
            act.wait_ge(branch_dve, LRU_DONE)
            copy_out("g5", lambda b: pool_u[:, b, PAD:])
            act.sem_inc(branch_act, 1)
            s = split_to(s, SG * 7 + 3)
            act.wait_ge(mod_step, MOD_EARLY + MOD_PROJ)
            copy_out("g6", lambda b: k_t[:, b, :])
            s = split_to(s, SG * 8 + 3)
            copy_out("g7", lambda b: k_t[:, 4 + b, :])
            act.wait_ge(mask_done, TT)
            done("poolmm")
            n = STAGE["poolmm"]
            for b in range(CT):
                o = at_b["pool_scale"] + b
                ch.put(nc.scalar.activation(pool_o[:, b, :], bank(n, b), ACT.Copy, scale=col_b[:, o:o + 1]))
            ch.wait()
            act.sem_inc(act_freed, 1)
            nc.scalar.activation(pool_sq[:], pool_o[:], ACT.Square).then_inc(branch_act, 1)
            nc.scalar.activation(lru_sq[:], lru_o[:], ACT.Square).then_inc(branch_act, 1)
            act.wait_ge(dve_freed, freed("D", STAGE["mod4"] + 1))
            s = split_to(s, SG * 9 + 3)
            done("ssq")
            copy_out("g8", lambda b: q_t[:, b, :], scale=HD ** -0.5)
            for b in range(2):
                ch.put(nc.scalar.activation(rnorm[:, b, :], bank(STAGE["ssq"], b), ACT.Sqrt, bias=eps_c[:], scale=1.0 / GW))
            ch.wait()
            act.sem_inc(act_freed, 1)
            act.sem_inc(root_ready, 1)
            s = split_to(s, SG * 10 + 3)
            copy_out("g9", lambda b: q_t[:, 4 + b, :], scale=HD ** -0.5)
            for g in (10, 11):
                s = split_to(s, SG * (g + 1) + 3)
                done(f"g{g}")
                for b in range(TT):
                    c0 = 512 * (g - 10)
                    nc.scalar.activation(v_hi[:, b, c0:c0 + 512], bank(STAGE[f"g{g}"], b), ACT.Copy).then_inc(act_hi, 1)
                act.wait_ge(act_hi, 9 + 4 * (g - 9))
                act.sem_inc(act_freed, 1)

            def head_split(hd):
                if hd >= 2:
                    act.wait_ge(s_done, TT * (hd - 1))
                nc.scalar.activation(q_hi[:, hd % 2, :], q_t[:, hd, :], ACT.Copy).then_inc(qk_hi, 1)
                nc.scalar.activation(k_hi[:, hd % 2, :], k_t[:, hd, :], ACT.Copy).then_inc(qk_hi, 1)

            def exps(it):
                act.wait_ge(max_ready, it + 1)
                j = it % PROB_SLOTS
                nc.scalar.activation(probs[:, j, :], probs[:, j, :], ACT.Exp, bias=nmax[:, j:j + 1], scale=-1.0,
                                     accum_out=asum[:, j:j + 1]).then_inc(exp_ready, 1)

            def pt_split(it):
                act.wait_ge(pt_done, it + 1)
                pair, half = divmod(it, 2)
                if pair >= 2:
                    act.wait_ge(pv_done, pair - 1)
                nc.scalar.activation(pt_hi[:, pair % 2, :, P * half:P * half + P],
                                     psum[:, PT_BANK[it % 2], :].rearrange("p (k q) -> p k q", k=TT), ACT.Copy).then_inc(pt_hi_ready, 1)

            def head_out(hd):
                act.wait_ge(pv_done, TT // 2 * (hd + 1))
                nc.scalar.activation(attn[:, hd, :], psum[:, O_BANK + hd % 2, :], ACT.Copy).then_inc(o_ready, 1)

            head_split(0)
            head_split(1)
            n_it = HEADS * TT
            for it in range(n_it + LAG_PV + 1):
                if 0 <= it - LAG_EXP < n_it:
                    exps(it - LAG_EXP)
                if 0 <= it - LAG_HI < n_it:
                    pt_split(it - LAG_HI)
                if it % TT == 1 and 2 <= it // TT + 1 < HEADS:
                    head_split(it // TT + 1)
                if it > LAG_PV and (it - LAG_PV) % TT == 0:
                    head_out((it - LAG_PV) // TT - 1)

            act.wait_ge(rinv_ready, 1)
            act.wait_ge(pt_lo_ready, HEADS * TT)
            act.wait_ge(pv_done, HEADS * TT // 2)
            for n in range(KD):
                k = out_tile(n)
                if k < HEADS:
                    if k == 0:
                        act.wait_ge(sq_used, HEADS)
                        nc.scalar.activation(rnorm[:, 0, :], psum[:, SQ_BANK, :], ACT.Sqrt, bias=eps_c[:],
                                             scale=1.0 / AW).then_inc(root_ready, 1)
                    act.wait_ge(mixed_full, k + 1)
                    src = mixed[:, k, :]
                else:
                    src = pool_o[:, k - HEADS, :] if k < HEADS + CT else lru_o[:, k - HEADS - CT, :]
                nc.scalar.activation(m_hi[:, k, :], src, ACT.Copy).then_inc(mixed_hi, 1)
            n0 = len(STAGES)

            def split_mlp(i, local):
                act.wait_ge(raw_landed[local % RING], i * (16 * STEP_SLABS // RING) + 16 * ((MLP0 + local) // RING + 1))
                act.wait_ge(slab_used, i * STEP_SLABS + (MLP0 + local - RING + 1))
                nc.scalar.activation(w_hi[:, local % RING, :, :], raw[:, local % RING, :, :], ACT.Copy).then_inc(hi_ready, 1)

            for d in range(TT):
                s = split_to(s, min(SG * (PROJ_GROUPS + d + 1) + 3, MLP0))
                if d == TT - 1:
                    for local in range(RING - 1):
                        split_mlp(0, local)
                done(f"out{d}")
                for t in range(TT):
                    k = TT * d + t
                    if k:
                        act.wait_ge(out_squared, k)
                    squares(bank(STAGE[f"out{d}"], t), sq_out[:], stat[:, 3 + d, t:t + 1]).then_inc(out_squared, 1)
                act.wait_ge(out_squared, TT * d + TT)
                act.sem_inc(act_freed, 1)
            act.wait_ge(rinv_ready, 2)
            nc.scalar.activation(stat[:, 1, 0:TT], stat[:, 0, 0:TT], ACT.Sqrt, bias=eps_c[:], scale=1.0 / D).then_inc(root_ready, 1)
            split_mlp(0, RING - 1)
            for t in range(TT):
                act.wait_ge(x1_ready, t + 1)
                ch.link(squares(y1[:, t, :], slab_1[:], stat[:, 0, 4 + t:5 + t]))
                nc.scalar.activation(stat[:, 1, 4 + t:5 + t], stat[:, 0, 4 + t:5 + t], ACT.Sqrt, bias=eps_c[:],
                                     scale=1.0 / D).then_inc(root_ready, 1)
            act.wait_ge(mul_ready, 2)
            for k in range(KD):
                act.wait_ge(turned, k + 1)
                h_high(1, k, psum[:, 4 * TURN_HALF + k % 4, :], h2_hi)
                if k % KS == KS - 1 and k >= 3:
                    split_mlp(0, RING + (k - 3) // KS)

            def up_stage(i, u):
                act.wait_ge(slab_used, i * STEP_SLABS + (MLP0 + SG * (u + 1)))
                for b in range(4):
                    if not isinstance(i, int) or 4 * u + b >= 2:
                        act.wait_ge(up_used, i * HT + (4 * u + b - 1))
                    nc.scalar.activation(u_relu[:, b % 2, :], bank(n0 + u, b), ACT.Relu).then_inc(up_relu, 1)
                act.wait_ge(up_relu, i * HT + (4 * u + 4))
                act.sem_inc(act_freed, 1)

            def mlp_step(i, begin):
                for local in range(STEP_SLABS):
                    if local >= begin:
                        split_mlp(i, local)
                    if local in (SG + 2, 2 * SG + 2):
                        up_stage(i, (local - 2) // SG - 1)

            mlp_step(0, EARLY_SPLITS)
            with act.Fori(1, STEPS) as i:
                mlp_step(i, 0)
            act.wait_ge(dve_freed, freed("D", n0) + DNG * STEPS)
            for t in range(TT):
                ch.link(squares(y2[:, t, :], junk2[:], stat[:, 0, 8 + t:9 + t]))
            nc.scalar.activation(stat[:, 1, 0:TT], stat[:, 0, 8:8 + TT], ACT.Sqrt, bias=eps_c[:], scale=1.0 / D).then_inc(root_ready, 1)

        @block.vector
        def _(dve):
            ch = Chain(dve, dve_chain)
            V = nc.vector

            def done(name):
                wait_stage(dve, name)

            def free():
                ch.wait()
                dve.sem_inc(dve_freed, 1)

            def cols(table, name, n):
                tile, at_ = (col_a, at_a) if table == "a" else (col_b, at_b)
                return tile[:, at_[name]:at_[name] + n]

            def rsqrt(v_src, n, dst, scale, tmp, root=None):
                root = stat[:, 1, 0:n] if root is None else root
                v = stat[:, 7, 0:n]
                ch.link(V.tensor_scalar(v, v_src, scale, EPS, ALU.mult, ALU.add))
                ch.link(V.reciprocal(dst, root))
                ch.link(V.tensor_tensor(tmp, dst, dst, ALU.mult))
                ch.link(V.tensor_tensor(tmp, tmp, v, ALU.mult))
                ch.link(V.tensor_scalar(tmp, tmp, -0.5, 1.5, ALU.mult, ALU.add))
                ch.link(V.tensor_tensor(dst, dst, tmp, ALU.mult))

            done("c")
            ch.put(V.tensor_copy(c_col[:], bank(STAGE["c"], 0)[:, 0:KD]))
            free()
            dve.sem_inc(c_copied, 1)
            dve.wait_ge(pos_in, 32)
            ch.put(V.tensor_copy(pos_k[:], pos_ki[:]))
            V.tensor_copy(pos_qf[0:TT, :], pos_qi[0:TT, :]).then_inc(vec_ready, 1)
            done("vec")
            n = STAGE["vec"]
            na, nb = sum(v.shape[0] for _, v in vec_a_rows), sum(v.shape[0] for _, v in vec_b_rows)
            ch.put(V.tensor_copy(col_a[:, 0:na], bank(n, 0)[:, 0:na]))
            ch.put(V.tensor_copy(col_b[:, 0:nb], bank(n, 1)[:, 0:nb]))
            ch.put(V.tensor_copy(pos_q[:], bank(n, 2)[:, 0:TT]))
            ch.put(V.tensor_copy(start_col[:], bank(n, 3)[:, 0:1]))
            free()
            dve.sem_inc(vec_ready, 1)
            for q in range(4):
                r32 = slice(32 * q, 32 * q + 32)
                ch.put(V.tensor_scalar(reach[r32, :], pos_k[r32, P * q:P * q + P], start_col[r32, :], None, ALU.subtract))
            ch.wait()
            dve.sem_inc(reach_ready, 1)
            dve.wait_ge(c_tanh, 1)
            ch.link(V.scalar_tensor_tensor(c_act[:], c_tmp[:], 1.0, c_col[:], ALU.add, ALU.mult))
            ch.link(V.tensor_scalar(c_act[:], c_act[:], 0.5, None, ALU.mult))
            lam = cols("b", "lam", CT)
            ch.link(V.tensor_scalar(lam_t[:, 2, :], lam, -1.0, None, ALU.mult))
            ch.link(V.tensor_tensor(lam_t[:, 0, :], lam_t[:, 2, :], lam, ALU.max))
            ch.link(V.tensor_scalar(lam_t[:, 2, :], lam_t[:, 2, :], 0.0, None, ALU.max))
            for k, name in enumerate(("r_b", "i_b")):
                ch.put(V.tensor_scalar(half_b[:, k, :], cols("b", name, CT), 0.5, None, ALU.mult))
            ch.wait()
            dve.sem_inc(vec_ready, 1)
            e_, z, z2, sp_ = lam_t[:, 1, :], lam_t[:, 3, :], lam_t[:, 4, :], lam_t[:, 5, :]

            def softplus():
                dve.wait_ge(c_tanh, 2)
                ch.link(V.tensor_scalar(z, e_, 2.0, None, ALU.add))
                ch.link(V.reciprocal(z, z))
                ch.link(V.tensor_tensor(z, z, e_, ALU.mult))
                ch.link(V.tensor_tensor(z2, z, z, ALU.mult))
                ch.link(V.tensor_scalar(sp_, z2, 1.0 / 17, 1.0 / 15, ALU.mult, ALU.add))
                for odd in (13, 11, 9, 7, 5, 3, 1):
                    ch.link(V.tensor_tensor(sp_, sp_, z2, ALU.mult))
                    ch.link(V.tensor_scalar(sp_, sp_, 1.0 / odd, None, ALU.add))
                ch.link(V.tensor_tensor(sp_, sp_, z, ALU.mult))
                ch.link(V.scalar_tensor_tensor(sp_, sp_, 2.0, lam_t[:, 2, :], ALU.mult, ALU.add))
                ch.link(V.tensor_scalar(sp_, sp_, -LRU_C / 4, None, ALU.mult))

            def mod_add(g):
                j, k = divmod(g, KD)
                acc = acc_b if j % 2 else acc_a
                slab = (slab_0, slab_1)[g % 2][:] if j == 5 else mod_slab[:, g % 2, :]
                dve.wait_ge(mod_landed[g % 2], 16 * (g // 2 + 1))
                if k == 0:
                    if j >= 2:
                        wait_stage(dve, f"mod{j - 2}")
                    V.tensor_scalar(acc[:], slab, c_act[:, k:k + 1], None, ALU.mult).then_inc(mod_step, 1)
                else:
                    dve.wait_ge(mod_step, g)
                    V.scalar_tensor_tensor(acc[:], slab, c_act[:, k:k + 1], acc[:], ALU.mult, ALU.add).then_inc(mod_step, 1)

            def mod_out(j):
                done(f"mod{j}")
                table = "a" if f"b_mod{j}" in at_a else "b"
                ch.link(V.tensor_tensor(mod[:, j, :], bank(STAGE[f"mod{j}"], 0)[:, 0:KD], cols(table, f"b_mod{j}", KD), ALU.add))
                dve.sem_inc(dve_freed, 1)
                if j in (2, 5):
                    ch.link(V.tensor_tensor(mod[:, j, :], mod[:, j, :], cols("b", "g_post1" if j == 2 else "g_post2", KD), ALU.mult))
                    dve.sem_inc(gate_col, 1)
                if j in (0, 3):
                    k = j // 3
                    ch.link(V.scalar_tensor_tensor(mul[:, k, :], mod[:, j, :], 1.0, cols("a", f"g_pre{k + 1}", KD), ALU.add, ALU.mult))
                if j in (1, 4):
                    dve.sem_inc(mul_ready, 1)

            def evacuate(name, dst, n, banks):
                done(name)
                for b in banks:
                    ch.put(V.tensor_copy(dst[:, 4 * n + b, :], bank(STAGE[name], b)))
                free()

            def scaled_identity(first, end, at_):
                for t in range(first, end):
                    V.tensor_scalar(diag[:, t, :], ident[:], stat[:, 2, at_ + t:at_ + t + 1], None, ALU.mult).then_inc(diag_ready, 1)

            for g in range(MOD_EARLY):
                mod_add(g)
                for k in range(16 * g // 3, min(16 * (g + 1) // 3, P)):
                    if k % 4 < 3:
                        if k >= 4:
                            dve.wait_ge(step_used, k - 3)
                        V.tensor_scalar(steps[:, k % 4, :], pos_k[:], reach[:, k:k + 1], None, ALU.is_le).then_inc(step_dve, 1)
                if g == 20:
                    softplus()
                if g == 25:
                    dve.wait_ge(root_ready, 1)
                    rsqrt(stat[:, 0, 0:TT], TT, stat[:, 2, 0:TT], 1.0 / D, stat[:, 2, 8:8 + TT])
                    scaled_identity(0, TT, 0)
                if g >= 28:
                    evacuate(f"xt{g - 28}", x_t, g - 28, (2, 3))

            def h_low(sub, k, src, hi, lo):
                ch.link(V.tensor_scalar(h_full[:, k % 2, :], src, mul[:, sub, k:k + 1], mod[:, (1, 4)[sub], k:k + 1],
                                        ALU.mult, ALU.add))
                V.tensor_tensor(lo[:, k, :], h_full[:, k % 2, :], hi[:, k, :].bitcast(F32), ALU.subtract).then_inc(h_ready, 1)

            mod_out(0)
            mod_out(1)
            dve.wait_ge(act_freed, freed("A", STAGE["xt3"] + 1))
            for k in range(KD):
                dve.wait_ge(h_hi_ready, k + 1)
                h_low(0, k, x_t[:, k, :], h_hi, h_lo)

            def beside(s):
                if s < MOD_PROJ:
                    mod_add(MOD_EARLY + s)
                if TOPK_AT <= s < TOPK_AT + TT * ROUNDS // 2:
                    for r in (2 * (s - TOPK_AT), 2 * (s - TOPK_AT) + 1):
                        topk_round(*divmod(r, ROUNDS))

            def is_late(t):
                ch.link(V.tensor_scalar(late[:], pos_k[:], pos_q[:, t:t + 1], None, ALU.is_gt))

            def topk_round(t, r):
                ch.link(V.max(top8[:], score[:, t, :]))
                ch.link(V.match_replace(score[:, t, :], top8[:], score[:, t, :], TAKEN))
                if r == ROUNDS - 1:
                    is_late(t)
                    ch.link(V.scalar_tensor_tensor(score[:, t, :], score[:, t, :], TAKEN / 2, late[:], ALU.is_gt, ALU.max))
                    if t == 0:
                        wait_stage(dve, "igate")
                    V.tensor_scalar(mask[:, t, :], score[:, t, :], NEG, None, ALU.mult).then_inc(mask_done, 1)

            def beside_to(s, upto):
                while s < upto:
                    beside(s)
                    s += 1
                return s

            def low(dst, stage, b, hi, signal, n_hi):
                dve.wait_ge(act_hi, n_hi)
                V.tensor_tensor(dst, bank(stage, b), hi.bitcast(F32), ALU.subtract).then_inc(signal, 1)

            s = beside_to(0, SG + 3)
            done("g0")
            low(ki_lo[:], STAGE["g0"], 0, ki_hi[:], idx_ready, 1)
            dve.wait_ge(idx_ready, 1)
            dve.sem_inc(dve_freed, 1)
            for g in (1, 2):
                s = beside_to(s, SG * (g + 1) + 3)
                done(f"g{g}")
                for b in range(4):
                    k = 4 * (g - 1) + b
                    low(qi_lo[:, k, :], STAGE[f"g{g}"], b, qi_hi[:, k, :], idx_ready, 2 + k)
                dve.wait_ge(idx_ready, 1 + 4 * g)
                dve.sem_inc(dve_freed, 1)
            done("widx")
            for t in range(TT):
                ch.put(V.tensor_scalar(w_idx[:, t, :], bank(STAGE["widx"], 0)[:, IH * t:IH * t + IH], (IH * ID) ** -0.5, None,
                                       ALU.mult))
            free()
            mod_out(2)
            for k in range(TT * IH):
                t, hd = divmod(k, IH)
                if hd == 0:
                    ch.link(V.tensor_scalar(score[:, t, :], pos_k[:], pos_q[:, t:t + 1], NEG, ALU.is_gt, ALU.mult))
                dve.wait_ge(relu_ready, k + 1)
                if hd:
                    dve.wait_ge(relu_used, k)
                V.scalar_tensor_tensor(score[:, t, :], relu[:, k % 2, :], w_idx[:, t, hd:hd + 1], score[:, t, :], ALU.mult,
                                       ALU.add).then_inc(relu_used, 1)
                if hd == IH - 1:
                    dve.wait_ge(relu_used, k + 1)
                    dve.sem_inc(score_done, 1)

            s = beside_to(s, SG * 4 + 3)
            dve.wait_ge(branch_act, 1)
            taps = cols("b", "conv_w", 4 * CT)
            for b in range(CT):
                tap = [taps[:, CT * j + b:CT * j + b + 1] for j in range(4)]
                ch.link(V.tensor_scalar(xc[:, b, :], lru_in[:, b, :], tap[3], cols("b", "conv_b", CT)[:, b:b + 1], ALU.mult, ALU.add))
                for j in (2, 1, 0):
                    w = 3 - j
                    ch.link(V.scalar_tensor_tensor(xc[:, b, w:], lru_in[:, b, :T - w], tap[j], xc[:, b, w:], ALU.mult, ALU.add))
            dve.sem_inc(branch_dve, 1)
            s = beside_to(s, SG * 5)
            mod_out(3)
            s = beside_to(s, SG * 5 + 3)
            dve.wait_ge(branch_act, 3)
            for b in range(CT):
                ch.put(V.tensor_scalar(r_t[:, b, :], r_t[:, b, :], 1.0, sp_[:, b:b + 1], ALU.add, ALU.mult))
            ch.wait()
            dve.sem_inc(branch_dve, 1)
            ch.link(V.scalar_tensor_tensor(xc[:], i_t[:], 1.0, xc[:], ALU.add, ALU.mult))
            dve.wait_ge(branch_act, 4)
            ch.link(V.tensor_scalar(i_t[:], r_t[:], -1.0, 1.0, ALU.mult, ALU.add))
            ch.link(V.reciprocal(i_t[:], i_t[:]))
            ch.link(V.tensor_tensor(xc[:], xc[:], i_t[:], ALU.mult))
            dve.wait_ge(branch_act, 5)
            ch.link(V.tensor_tensor(xc[:], xc[:], lru_in[:], ALU.mult))
            ch.link(V.scalar_tensor_tensor(r_t[:], r_t[:], 1.0, i_t[:], ALU.add, ALU.mult))
            for b in range(CT):
                ch.put(V.tensor_tensor_scan(i_t[:, b, :], r_t[:, b, :], xc[:, b, :], 0.0, ALU.mult, ALU.add))
            ch.wait()
            dve.sem_inc(branch_dve, 1)
            s = beside_to(s, SG * 5 + 6)
            dve.wait_ge(branch_act, 6)
            ch.link(V.tensor_scalar(r_t[:], r_t[:], 0.044715, 1.0, ALU.mult, ALU.add))
            ch.link(V.tensor_tensor(r_t[:], r_t[:], gate_in[:], ALU.mult))
            dve.sem_inc(branch_dve, 1)
            dve.wait_ge(branch_act, 7)
            ch.link(V.scalar_tensor_tensor(gate_in[:], lru_in[:], 1.0, gate_in[:], ALU.add, ALU.mult))
            wait_stage(dve, "mod3")
            ch.link(V.scalar_tensor_tensor(lru_o[:], i_t[:], 0.5, gate_in[:], ALU.mult, ALU.mult))
            dve.sem_inc(branch_dve, 1)
            s = beside_to(s, SG * 6 + 5)
            for t_ in (pool_u, pool_b, pool_c):
                ch.put(V.memset(t_[:, :, 0:PAD], 0.0))
            ch.wait()
            dve.wait_ge(branch_act, 8)
            src, dst, w = pool_u, pool_b, 1
            for b in range(CT):
                ch.link(V.tensor_tensor(dst[:, b:, PAD:], src[:, b:, PAD:], src[:, b:, PAD - w:PAD - w + T], ALU.add))
                src, dst, w = dst, (pool_c if dst is pool_b else pool_b), 2 * w
            for b in range(CT):
                win = 2 ** (b + 1)
                o = (pool_b, pool_c)[b % 2]
                ch.link(V.tensor_tensor(pool_fix[:, b, 0:win], o[:, b, PAD:PAD + win], inv_n[:, 0:win], ALU.mult))
                ch.link(V.scalar_tensor_tensor(o[:, b, PAD:], o[:, b, PAD:], 1.0 / win, pool_u[:, b, PAD:], ALU.mult, ALU.subtract))
                ch.link(V.tensor_tensor(o[:, b, PAD:PAD + win], pool_fix[:, b, 0:win], pool_u[:, b, PAD:PAD + win], ALU.subtract))
            dve.sem_inc(branch_dve, 1)
            s = beside_to(s, SG * 7 + 3)
            mod_out(4)
            s = beside_to(s, TOPK_AT + TT * ROUNDS // 2)
            dve.wait_ge(root_ready, 2)
            for k, (o, g) in enumerate(((pool_o, "g_pool"), (lru_o, "g_lru"))):
                ch.link(V.reciprocal(rnorm[:, k, :], rnorm[:, k, :]))
                for b in range(CT):
                    ch.put(V.scalar_tensor_tensor(o[:, b, :], o[:, b, :], cols("b", g, CT)[:, b:b + 1], rnorm[:, k, :],
                                                  ALU.mult, ALU.mult))
            ch.wait()
            dve.sem_inc(rinv_ready, 1)
            for g in (10, 11):
                done(f"g{g}")
                for b in range(TT):
                    c0 = 512 * (g - 10)
                    k = 4 * (g - 10) + b
                    low(v_lo[:, b, c0:c0 + 512], STAGE[f"g{g}"], b, v_hi[:, b, c0:c0 + 512], idx_ready, 10 + k)
                dve.wait_ge(idx_ready, 9 + 4 * (g - 9))
                dve.sem_inc(dve_freed, 1)

            def split(s):
                dve.wait_ge(hi_ready, s + 1)
                V.tensor_tensor(w_lo[:, s % RING, :, :], raw[:, s % RING, :, :], w_hi[:, s % RING, :, :].bitcast(F32),
                                ALU.subtract).then_inc(lo_dve, 1)

            for s in range(PROJ_SLABS, PROJ_SLABS + 3):
                split(s)

            def head_split(hd):
                dve.wait_ge(qk_hi, 2 * hd + 1)
                V.tensor_tensor(q_lo[:, hd, :], q_t[:, hd, :], q_hi[:, hd % 2, :].bitcast(F32), ALU.subtract).then_inc(q_lo_ready, 1)

            def logits(it):
                hd, t = divmod(it, TT)
                dve.wait_ge(bm_ready, it + 1)
                dve.wait_ge(s_done, it + 1)
                if it >= PROB_SLOTS:
                    dve.wait_ge(pt_done, it - PROB_SLOTS + 1)
                j = it % PROB_SLOTS
                V.tensor_tensor_reduce(out=probs[:, j, :], in0=psum[:, S_BANK + it % 3, :], in1=bm[:, it % BM_SLOTS, :], scale=-1.0,
                                       scalar=3e38, op0=ALU.add, op1=ALU.min, accum_out=nmax[:, j:j + 1]).then_inc(max_ready, 1)

            def normalise(it):
                j = it % PROB_SLOTS
                dve.wait_ge(exp_ready, it + 1)
                ch.link(V.reciprocal(arec[:, j:j + 1], asum[:, j:j + 1]))
                V.tensor_scalar(probs[:, j, :], probs[:, j, :], arec[:, j:j + 1], None, ALU.mult).then_inc(probs_ready, 1)

            def pt_split(it):
                dve.wait_ge(pt_hi_ready, it + 1)
                pair, half = divmod(it, 2)
                q = slice(P * half, P * half + P)
                V.tensor_tensor(pt_lo[:, pair % 2, :, q], psum[:, PT_BANK[it % 2], :].rearrange("p (k q) -> p k q", k=TT),
                                pt_hi[:, pair % 2, :, q].bitcast(F32), ALU.subtract).then_inc(pt_lo_ready, 1)

            head_split(0)
            head_split(1)
            n_it = HEADS * TT
            for it in range(n_it + LAG_LO):
                if it < n_it:
                    logits(it)
                if 0 <= it - LAG_NORM < n_it:
                    normalise(it - LAG_NORM)
                if 0 <= it - LAG_LO < n_it:
                    pt_split(it - LAG_LO)
                if it % TT == 2 and 2 <= it // TT + 1 < HEADS:
                    head_split(it // TT + 1)

            for n in range(KD):
                k = out_tile(n)
                if k < HEADS:
                    if k == 0:
                        dve.wait_ge(root_ready, 3)
                        ch.link(V.reciprocal(rnorm[:, 0, :], rnorm[:, 0, :]))
                    src = mixed[:, k, :]
                    V.scalar_tensor_tensor(src, attn[:, k, :], cols("b", "g_attn", HEADS)[:, k:k + 1], rnorm[:, 0, :],
                                           ALU.mult, ALU.mult).then_inc(mixed_full, 1)
                    dve.wait_ge(mixed_full, k + 1)
                else:
                    src = pool_o[:, k - HEADS, :] if k < HEADS + CT else lru_o[:, k - HEADS - CT, :]
                dve.wait_ge(mixed_hi, n + 1)
                V.tensor_tensor(m_lo[:, k, :], src, m_hi[:, k, :].bitcast(F32), ALU.subtract).then_inc(mixed_ready, 1)

            def split_mlp(i, local):
                dve.wait_ge(hi_ready, i * STEP_SLABS + (MLP0 + local + 1))
                V.tensor_tensor(w_lo[:, local % RING, :, :], raw[:, local % RING, :, :],
                                w_hi[:, local % RING, :, :].bitcast(F32), ALU.subtract).then_inc(lo_dve, 1)

            s = PROJ_SLABS + 3
            g = 5 * KD
            for d in range(TT):
                while s < min(SG * (PROJ_GROUPS + d + 1) + 3, MLP0):
                    split(s)
                    if s % 2 and g < 6 * KD:
                        mod_add(g)
                        g += 1
                    s += 1
                if d == TT - 1:
                    while g < 6 * KD:
                        mod_add(g)
                        g += 1
                    for local in range(RING - 1):
                        split_mlp(0, local)
                done(f"out{d}")
                if d == 0:
                    dve.wait_ge(g_landed, 16)
                for t in range(TT):
                    dve.wait_ge(out_squared, TT * d + t + 1)
                    if d == TT - 1 and t == TT - 1:
                        ch.link(V.tensor_reduce(stat[:, 0, 0:TT], stat[:, 3:7, 0:TT].rearrange("p d t -> p t d"), AXX, ALU.add))
                        dve.sem_inc(rinv_ready, 1)
                    ch.put(V.tensor_tensor(y1[:, t, 512 * d:512 * d + 512], bank(STAGE[f"out{d}"], t),
                                           g1_bc[:, 512 * d:512 * d + 512], ALU.mult))
                free()

            def x1_norm(t):
                dve.wait_ge(root_ready, 5 + t)
                rsqrt(stat[:, 0, 4 + t:5 + t], 1, stat[:, 2, 4 + t:5 + t], 1.0 / D, stat[:, 2, 12:13], root=stat[:, 1, 4 + t:5 + t])
                scaled_identity(t, t + 1, 4)

            dve.wait_ge(root_ready, 4)
            rsqrt(stat[:, 0, 0:TT], TT, stat[:, 2, 0:TT], 1.0 / D, stat[:, 2, 8:8 + TT])
            split_mlp(0, RING - 1)
            for t in range(TT):
                dve.wait_ge(x_again[t], 16)
                V.scalar_tensor_tensor(y1[:, t, :], y1[:, t, :], stat[:, 2, t:t + 1], x_in[t][:], ALU.mult,
                                       ALU.add).then_inc(x1_ready, 1)
                if t:
                    x1_norm(t - 1)
            mod_out(5)
            x1_norm(TT - 1)
            for k in range(KD):
                dve.wait_ge(h_hi_ready, KD + k + 1)
                h_low(1, k, psum[:, 4 * TURN_HALF + k % 4, :], h2_hi, h2_lo)
                dve.wait_ge(h_ready, KD + k + 1)
                dve.sem_inc(turned_used, 1)
                if k % KS == KS - 1 and k >= 3:
                    split_mlp(0, RING + (k - 3) // KS)

            n0, d0 = len(STAGES), freed("D", len(STAGES))

            c0 = ch.n

            def square_stage(i, u):
                for b in range(4):
                    k = 4 * u + b
                    dve.wait_ge(up_relu, i * HT + (k + 1))
                    if not isinstance(i, int) or k >= 2:
                        dve.wait_ge(u2_ready, i * HT + (k - 1))
                    V.tensor_tensor(u_sq[:, b % 2, :], u_relu[:, b % 2, :], u_relu[:, b % 2, :], ALU.mult).then_inc(up_used, 1)
                    dve.wait_ge(up_used, i * HT + (k + 1))
                    V.tensor_copy(u2_hi[:, k, :], u_sq[:, b % 2, :]).then_inc(dve_chain, 1)
                    dve.wait_ge(dve_chain, i * HT + (c0 + k + 1))
                    V.tensor_tensor(u2_lo[:, k, :], u_sq[:, b % 2, :], u2_hi[:, k, :].bitcast(F32), ALU.subtract).then_inc(u2_ready, 1)

            def add_stage(i, d):
                dve.wait_ge(slab_used, i * STEP_SLABS + (MLP0 + UPG * SG + DS * (d + 1)))
                for t in range(TT):
                    y = y2[:, t, 512 * d:512 * d + 512]
                    if isinstance(i, int) and i == 0:
                        if d == 0:
                            dve.wait_ge(turned, KD)
                            for stored in x1_stored:
                                dve.wait_ge(stored, 16)
                        last = V.tensor_copy(y, bank(n0 + UPG + d, t))
                    else:
                        last = V.tensor_tensor(y, y, bank(n0 + UPG + d, t), ALU.add)
                    if t == TT - 1:
                        last.then_inc(dve_freed, 1)

            def step(i, before, begin=0):
                for local in range(STEP_SLABS):
                    if local >= begin:
                        split_mlp(i, local)
                    if local == 2 and before is not None:
                        dve.wait_ge(y2_zero, 1)
                        add_stage(before, DNG - 1)
                    if local in (SG + 2, 2 * SG + 2):
                        square_stage(i, (local - 2) // SG - 1)
                    d, r = divmod(local - UPG * SG - DS - 2, DS)
                    if r == 0 and 0 <= d < DNG - 1:
                        add_stage(i, d)

            step(0, None, EARLY_SPLITS)
            with dve.Fori(1, STEPS) as i:
                step(i, i - 1)
            add_stage(STEPS - 1, DNG - 1)
            ch.n = c0 + HT * STEPS
            dve.wait_ge(root_ready, 9)
            rsqrt(stat[:, 0, 8:8 + TT], TT, stat[:, 2, 0:TT], 1.0 / D, stat[:, 2, 8:8 + TT])
            dve.wait_ge(g_landed, 32)
            dve.wait_ge(x1_back, 16)
            for t in range(TT):
                ch.link(V.scalar_tensor_tensor(y2[:, t, :], y2[:, t, :], stat[:, 2, t:t + 1], g2_bc[:], ALU.mult, ALU.mult))
                V.tensor_tensor(x1_in[:, t, :], x1_in[:, t, :], y2[:, t, :], ALU.add).then_inc(final_ready, 1)


INPUTS = ["x", "c", "positions", "rel_bias", "w_mod", "b_mod", "g_pre_mix", "g_post_mix", "g_pre_mlp", "g_post_mlp",
          "w_in", "pool_w", "pool_scale", "conv_w", "conv_b", "gate_r_w", "gate_r_b", "gate_i_w", "gate_i_b",
          "lru_lambda", "g_attn_out", "g_pool_out", "g_lru_out", "w_out", "w_mlp_up", "w_mlp_down"]


def kernel(**inputs):
    import concourse.bacc as bacc
    from concourse.bass_utils import run_bass_kernel_spmd

    nc = bacc.Bacc("TRN2", target_bir_lowering=False, num_devices=1)
    arrays, args = {}, []
    for name in INPUTS:
        a = np.ascontiguousarray(inputs[name])
        arrays[f"in_{name}"] = a
        args.append(nc.dram_tensor(f"in_{name}", a.shape, mybir.dt.from_np(a.dtype), kind="ExternalInput").ap())
    args.append(nc.dram_tensor("out_x", (1, T, D), F32, kind="ExternalOutput").ap())
    build(nc, *args)
    r = run_bass_kernel_spmd(nc, [arrays], core_ids=[0])
    return r.results[0]["out_x"]
```

```python
from contextlib import ExitStack

import numpy as np
import concourse.bass as bass
from concourse import mybir

F32 = mybir.dt.float32
F32R = mybir.dt.float32r
BF16 = mybir.dt.bfloat16
I32 = mybir.dt.int32
ALU = mybir.AluOpType
ACT = mybir.ActivationFunctionType
AXX = mybir.AxisListType.X

P = 128
D = 2048
T = 512
KD = D // P
TT = T // P
HEADS, HD = 8, 128
AW = HEADS * HD
IH, ID = 16, 64
GW = 512
CT = GW // P
TOPK = min(256, T // 4)
ROUNDS = TOPK // 8
HIDDEN = 4 * D
NBUCKET, MAXDIST = 32, 128
EPS = 1e-6
LRU_C = 8.0
NEG = -1e30
TAKEN = -3e38

C_Q, C_K, C_V, C_QI = 0, AW, 2 * AW, 3 * AW
C_KI = C_QI + IH * ID
C_WI = C_KI + ID
C_POOL = C_WI + IH
C_LRU = C_POOL + GW
C_GATE = C_LRU + GW

RING = 4
KS = 2
SG = KD // KS
G_KW, G_QI, G_LRU, G_GATE, G_POOL, G_K, G_Q, G_V = 0, 1, 3, 4, 5, 6, 8, 10
PROJ_GROUPS = 12
PROJ_SLABS = PROJ_GROUPS * SG
OUT_SLABS = TT * SG
MLP0 = PROJ_SLABS + OUT_SLABS
CHUNK = 1024
STEPS = HIDDEN // CHUNK
HT = CHUNK // P
UPG, DNG = CHUNK // 512, D // 512
DS = HT // KS
STEP_SLABS = UPG * SG + DNG * DS

SHIFT1, SCALE1, GATE1, SHIFT2, SCALE2, GATE2 = range(6)
MOD_ORDER = [SCALE1, SHIFT1, GATE1, SCALE2, SHIFT2, GATE2]
MOD_EARLY = 2 * KD
MOD_PROJ = 3 * KD
MOD_AGAIN = 3 * SG + 3


def mod_beside(s):
    if SG <= s < 3 * SG:
        return MOD_EARLY + s - SG
    if MOD_AGAIN <= s < MOD_AGAIN + 2 * KD - TT:
        return MOD_EARLY + KD + TT + s - MOD_AGAIN
    return None



STAGES = (
    [("c", "D"), ("pos", "D"), ("bias0", "A"), ("bias1", "A"), ("vec", "D")] + [(f"bias{n}", "A") for n in range(2, 8)] + [("mod0", "D")] + [(f"xt{t}", "AD") for t in range(TT)] + [("mod1", "D")]
    + [("g0", "AD"), ("g1", "AD"), ("widx", "D"), ("g2", "AD")]
    + [(f"dots{n}", "A") for n in range(TT * IH // 4)]
    + [("g3", "A"), ("mod2", "D"), ("g4", "A"), ("mod3", "D"), ("rgate", "A"), ("igate", "A"), ("g5", "A"), ("g6", "A"),
       ("mod4", "D"), ("g7", "A"), ("g8", "A"), ("g9", "A"), ("poolmm", "A"), ("g10", "AD"), ("ssq", "A"),
       ("g11", "AD")]
    + [("out0", "AD"), ("out1", "AD"), ("out2", "AD"), ("mod5", "D"), ("out3", "AD")]
)
STAGE = {name: n for n, (name, _) in enumerate(STAGES)}
TURN_HALF = (len(STAGES) + 1) % 2


GROUP_OF = {f"g{g}": g for g in range(PROJ_GROUPS)} | {f"out{d}": PROJ_GROUPS + d for d in range(TT)}

CONV_DONE, U_ARG, SCANNED, GELU_ARG, LRU_DONE, POOL_DIFF, SQ_SUMMED = range(1, 8)
BRANCH_SQ = 10
X_AT = (2, 3, 4, 5)
TOPK_AT = 56
PROB_SLOTS, BM_SLOTS = 4, 8
S_BANK, SQ_BANK = 4 * (STAGE["out0"] % 2), 4 * ((STAGE["out0"] + 1) % 2)
O_BANK = SQ_BANK + 1
PT_BANK = (S_BANK + 3, SQ_BANK + 3)
LAG_EXP, LAG_NORM, LAG_TURN, LAG_HI, LAG_LO, LAG_PV = 0, 1, 3, 2, 3, 5
TILE_ORDER = ((0,), (1,), (2,), (3,))
EARLY_SPLITS = RING + (KD - 4) // KS + 1
assert EARLY_SPLITS <= SG + 3


def freed(who, n):
    return sum(who in by for _, by in STAGES[:n])


def dots_of(n):
    pair, n = divmod(n, 2 * IH)
    return 2 * pair + n % 2, n // 2


def out_tile(n):
    return (n + HEADS) % KD


def pool_makes(k):
    return k % 4 == 3 or k % 8 == 1


def steps_by_pool(k):
    return sum(pool_makes(n) for n in range(k))


def bucket_starts():
    exact = NBUCKET // 2
    return [b if b < exact else int(np.ceil(exact * (MAXDIST / exact) ** ((b - exact) / (NBUCKET - exact)) - 1e-9))
            for b in range(NBUCKET)]


def build(nc, x, c, positions, rel_bias, w_mod, b_mod, g_pre_mix, g_post_mix, g_pre_mlp, g_post_mlp, w_in,
          pool_w, pool_scale, conv_w, conv_b, gate_r_w, gate_r_b, gate_i_w, gate_i_b, lru_lambda,
          g_attn_out, g_pool_out, g_lru_out, w_out, w_mlp_up, w_mlp_down, out):
    def rows(w):
        return w.rearrange("a (t p) n -> p (a t) n", p=P)

    def vec_rows(v):
        return v.rearrange("a (r p) -> (a r) p", p=P)

    x_d, out_d = rows(x), rows(out)
    w_mod_d, w_in_d, w_out_d = rows(w_mod), rows(w_in), rows(w_out)
    w_up_d, w_down_d = rows(w_mlp_up), rows(w_mlp_down)
    bias_s = nc.dram_tensor("bias_s", (T * HEADS, T), F32, kind="Internal").ap()
    gate_s = nc.dram_tensor("gate_s", (2, D), F32, kind="Internal").ap()
    x1_s = nc.dram_tensor("x1_s", (P, TT, D), F32, kind="Internal").ap()
    bias_h = bias_s.rearrange("(q t h) k -> h q t k", q=P, t=TT)

    b_rows = vec_rows(b_mod)
    vec_a_rows = [("g_pre1", vec_rows(g_pre_mix)), ("g_pre2", vec_rows(g_pre_mlp)),
                  ("b_mod0", b_rows[SCALE1 * KD:(SCALE1 + 1) * KD]), ("b_mod1", b_rows[SHIFT1 * KD:(SHIFT1 + 1) * KD]),
                  ("b_mod3", b_rows[SCALE2 * KD:(SCALE2 + 1) * KD]), ("b_mod4", b_rows[SHIFT2 * KD:(SHIFT2 + 1) * KD])]
    vec_b_rows = [("conv_w", conv_w.rearrange("a j (r p) -> (a j r) p", p=P)), ("conv_b", vec_rows(conv_b)),
                  ("r_b", vec_rows(gate_r_b)), ("i_b", vec_rows(gate_i_b)), ("lam", vec_rows(lru_lambda)),
                  ("pool_scale", vec_rows(pool_scale)), ("g_attn", vec_rows(g_attn_out)),
                  ("g_pool", vec_rows(g_pool_out)), ("g_lru", vec_rows(g_lru_out)),
                  ("b_mod2", b_rows[GATE1 * KD:(GATE1 + 1) * KD]), ("b_mod5", b_rows[GATE2 * KD:(GATE2 + 1) * KD]),
                  ("g_post1", vec_rows(g_post_mix)), ("g_post2", vec_rows(g_post_mlp))]
    at_a, at_b = {}, {}
    for at, table in ((at_a, vec_a_rows), (at_b, vec_b_rows)):
        n = 0
        for name, v in table:
            at[name] = n
            n += v.shape[0]
        assert n <= P
    n_small = len(vec_a_rows) + len(vec_b_rows)

    with ExitStack() as ctx:
        def sb(name, shape, dt):
            return ctx.enter_context(nc.sbuf_tensor(name, shape, dt))

        def sem(name):
            return ctx.enter_context(nc.semaphore(name))

        raw = sb("raw", [P, RING, KS, 512], F32)
        w_hi = sb("w_hi", [P, RING, KS, 512], F32R)
        w_lo = sb("w_lo", [P, RING, KS, 512], F32R)
        ident = sb("ident", [P, P], F32)
        ones = sb("ones", [P, P], F32)
        col_a = sb("col_a", [P, P], F32)
        col_b = sb("col_b", [P, P], F32)
        pos_k = sb("pos_k", [P, T], F32)
        pos_q = sb("pos_q", [P, TT], F32)
        start_col = sb("start_col", [P, 1], F32)
        rb = sb("rb", [P, HEADS], F32)
        rb_prev = sb("rb_prev", [P, HEADS], F32)
        rb_step = sb("rb_step", [P, HEADS], F32)
        c_col = sb("c_col", [P, KD], F32)
        c_act = sb("c_act", [P, KD], F32)
        c_tmp = sb("c_tmp", [P, KD], F32)
        mod = sb("mod", [P, 6, KD], F32)
        mul = sb("mul", [P, 2, KD], F32)
        w_idx = sb("w_idx", [P, TT, IH], F32)
        lam_t = sb("lam_t", [P, 8, CT], F32)
        half_b = sb("half_b", [P, 2, CT], F32)
        stat = sb("stat", [P, 8, 16], F32)
        eps_c = sb("eps_c", [P, 1], F32)
        inv_n = sb("inv_n", [P, 16], F32)
        pool_fix = sb("pool_fix", [P, CT, 16], F32)
        top8 = sb("top8", [P, 8], F32)
        nmax = sb("nmax", [P, PROB_SLOTS], F32)
        asum = sb("asum", [P, PROB_SLOTS], F32)
        arec = sb("arec", [P, PROB_SLOTS], F32)

        def at(kb, name, shape, dt):
            with ExitStack() as e:
                if kb:
                    e.enter_context(nc.sbuf_tensor(f"below_{name}", [P, int(kb * 256)], F32))
                return e.enter_context(nc.sbuf_tensor(name, shape, dt))

        bias_out = at(32, "bias_out", [P, 4, T], F32)
        steps = at(4, "steps", [P, 4, T], F32R)
        junk = at(20, "junk", [P, D], F32)
        vec_a = at(28, "vec_a", [P, P], F32)
        vec_b = at(28.5, "vec_b", [P, P], F32)
        c_row = at(31, "c_row", [P, P], F32)
        pos_qi = at(29, "pos_qi", [P, P], I32)
        pos_qf = at(29.5, "pos_qf", [P, P], F32)
        start_row = at(30, "start_row", [P, P], F32)
        reach = at(30.5, "reach", [P, P], F32)
        x_tok = at(84, "x_tok", [P, TT, D], F32)
        blk = at(116, "blk", [P, 4, P], F32)
        blk_hi = at(118, "blk_hi", [P, 4, P], F32R)
        blk_lo = at(120, "blk_lo", [P, 4, P], F32R)
        diag = at(150, "diag", [P, TT, P], F32)
        pos_ki = at(148, "pos_ki", [P, T], I32)
        acc_a = at(124, "acc_a", [P, D], F32)
        acc_b = at(12, "acc_b", [P, D], F32)
        mod_slabs = [at(kb, f"mod_slab{i}", [P, D], F32) for i, kb in enumerate((132, 140, 40))]
        h_full = at(0, "h_full", [P, 2, T], F32)
        h_hi = at(20, "h_hi", [P, KD, T], F32R)
        h_lo = at(52, "h_lo", [P, KD, T], F32R)
        x_t = at(52, "x_t", [P, KD, T], F32)
        score = at(4, "score", [P, TT, T], F32)
        qi_hi = at(84, "qi_hi", [P, IH // 2, T], F32R)
        qi_lo = at(100, "qi_lo", [P, IH // 2, T], F32R)
        ki_hi = [at(116, "ki_hi0", [P, T], F32R), at(0, "ki_hi1", [P, T], F32R)]
        ki_lo = [at(118, "ki_lo0", [P, T], F32R), at(2, "ki_lo1", [P, T], F32R)]
        relu = at(120, "relu", [P, 2, T], F32)
        widx_t = at(148, "widx_t", [P, T], F32)
        late = at(150, "late", [P, T], F32)
        gates_w = at(0, "gates_w", [P, 2, CT, P], F32)
        gate_in = at(84, "gate_in", [P, CT, T], F32)
        xc = at(92, "xc", [P, CT, T], F32)
        lru_in = at(100, "lru_in", [P, CT, T], F32)
        r_t = at(108, "r_t", [P, CT, T], F32)
        i_t = at(116, "i_t", [P, CT, T], F32)
        PAD = 8
        pool_u = at(84, "pool_u", [P, CT, PAD + T], F32)
        pool_b = at(93, "pool_b", [P, CT, PAD + T], F32)
        pool_c = at(102, "pool_c", [P, CT, PAD + T], F32)
        pool_ws = at(148, "pool_ws", [P, CT, P], F32)
        pool_sq = at(92, "pool_sq", [P, CT, T], F32)
        lru_sq = at(84, "lru_sq", [P, CT, T], F32)
        rnorm = at(148, "rnorm", [P, 2, T], F32)
        mask = at(0, "mask", [P, TT, T], BF16)
        pool_o = at(4, "pool_o", [P, CT, T], F32)
        lru_o = at(12, "lru_o", [P, CT, T], F32)
        v_hi = at(84, "v_hi", [P, TT, AW], F32R)
        v_lo = at(100, "v_lo", [P, TT, AW], F32R)
        q_t = at(116, "q_t", [P, HEADS, T], F32)
        k_t = at(132, "k_t", [P, HEADS, T], F32)
        attn = at(20, "attn", [P, HEADS, T], F32)
        bm = at(36, "bm", [P, BM_SLOTS, T], F32)
        q_hi = at(52, "q_hi", [P, 2, T], F32R)
        k_hi = at(56, "k_hi", [P, 2, T], F32R)
        q_lo = at(116, "q_lo", [P, HEADS, T], F32R)
        k_lo = at(132, "k_lo", [P, HEADS, T], F32R)
        probs = at(60, "probs", [P, PROB_SLOTS, T], F32)
        pt_hi = at(68, "pt_hi", [P, 2, TT, 2 * P], F32R)
        pt_lo = at(76, "pt_lo", [P, 2, TT, 2 * P], F32R)
        attn_sq = at(150, "attn_sq", [P, T], F32)
        m_hi = at(84, "m_hi", [P, KD, T], F32R)
        m_lo = at(116, "m_lo", [P, KD, T], F32R)
        mixed = at(20, "mixed", [P, HEADS, T], F32)
        x_in = [at(kb, f"x_in{t}", [P, D], F32) for t, kb in enumerate((20, 28, 4, 12))]
        y1 = at(36, "y1", [P, TT, D], F32)
        g1_bc = at(68, "g1_bc", [P, D], F32)
        slab_0 = at(4, "slab_0", [P, D], F32)
        slab_1 = at(76, "slab_1", [P, D], F32)

        def mod_slot(g):
            if g < MOD_EARLY:
                return mod_slabs[g % 3][:], g % 3, g // 3
            before = [len(range(i, MOD_EARLY, 3)) for i in range(2)]
            n = g - MOD_EARLY
            mem = (slab_0, slab_1) if g >= 5 * KD else mod_slabs
            return mem[n % 2][:], n % 2, before[n % 2] + n // 2
        sq_out = at(148, "sq_out", [P, T], F32)
        h2_hi = at(84, "h2_hi", [P, KD, T], F32R)
        h2_lo = at(116, "h2_lo", [P, KD, T], F32R)
        y2 = at(20, "y2", [P, TT, D], F32)
        u2_hi = at(52, "u2_hi", [P, HT, T], F32R)
        u2_lo = at(68, "u2_lo", [P, HT, T], F32R)
        u_relu = at(0, "u_relu", [P, 2, T], F32)
        u_sq = at(4, "u_sq", [P, 2, T], F32)
        g2_bc = at(12, "g2_bc", [P, D], F32)
        x1_in = at(84, "x1_in", [P, TT, D], F32)
        junk2 = at(116, "junk2", [P, D], F32)

        psum = ctx.enter_context(nc.psum_tensor("psum", [P, 8, 512], F32))

        def bank(stage, b):
            return psum[:, 4 * (stage % 2) + b, :]

        raw_landed = [sem(f"raw_landed{i}") for i in range(RING)]
        hi_ready, lo_pool, lo_dve, slab_used = sem("hi_ready"), sem("lo_pool"), sem("lo_dve"), sem("slab_used")
        stage_done, act_freed, dve_freed = sem("stage_done"), sem("act_freed"), sem("dve_freed")
        dve_chain, act_chain, pool_chain = sem("dve_chain"), sem("act_chain"), sem("pool_chain")
        c_in, ident_ready, small_in, pos_in, x_landed = sem("c_in"), sem("ident_ready"), sem("small_in"), sem("pos_in"), [sem(f"x_landed{t}") for t in range(TT)]
        mod_landed, mod_step = [sem(f"mod_landed{i}") for i in range(3)], sem("mod_step")
        start_ready = sem("start_ready")
        consts, rb_in, blk_ready, reach_ready = sem("consts"), sem("rb_in"), sem("blk_ready"), sem("reach_ready")
        step_dve, step_pool, step_used = sem("step_dve"), sem("step_pool"), sem("step_used")
        bias_stored = [sem(f"bias_stored{i}") for i in range(4)]
        vec_ready, c_tanh, c_copied, diag_ready = sem("vec_ready"), sem("c_tanh"), sem("c_copied"), sem("diag_ready")
        ssq_ready, root_ready, rinv_ready = sem("ssq_ready"), sem("root_ready"), sem("rinv_ready")
        mul_ready, h_hi_ready, h_ready = sem("mul_ready"), sem("h_hi_ready"), sem("h_ready")
        turned, turned_used = sem("turned"), sem("turned_used")
        act_hi = sem("act_hi")
        idx_ready, widx_copied = sem("idx_ready"), sem("widx_copied")
        relu_ready, relu_used, score_done = sem("relu_ready"), sem("relu_used"), sem("score_done")
        gates_in, pool_in = sem("gates_in"), sem("pool_in")
        branch_act, branch_dve = sem("branch_act"), sem("branch_dve")
        out_squared, tile_done = sem("out_squared"), sem("tile_done")
        mask_done, gate_col, gate_stored, g_landed = sem("mask_done"), sem("gate_col"), sem("gate_stored"), sem("g_landed")
        bias_landed = [sem(f"bias_landed{i}") for i in range(BM_SLOTS)]
        bm_ready = sem("bm_ready")
        qk_hi, q_lo_ready, k_lo_ready = sem("qk_hi"), sem("q_lo_ready"), sem("k_lo_ready")
        s_done, max_ready, exp_ready, probs_ready, pt_done, pt_hi_ready, pt_lo_ready = (
            sem("s_done"), sem("max_ready"), sem("exp_ready"), sem("probs_ready"), sem("pt_done"),
            sem("pt_hi_ready"), sem("pt_lo_ready"))
        pv_done, o_ready, sq_ready, sq_used = sem("pv_done"), sem("o_ready"), sem("sq_ready"), sem("sq_used")
        mixed_full, mixed_hi, mixed_ready = sem("mixed_full"), sem("mixed_hi"), sem("mixed_ready")
        x_again, x1_ready, x1_stored = [sem(f"x_again{t}") for t in range(TT)], sem("x1_ready"), [sem(f"x1_stored{t}") for t in range(TT)]
        y2_zero, y2_done, y2_squared = sem("y2_zero"), sem("y2_done"), sem("y2_squared")
        up_relu, up_used, u2_ready = sem("up_relu"), sem("up_used"), sem("u2_ready")
        x1_back, final_ready, out_stored = sem("x1_back"), sem("final_ready"), sem("out_stored")

        class Chain:

            def __init__(self, eng, counter):
                self.eng, self.counter, self.n = eng, counter, 0

            def put(self, instruction):
                instruction.then_inc(self.counter, 1)
                self.n += 1
                return self.n

            def wait(self, n=None):
                self.eng.wait_ge(self.counter, self.n if n is None else n)

            def link(self, instruction):
                self.put(instruction)
                self.wait()

        def slab_source(s):
            g, j = divmod(s, SG)
            k = slice(KS * j, KS * j + KS)
            if g == G_KW:
                return w_in_d[:, k, C_KI:C_KI + 192], 192
            if g < PROJ_GROUPS:
                col = {G_QI: C_QI, G_QI + 1: C_QI + 512, G_LRU: C_LRU, G_GATE: C_GATE, G_POOL: C_POOL, G_K: C_K,
                       G_K + 1: C_K + 512, G_Q: C_Q, G_Q + 1: C_Q + 512, G_V: C_V, G_V + 1: C_V + 512}[g]
                return w_in_d[:, k, col:col + 512], 512
            col = 512 * (g - PROJ_GROUPS)
            k = slice(out_tile(KS * j), out_tile(KS * j) + KS)
            return w_out_d[:, k, col:col + 512], 512

        def wait_lo(eng, s):
            if s < PROJ_SLABS:
                eng.wait_ge(lo_pool, s + 1)
            else:
                eng.wait_ge(lo_dve, s - PROJ_SLABS + 1)

        def wait_stage(eng, name):
            if name in GROUP_OF:
                eng.wait_ge(slab_used, SG * (GROUP_OF[name] + 1))
            elif name.startswith("bias"):
                eng.wait_ge(step_used, 16 * (int(name[4:]) + 1))
            else:
                counted = [k for k, _ in STAGES if k not in GROUP_OF and not k.startswith("bias")]
                eng.wait_ge(stage_done, counted.index(name) + 1)

        def tile_finished(eng, t):
            if t < TT - 1:
                eng.wait_ge(tile_done, t + 1)
            else:
                wait_stage(eng, "out3")

        def store_gate(eng, k):
            with nc.allow_non_contiguous_dma(reason="2048 elements"):
                eng.dma_start(gate_s[k:k + 1, :].rearrange("a (r p) -> p (a r)", p=P),
                              mod[:, (2, 5)[k], :]).then_inc(gate_stored, 16)

        block = ctx.enter_context(nc.Block())

        @block.sync
        def _(sp):
            def load_slab(s):
                if s >= RING:
                    wait_lo(sp, s - RING)
                src, n = slab_source(s)
                sp.dma_start(raw[:, s % RING, :, 0:n], src).then_inc(raw_landed[s % RING], 16)

            def load_mod(g):
                j, k = divmod(g, KD)
                dst, slot, _ = mod_slot(g)
                last = max([n for n in range(g) if mod_slot(n)[1] == slot], default=-1)
                if last >= 0:
                    sp.wait_ge(mod_step, last + 1)
                m = MOD_ORDER[j]
                sp.dma_start(dst, w_mod_d[:, k, D * m:D * (m + 1)]).then_inc(mod_landed[slot], 16)

            sp.dma_start(c_row[0:KD, :], vec_rows(c)).then_inc(c_in, 16)
            for g in range(MOD_EARLY):
                load_mod(g)
                if g == 3:
                    for v, table in ((vec_a, vec_a_rows), (vec_b, vec_b_rows)):
                        n = 0
                        for _, src in table:
                            sp.dma_start(v[n:n + src.shape[0], :], src).then_inc(small_in, 16)
                            n += src.shape[0]
                if g in X_AT:
                    t = X_AT.index(g)
                    sp.dma_start(x_tok[:, t, :], x_d[:, t, :]).then_inc(x_landed[t], 16)
                if g == MOD_EARLY - 3:
                    load_slab(0)
                    load_slab(1)
            for s in range(PROJ_SLABS):
                if mod_beside(s) is not None:
                    load_mod(mod_beside(s))
                load_slab(s + 2)
                if s == MOD_AGAIN - 3:
                    for t in range(TT):
                        load_mod(MOD_EARLY + KD + t)
                if s == MOD_AGAIN + 1:
                    sp.wait_ge(score_done, 1)
                    for k, w in enumerate((gate_r_w, gate_i_w)):
                        sp.dma_start(gates_w[:, k, :, :], w.rearrange("a g c d -> c (a g) d")).then_inc(gates_in, 16)
                if s == 44:
                    sp.wait_ge(gate_col, 1)
                    store_gate(sp, 0)
                if s == 50:
                    sp.dma_start(pool_ws[:], pool_w.rearrange("a g c d -> c (a g) d")).then_inc(pool_in, 16)

            load_slab(PROJ_SLABS + 2)
            load_slab(PROJ_SLABS + 3)
            wait_stage(sp, "g11")
            for it in range(HEADS * TT):
                if it >= BM_SLOTS:
                    sp.wait_ge(max_ready, it - BM_SLOTS + 1)
                sp.dma_start(bm[:, it % BM_SLOTS, :], bias_h[it // TT][:, it % TT, :]).then_inc(bias_landed[it % BM_SLOTS], 16)

            for s in range(PROJ_SLABS, MLP0):
                k = s - PROJ_SLABS
                if s + RING < MLP0:
                    load_slab(s + RING)
                if k == 0:
                    sp.wait_ge(gate_stored, 16)
                    sp.wait_ge(pt_lo_ready, HEADS * TT)
                    sp.wait_ge(pv_done, HEADS * TT // 2)
                    sp.dma_start(g1_bc[:], gate_s[0:1, :].to_broadcast([P, D])).then_inc(g_landed, 16)
                if k == SG:
                    sp.wait_ge(mixed_ready, KD)
                if SG <= k < SG + KD:
                    load_mod(5 * KD + k - SG)
                if k in (2 * SG, 2 * SG + 4):
                    t = (k - 2 * SG) // 4
                    sp.dma_start(x_in[t][:], x_d[:, t, :]).then_inc(x_again[t], 16)
                if k == SG + KD + 1:
                    sp.wait_ge(mod_step, 6 * KD)
                    sp.dma_start(x_in[2][:], x_d[:, 2, :]).then_inc(x_again[2], 16)

            def load_mlp(s, i, local):
                wait_count = MLP0 - PROJ_SLABS - RING + 1 + local
                sp.wait_ge(lo_dve, i * STEP_SLABS + wait_count)
                if local < UPG * SG:
                    g, j = divmod(local, SG)
                    src = w_up_d[:, KS * j:KS * j + KS, bass.ds(i * CHUNK + 512 * g, 512)]
                else:
                    g, j = divmod(local - UPG * SG, DS)
                    src = w_down_d[:, bass.ds(i * HT + KS * j, KS), 512 * g:512 * g + 512]
                sp.dma_start(raw[:, s % RING, :, :], src).then_inc(raw_landed[s % RING], 16)

            wait_stage(sp, "mod5")
            sp.dma_start(x_in[3][:], x_d[:, 3, :]).then_inc(x_again[3], 16)
            for local in range(STEP_SLABS):
                load_mlp(MLP0 + local, 0, local)
                if local == RING - 1:
                    for t in range(TT):
                        sp.wait_ge(x1_ready, t + 1)
                        sp.dma_start(x1_s[:, t, :], y1[:, t, :]).then_inc(x1_stored[t], 16)
                    sp.wait_ge(gate_col, 2)
                    store_gate(sp, 1)
            with sp.Fori(1, STEPS) as i:
                for local in range(STEP_SLABS):
                    load_mlp(MLP0 + local, i, local)
            sp.wait_ge(gate_stored, 32)
            sp.dma_start(g2_bc[:], gate_s[1:2, :].to_broadcast([P, D])).then_inc(g_landed, 16)
            for t in range(TT):
                sp.wait_ge(x1_stored[t], 16)
            sp.wait_ge(slab_used, MLP0 + STEP_SLABS * (STEPS - 1) + UPG * SG)
            sp.dma_start(x1_in[:], x1_s).then_inc(x1_back, 16)
            for k in range(2 * TT):
                t, half = k // 2, slice(D // 2 * (k % 2), D // 2 * (k % 2) + D // 2)
                sp.wait_ge(final_ready, k + 1)
                sp.dma_start(out_d[:, t, half], x1_in[:, t, half]).then_inc(out_stored, 16)
            sp.wait_ge(out_stored, 16 * 2 * TT)
            for stored in bias_stored:
                sp.wait_ge(stored, 16 * 8)

        @block.gpsimd
        def _(pool):
            ch = Chain(pool, pool_chain)
            ch.put(nc.gpsimd.memset(ones[:], 1.0))
            ch.link(nc.gpsimd.memset(ident[:], 0.0))
            nc.gpsimd.affine_select(out=ident[:], in_=ident[:], compare_op=ALU.not_equal, fill=1.0, base=0,
                                    pattern=[[-1, P]], channel_multiplier=1).then_inc(ident_ready, 1)
            nc.gpsimd.memset(rb_prev[:], 0.0).then_inc(consts, 1)
            row = start_row[0:1, :].rearrange("a (q b) -> a b q", q=4)
            for b, start in enumerate(bucket_starts()):
                ch.put(nc.gpsimd.memset(row[:, b, :], float(start)))
            ch.wait()
            pool.sem_inc(start_ready, 1)
            ch.put(nc.gpsimd.memset(blk[:], 0.0))
            for n in range(16):
                ch.put(nc.gpsimd.memset(inv_n[:, n:n + 1], 1.0 / (n + 1)))
            ch.put(nc.gpsimd.memset(eps_c[:], EPS))
            ch.wait()
            pool.wait_ge(rb_in, 16 * 8)
            ch.link(nc.gpsimd.tensor_tensor(rb_step[:], rb[:], rb_prev[:], ALU.subtract))
            for q in range(4):
                for j in range(4):
                    o = 32 * j + 8 * q
                    ch.put(nc.gpsimd.tensor_copy(blk[32 * q:32 * q + 32, j, o:o + 8], rb_step[32 * q:32 * q + 32, :]))
            ch.wait()
            ch.link(nc.gpsimd.tensor_copy(blk_hi[:], blk[:]))
            nc.gpsimd.tensor_tensor(blk_lo[:], blk[:], blk_hi[:].bitcast(F32), ALU.subtract).then_inc(blk_ready, 1)
            pool.wait_ge(blk_ready, 1)
            nc.gpsimd.memset(stat[:], 0.0).then_inc(consts, 1)
            pool.wait_ge(reach_ready, 1)
            for n in range(P):
                if not pool_makes(n):
                    continue
                if n >= 4:
                    pool.wait_ge(step_used, n - 3)
                nc.gpsimd.tensor_scalar(steps[:, n % 4, :], pos_k[:], reach[:, n:n + 1], None,
                                        ALU.is_le).then_inc(step_pool, 1)
            for s in range(PROJ_SLABS):
                pool.wait_ge(hi_ready, s + 1)
                r, hi, lo = raw[:, s % RING, :, :], w_hi[:, s % RING, :, :], w_lo[:, s % RING, :, :]
                if s < SG:
                    ch.put(nc.gpsimd.tensor_tensor(lo[:, :, 0:64], r[:, :, 0:64], hi[:, :, 0:64].bitcast(F32), ALU.subtract))
                    ch.wait()
                    r, hi, lo = r[:, :, 0:192], hi[:, :, 64:256], lo[:, :, 64:256]
                nc.gpsimd.tensor_tensor(lo, r, hi.bitcast(F32), ALU.subtract).then_inc(lo_pool, 1)
            pool.wait_ge(mask_done, TT)

            def k_low(hd):
                pool.wait_ge(qk_hi, 2 * hd + 2)
                nc.gpsimd.tensor_tensor(k_lo[:, hd, :], k_t[:, hd, :], k_hi[:, hd % 2, :].bitcast(F32),
                                        ALU.subtract).then_inc(k_lo_ready, 1)

            def squares_of(hd):
                pool.wait_ge(o_ready, hd + 1)
                if hd >= 1:
                    pool.wait_ge(sq_used, hd)
                nc.gpsimd.tensor_tensor(attn_sq[:], attn[:, hd, :], attn[:, hd, :], ALU.mult).then_inc(sq_ready, 1)

            k_low(0)
            for it in range(HEADS * TT):
                b = bm[:, it % BM_SLOTS, :]
                pool.wait_ge(bias_landed[it % BM_SLOTS], 16 * (it // BM_SLOTS + 1))
                nc.gpsimd.tensor_tensor(b, b, mask[:, it % TT, :], ALU.add).then_inc(bm_ready, 1)
                hd = it // TT
                if it == 1:
                    k_low(1)
                if it % TT == TT - 1 and 2 <= hd + 1 < HEADS:
                    k_low(hd + 1)
                if it % TT == 1 and hd >= 3:
                    squares_of(hd - 3)
            for hd in range(HEADS - 3, HEADS):
                squares_of(hd)
            pool.wait_ge(turned, KD)
            for stored in x1_stored:
                pool.wait_ge(stored, 16)
            nc.gpsimd.memset(y2[:, :, D - 512:D], 0.0).then_inc(y2_zero, 1)

        @block.tensor
        def _(pe):
            def begin(n):
                if n >= 2:
                    if freed("A", n - 1):
                        pe.wait_ge(act_freed, freed("A", n - 1))
                    if freed("D", n - 1):
                        pe.wait_ge(dve_freed, freed("D", n - 1))

            def three(o, a_hi, a_lo, b_hi, b_lo, first, last):
                nc.tensor.matmul(o, a_hi, b_hi, start=first, stop=False)
                nc.tensor.matmul(o, a_hi, b_lo, start=False, stop=False)
                return nc.tensor.matmul(o, a_lo, b_hi, start=False, stop=last)

            def weights(slot, j, cols):
                return w_hi[:, slot, j, cols], w_lo[:, slot, j, cols]

            def features_out(stage, slot, j, act, kt, first, last_, tiles=4):
                for b in range(tiles):
                    last = three(bank(stage, b), *weights(slot, j, slice(P * b, P * b + P)),
                                 act[0][:, kt, :], act[1][:, kt, :], first, last_)
                return last

            def tokens_out(stage, slot, j, act, kt, first, last_, tiles=range(TT)):
                for b in tiles:
                    tok = slice(P * b, P * b + P)
                    last = three(bank(stage, b), act[0][:, kt, tok], act[1][:, kt, tok],
                                 *weights(slot, j, slice(0, 512)), first, last_)
                return last

            def group(g, stage, emit, act, ready=None, tile=lambda n: n, **how):
                begin(stage)
                for j in range(SG):
                    s = g * SG + j
                    wait_lo(pe, s)
                    for k in range(KS):
                        if ready is not None:
                            pe.wait_ge(ready, KS * j + k + 1)
                        n = KS * j + k
                        last = emit(stage, s % RING, k, act, tile(n), n == 0, n == KD - 1, **how)
                    last.then_inc(slab_used, 1)

            def mod_sum(j):
                n = STAGE[f"mod{j}"]
                begin(n)
                pe.wait_ge(mod_step, KD * (j + 1))
                acc = acc_b if j % 2 else acc_a
                for k in range(KD):
                    last = nc.tensor.matmul(bank(n, 0)[:, k:k + 1], acc[:, P * k:P * k + P], ones[:, 0:1],
                                            start=True, stop=True)
                last.then_inc(stage_done, 1)

            def transposed(o, src, kt):
                for t in range(TT):
                    last = nc.tensor.matmul(o[:, P * t:P * t + P], src[:, t, P * kt:P * kt + P], diag[:, t, :],
                                            start=True, stop=True)
                return last

            pe.wait_ge(c_in, 16)
            pe.wait_ge(ident_ready, 1)
            nc.tensor.transpose(bank(STAGE["c"], 0)[:, 0:KD], c_row[0:KD, :], ident[0:KD, 0:KD]).then_inc(stage_done, 1)
            pe.wait_ge(start_ready, 1)
            pe.wait_ge(vec_ready, 1)
            n = STAGE["pos"]
            nc.tensor.transpose(bank(n, 0)[:, 0:TT], pos_qf[0:TT, :], ident[0:TT, 0:TT])
            nc.tensor.matmul(bank(n, 1)[:, 0:1], start_row[0:1, :], ones[0:1, 0:1], start=True,
                             stop=True).then_inc(stage_done, 1)
            pe.wait_ge(blk_ready, 1)

            def small_vectors():
                n = STAGE["vec"]
                begin(n)
                pe.wait_ge(small_in, 16 * n_small)
                na, nb = sum(v.shape[0] for _, v in vec_a_rows), sum(v.shape[0] for _, v in vec_b_rows)
                nc.tensor.transpose(bank(n, 0)[:, 0:na], vec_a[0:na, :], ident[0:na, 0:na])
                nc.tensor.transpose(bank(n, 1)[:, 0:nb], vec_b[0:nb, :], ident[0:nb, 0:nb]).then_inc(stage_done, 1)

            for m in range(8):
                if m == 2:
                    small_vectors()
                n = STAGE[f"bias{m}"]
                begin(n)
                for b in range(4):
                    for j in range(4):
                        k = 16 * m + 4 * b + j
                        if pool_makes(k):
                            pe.wait_ge(step_pool, steps_by_pool(k) + 1)
                        else:
                            pe.wait_ge(step_dve, k - steps_by_pool(k) + 1)
                        nc.tensor.matmul(bank(n, b), blk_hi[:, j, :], steps[:, k % 4, :], start=j == 0, stop=False)
                        last = nc.tensor.matmul(bank(n, b), blk_lo[:, j, :], steps[:, k % 4, :], start=False, stop=j == 3)
                        last.then_inc(step_used, 1)

            mod_sum(0)
            pe.wait_ge(diag_ready, TT)
            for n in range(TT):
                begin(STAGE[f"xt{n}"])
                for b in range(4):
                    last = transposed(bank(STAGE[f"xt{n}"], b), x_tok, 4 * n + b)
                last.then_inc(stage_done, 1)
            mod_sum(1)

            h = (h_hi, h_lo)
            group(G_KW, STAGE["g0"], features_out, h, ready=h_ready, tiles=2)
            group(G_QI, STAGE["g1"], features_out, h)
            n = STAGE["widx"]
            begin(n)
            pe.wait_ge(widx_copied, 1)
            for t in range(TT):
                last = nc.tensor.transpose(bank(n, 0)[:, IH * t:IH * t + IH], widx_t[0:IH, P * t:P * t + P],
                                           ident[0:IH, 0:IH])
            last.then_inc(stage_done, 1)
            group(G_QI + 1, STAGE["g2"], features_out, h)
            for m in range(TT * IH // 4):
                if m == 0:
                    pe.wait_ge(idx_ready, 1 + IH // 4)
                elif dots_of(4 * m)[1] == IH // 2:
                    pe.wait_ge(idx_ready, 1 + IH // 2)
                n = STAGE[f"dots{m}"]
                begin(n)
                for b in range(4):
                    t, hd = dots_of(4 * m + b)
                    tok = slice(P * t, P * t + P)
                    last = three(bank(n, b), qi_hi[:, hd // 2, tok], qi_lo[:, hd // 2, tok], ki_hi[hd % 2][:],
                                 ki_lo[hd % 2][:], True, True)
                last.then_inc(stage_done, 1)
            group(G_LRU, STAGE["g3"], features_out, h)
            mod_sum(2)
            group(G_GATE, STAGE["g4"], features_out, h)
            mod_sum(3)
            pe.wait_ge(gates_in, 32)
            pe.wait_ge(branch_dve, CONV_DONE)
            for k, name in enumerate(("rgate", "igate")):
                n = STAGE[name]
                begin(n)
                for b in range(CT):
                    last = nc.tensor.matmul(bank(n, b), gates_w[:, k, b, :], xc[:, b, :], start=True, stop=True)
                last.then_inc(stage_done, 1)
            group(G_POOL, STAGE["g5"], features_out, h)
            group(G_K, STAGE["g6"], features_out, h)
            mod_sum(4)
            group(G_K + 1, STAGE["g7"], features_out, h)
            group(G_Q, STAGE["g8"], features_out, h)
            group(G_Q + 1, STAGE["g9"], features_out, h)
            n = STAGE["poolmm"]
            begin(n)
            pe.wait_ge(pool_in, 16)
            pe.wait_ge(branch_dve, POOL_DIFF)
            for b in range(CT):
                last = nc.tensor.matmul(bank(n, b), pool_ws[:, b, :], (pool_b, pool_c)[b % 2][:, b, PAD:], start=True,
                                        stop=True)
            last.then_inc(stage_done, 1)
            group(G_V, STAGE["g10"], tokens_out, h)
            n = STAGE["ssq"]
            begin(n)
            pe.wait_ge(branch_dve, SQ_SUMMED)
            for b, sq in enumerate((pool_sq, lru_sq)):
                last = nc.tensor.matmul(bank(n, b), ones[:], sq[:, 0, :], start=True, stop=True)
            last.then_inc(stage_done, 1)
            group(G_V + 1, STAGE["g11"], tokens_out, h)

            pe.wait_ge(act_freed, freed("A", STAGE["ssq"] + 1))

            def scores_of(it):
                hd, t = divmod(it, TT)
                if t == 0:
                    pe.wait_ge(q_lo_ready, hd + 1)
                    pe.wait_ge(k_lo_ready, hd + 1)
                if it >= 3:
                    pe.wait_ge(max_ready, it - 2)
                tok = slice(P * t, P * t + P)
                three(psum[:, S_BANK + it % 3, :], q_hi[:, hd % 2, tok], q_lo[:, hd, tok], k_hi[:, hd % 2, :],
                      k_lo[:, hd, :], True, True).then_inc(s_done, 1)

            def transpose_of(it):
                if it == 0:
                    pe.wait_ge(act_freed, freed("A", STAGE["g11"] + 1))
                    pe.wait_ge(dve_freed, freed("D", STAGE["g11"] + 1))
                pe.wait_ge(probs_ready, it + 1)
                if it >= 2:
                    pe.wait_ge(pt_lo_ready, it - 1)
                for k in range(TT):
                    last = nc.tensor.transpose(psum[:, PT_BANK[it % 2], P * k:P * k + P],
                                               probs[:, it % PROB_SLOTS, P * k:P * k + P], ident[:])
                last.then_inc(pt_done, 1)

            def values_of(pair):
                hd, half = divmod(pair, TT // 2)
                if half == 0 and hd >= 2:
                    pe.wait_ge(o_ready, hd - 1)
                pe.wait_ge(pt_lo_ready, 2 * pair + 2)
                cols = slice(HD * hd, HD * hd + HD)
                o = psum[:, O_BANK + hd % 2, 2 * P * half:2 * P * half + 2 * P]
                for k in range(TT):
                    last = three(o, v_hi[:, k, cols], v_lo[:, k, cols], pt_hi[:, pair % 2, k, :], pt_lo[:, pair % 2, k, :],
                                 k == 0, k == TT - 1)
                last.then_inc(pv_done, 1)

            def square_sum(hd):
                pe.wait_ge(sq_ready, hd + 1)
                nc.tensor.matmul(psum[:, SQ_BANK, :], ones[:], attn_sq[:], start=hd == 0, stop=hd == HEADS - 1).then_inc(sq_used, 1)

            n_it = HEADS * TT
            for it in range(n_it + LAG_PV):
                if it < n_it:
                    scores_of(it)
                if 0 <= it - LAG_TURN < n_it:
                    transpose_of(it - LAG_TURN)
                v = it - LAG_PV
                if v >= 0 and v % 2:
                    values_of(v // 2)
                    if v % TT == 1 and v // TT >= 2:
                        square_sum(v // TT - 2)
            square_sum(HEADS - 2)
            square_sum(HEADS - 1)

            pe.wait_ge(o_ready, HEADS)
            pe.wait_ge(pt_lo_ready, HEADS * TT)
            for d in range(TT):
                if d < TT - 1:
                    group(PROJ_GROUPS + d, STAGE[f"out{d}"], tokens_out, (m_hi, m_lo),
                          ready=mixed_ready if d == 0 else None, tile=out_tile)
                    continue
                mod_sum(5)
                n = STAGE[f"out{d}"]
                begin(n)
                half = SG // 2
                for tiles, slabs in [(range(TT), range(half))] + [(tiles, range(half, SG)) for tiles in TILE_ORDER]:
                    for j in slabs:
                        s = (PROJ_GROUPS + d) * SG + j
                        wait_lo(pe, s)
                        for k in range(KS * j, KS * j + KS):
                            last = tokens_out(n, s % RING, k % KS, (m_hi, m_lo), out_tile(k), k == 0, k == KD - 1, tiles)
                        if j == SG - 1 and tiles is not TILE_ORDER[-1]:
                            last.then_inc(tile_done, len(tiles))
                        elif j < half or tiles is TILE_ORDER[-1]:
                            last.then_inc(slab_used, 1)

            n0, a0, d0 = len(STAGES), freed("A", len(STAGES)), freed("D", len(STAGES))
            pe.wait_ge(act_freed, a0)
            pe.wait_ge(dve_freed, d0)

            def turn_x1(kt):
                if kt >= 4:
                    pe.wait_ge(turned_used, kt - 3)
                transposed(psum[:, 4 * TURN_HALF + kt % 4, :], y1, kt).then_inc(turned, 1)

            def mlp_step(i, first_step, stages=UPG + DNG):
                for u in range(stages):
                    if not first_step or u >= UPG:
                        if u < UPG:
                            pe.wait_ge(dve_freed, i * DNG + (d0 - UPG + 1 + u))
                        elif u < 2 * UPG:
                            pe.wait_ge(act_freed, i * UPG + (a0 + 1 + u - UPG))
                        else:
                            pe.wait_ge(dve_freed, i * DNG + (d0 + u - 2 * UPG + 1))
                    elif u == 0:
                        pe.wait_ge(diag_ready, 2 * TT)
                        for kt in range(4):
                            turn_x1(kt)
                    else:
                        pe.wait_ge(turned_used, KD)
                    slabs, nk = (SG, KD) if u < UPG else (DS, HT)
                    first = SG * u if u < UPG else UPG * SG + DS * (u - UPG)
                    for j in range(slabs):
                        local = first + j
                        pe.wait_ge(lo_dve, i * STEP_SLABS + (MLP0 - PROJ_SLABS + local + 1))
                        for k in range(KS):
                            kt = KS * j + k
                            if u < UPG:
                                if first_step and u == 0:
                                    pe.wait_ge(h_ready, KD + kt + 1)
                                last = features_out(n0 + u, local % RING, k, (h2_hi, h2_lo), kt, kt == 0, kt == nk - 1)
                            else:
                                if u == UPG:
                                    pe.wait_ge(u2_ready, i * HT + (kt + 1))
                                last = tokens_out(n0 + u, local % RING, k, (u2_hi, u2_lo), kt, kt == 0, kt == nk - 1)
                        last.then_inc(slab_used, 1)
                        if first_step and u == 0:
                            for kt in range(KS * j + 4, min(KS * j + 4 + KS, KD)):
                                turn_x1(kt)

            def last_stage(i):
                u = UPG + DNG - 1
                pe.wait_ge(dve_freed, i * DNG + (d0 + u - 2 * UPG + 1))
                for tiles in TILE_ORDER:
                    for kt in range(HT):
                        local = UPG * SG + DS * (DNG - 1) + kt // KS
                        if tiles is TILE_ORDER[0]:
                            pe.wait_ge(lo_dve, i * STEP_SLABS + (MLP0 - PROJ_SLABS + local + 1))
                        last = tokens_out(n0 + u, local % RING, kt % KS, (u2_hi, u2_lo), kt, kt == 0, kt == HT - 1, tiles)
                    last.then_inc(tile_done, len(tiles))

            mlp_step(0, True)
            with pe.Fori(1, STEPS - 1) as i:
                mlp_step(i, False)
            mlp_step(STEPS - 1, False, UPG + DNG - 1)
            last_stage(STEPS - 1)

        @block.scalar
        def _(act):
            ch = Chain(act, act_chain)

            def split(s):
                act.wait_ge(raw_landed[s % RING], 16 * (s // RING + 1))
                if s >= RING:
                    act.wait_ge(slab_used, s - RING + 1)
                r, hi = raw[:, s % RING, :, :], w_hi[:, s % RING, :, :]
                if s < SG:
                    ch.link(nc.scalar.activation(hi[:, :, 0:64], r[:, :, 0:64], ACT.Copy))
                    r, hi = r[:, :, 0:192], hi[:, :, 64:256]
                nc.scalar.activation(hi, r, ACT.Copy).then_inc(hi_ready, 1)

            def done(name):
                wait_stage(act, name)

            def squares(src, dst, col):
                return nc.scalar.activation(dst, src, ACT.Square, accum_out=col)

            def evacuate(name, dst, n, banks):
                done(name)
                for b in banks:
                    ch.put(nc.scalar.activation(dst[:, 4 * n + b, :], bank(STAGE[name], b), ACT.Copy))
                ch.wait()
                act.sem_inc(act_freed, 1)

            def h_high(sub, k, src, dst):
                nc.scalar.activation(dst[:, k, :], src, ACT.Identity, bias=mod[:, (1, 4)[sub], k:k + 1],
                                     scale=mul[:, sub, k:k + 1]).then_inc(h_hi_ready, 1)

            act.dma_start(pos_ki[:], positions[0:1, :].to_broadcast([P, T])).then_inc(pos_in, 16)
            act.dma_start(pos_qi[0:TT, :], positions.rearrange("a (r p) -> (a r) p", p=P)).then_inc(pos_in, 16)
            act.wait_ge(consts, 1)
            for q in range(4):
                act.dma_start(rb[32 * q:32 * q + NBUCKET, :], rel_bias).then_inc(rb_in, 16)
                act.dma_start(rb_prev[32 * q + 1:32 * q + NBUCKET, :], rel_bias[0:NBUCKET - 1, :]).then_inc(rb_in, 16)
            act.wait_ge(c_copied, 1)
            nc.scalar.activation(c_tmp[:], c_col[:], ACT.Tanh, scale=0.5).then_inc(c_tanh, 1)
            act.wait_ge(consts, 2)

            def bias_store(k):
                act.wait_ge(act_chain, bias_at[k])
                act.dma_start(bias_s[P * k:P * k + P, :], bias_out[:, k % 4, :]).then_inc(bias_stored[k % 4], 16)

            bias_at = []
            xs = 0
            for m in range(8):
                done(f"bias{m}")
                for b in range(4):
                    k = 4 * m + b
                    if k >= 4:
                        act.wait_ge(bias_stored[k % 4], 16 * (k // 4))
                    bias_at.append(ch.put(nc.scalar.activation(bias_out[:, k % 4, :], bank(STAGE[f"bias{m}"], b), ACT.Copy)))
                    if b == 3:
                        ch.wait()
                        act.sem_inc(act_freed, 1)
                    bias_store(k)
                if m == 3:
                    act.wait_ge(vec_ready, 2)
                    nc.scalar.activation(lam_t[:, 1, :], lam_t[:, 0, :], ACT.Exp, scale=-1.0).then_inc(c_tanh, 1)
                t = m - 2
                if 0 <= t < TT:
                    act.wait_ge(x_landed[t], 16)
                    if t:
                        act.wait_ge(ssq_ready, t)
                    squares(x_tok[:, t, :], junk[:], stat[:, 0, t:t + 1]).then_inc(ssq_ready, 1)
                if t == TT - 1:
                    act.wait_ge(ssq_ready, TT)
                    nc.scalar.activation(stat[:, 1, 0:TT], stat[:, 0, 0:TT], ACT.Sqrt, bias=eps_c[:],
                                         scale=1.0 / D).then_inc(root_ready, 1)
            for n in range(TT):
                evacuate(f"xt{n}", x_t, n, (0, 1))
            s = 0
            split(0)
            split(1)
            act.wait_ge(mul_ready, 1)
            act.wait_ge(dve_freed, freed("D", STAGE["xt3"] + 1))
            for stored in bias_stored:
                act.wait_ge(stored, 16 * 8)
            s = 2
            for k in range(KD):
                h_high(0, k, x_t[:, k, :], h_hi)
                if k % KS == KS - 1:
                    split(s)
                    s += 1

            def split_to(s, upto):
                while s < upto:
                    split(s)
                    s += 1
                return s

            s = split_to(s, SG + 3)
            done("g0")
            n = STAGE["g0"]
            ch.put(nc.scalar.activation(ki_hi[0][0:ID, :], bank(n, 0)[0:ID, :], ACT.Copy))
            ch.wait()
            nc.scalar.activation(ki_hi[1][ID:P, :], bank(n, 0)[ID:P, :], ACT.Copy).then_inc(act_hi, 1)
            nc.scalar.activation(widx_t[0:IH, :], bank(n, 1)[0:IH, :], ACT.Copy).then_inc(widx_copied, 1)
            act.wait_ge(widx_copied, 1)
            act.wait_ge(act_hi, 1)
            act.sem_inc(act_freed, 1)
            for g in (1, 2):
                s = split_to(s, SG * (g + 1) + 3)
                done(f"g{g}")
                for b in range(4):
                    nc.scalar.activation(qi_hi[:, 4 * (g - 1) + b, :], bank(STAGE[f"g{g}"], b), ACT.Copy).then_inc(act_hi, 1)
                act.wait_ge(act_hi, 1 + 4 * g)
                act.sem_inc(act_freed, 1)
            for m in range(TT * IH // 4):
                done(f"dots{m}")
                for b in range(4):
                    k = 4 * m + b
                    if k >= 2:
                        act.wait_ge(relu_used, k - 1)
                    nc.scalar.activation(relu[:, k % 2, :], bank(STAGE[f"dots{m}"], b), ACT.Relu).then_inc(relu_ready, 1)
                act.wait_ge(relu_ready, 4 * m + 4)
                act.sem_inc(act_freed, 1)

            def copy_out(name, dst, scale=1.0):
                done(name)
                for b in range(4):
                    ch.put(nc.scalar.activation(dst(b), bank(STAGE[name], b), ACT.Copy, scale=scale))
                ch.wait()
                act.sem_inc(act_freed, 1)

            s = split_to(s, SG * 4 + 3)
            act.wait_ge(score_done, 1)
            copy_out("g3", lambda b: lru_in[:, b, :])
            act.sem_inc(branch_act, 1)
            s = split_to(s, SG * 5 + 3)
            copy_out("g4", lambda b: gate_in[:, b, :])
            act.sem_inc(branch_act, 1)
            for k, (name, dst) in enumerate((("rgate", r_t), ("igate", i_t))):
                done(name)
                for b in range(CT):
                    ch.put(nc.scalar.activation(dst[:, b, :], bank(STAGE[name], b), ACT.Tanh, bias=half_b[:, k, b:b + 1],
                                                scale=0.5))
                ch.wait()
                act.sem_inc(act_freed, 1)
            act.sem_inc(branch_act, 1)
            act.wait_ge(branch_dve, U_ARG)
            ch.link(nc.scalar.activation(i_t[:], r_t[:], ACT.Exp, scale=2.0))
            act.sem_inc(branch_act, 1)
            ch.link(nc.scalar.activation(r_t[:], r_t[:], ACT.Tanh))
            s = split_to(s, SG * 5 + 5)
            ch.link(nc.scalar.activation(lru_in[:], r_t[:], ACT.Sqrt, scale=-0.25))
            act.sem_inc(branch_act, 1)
            act.wait_ge(branch_dve, SCANNED)
            ch.link(nc.scalar.activation(i_t[:], gate_in[:], ACT.Square))
            act.sem_inc(branch_act, 1)
            s = split_to(s, SG * 6 + 3)
            act.wait_ge(branch_dve, GELU_ARG)
            ch.link(nc.scalar.activation(lru_in[:], i_t[:], ACT.Tanh, scale=float(np.sqrt(2 / np.pi))))
            act.sem_inc(branch_act, 1)
            act.wait_ge(branch_dve, LRU_DONE)
            copy_out("g5", lambda b: pool_u[:, b, PAD:])
            act.sem_inc(branch_act, 1)
            s = split_to(s, SG * 7 + 3)
            act.wait_ge(mod_step, MOD_EARLY + MOD_PROJ)
            copy_out("g6", lambda b: k_t[:, b, :])
            s = split_to(s, SG * 8 + 3)
            copy_out("g7", lambda b: k_t[:, 4 + b, :])
            act.wait_ge(dve_freed, freed("D", STAGE["mod4"] + 1))
            s = split_to(s, SG * 9 + 3)
            copy_out("g8", lambda b: q_t[:, b, :], scale=HD ** -0.5)
            s = split_to(s, SG * 10 + 3)
            copy_out("g9", lambda b: q_t[:, 4 + b, :], scale=HD ** -0.5)
            act.wait_ge(mask_done, TT)
            done("poolmm")
            n = STAGE["poolmm"]
            for b in range(CT):
                o = at_b["pool_scale"] + b
                ch.put(nc.scalar.activation(pool_o[:, b, :], bank(n, b), ACT.Copy, scale=col_b[:, o:o + 1]))
            ch.wait()
            act.sem_inc(act_freed, 1)
            nc.scalar.activation(pool_sq[:], pool_o[:], ACT.Square).then_inc(branch_act, 1)
            nc.scalar.activation(lru_sq[:], lru_o[:], ACT.Square).then_inc(branch_act, 1)
            def head_split(hd):
                if hd >= 2:
                    act.wait_ge(s_done, TT * (hd - 1))
                nc.scalar.activation(q_hi[:, hd % 2, :], q_t[:, hd, :], ACT.Copy).then_inc(qk_hi, 1)
                nc.scalar.activation(k_hi[:, hd % 2, :], k_t[:, hd, :], ACT.Copy).then_inc(qk_hi, 1)

            for g in (10, 11):
                s = split_to(s, SG * (g + 1) + 3)
                if g == 10:
                    done("ssq")
                done(f"g{g}")
                if g == 11:
                    head_split(0)
                    head_split(1)
                for b in range(TT):
                    c0 = 512 * (g - 10)
                    nc.scalar.activation(v_hi[:, b, c0:c0 + 512], bank(STAGE[f"g{g}"], b), ACT.Copy).then_inc(act_hi, 1)
                act.wait_ge(act_hi, 9 + 4 * (g - 9))
                act.sem_inc(act_freed, 1)
                if g == 10:
                    for b in range(2):
                        ch.put(nc.scalar.activation(rnorm[:, b, :], bank(STAGE["ssq"], b), ACT.Sqrt, bias=eps_c[:], scale=1.0 / GW))
                    ch.wait()
                    act.sem_inc(act_freed, 1)
                    act.sem_inc(root_ready, 1)

            def exps(it):
                act.wait_ge(max_ready, it + 1)
                j = it % PROB_SLOTS
                nc.scalar.activation(probs[:, j, :], probs[:, j, :], ACT.Exp, bias=nmax[:, j:j + 1], scale=-1.0,
                                     accum_out=asum[:, j:j + 1]).then_inc(exp_ready, 1)

            def pt_split(it):
                act.wait_ge(pt_done, it + 1)
                pair, half = divmod(it, 2)
                if pair >= 2:
                    act.wait_ge(pv_done, pair - 1)
                nc.scalar.activation(pt_hi[:, pair % 2, :, P * half:P * half + P],
                                     psum[:, PT_BANK[it % 2], :].rearrange("p (k q) -> p k q", k=TT), ACT.Copy).then_inc(pt_hi_ready, 1)

            def head_out(hd):
                act.wait_ge(pv_done, TT // 2 * (hd + 1))
                nc.scalar.activation(attn[:, hd, :], psum[:, O_BANK + hd % 2, :], ACT.Copy).then_inc(o_ready, 1)

            n_it = HEADS * TT
            for it in range(n_it + LAG_PV + 1):
                if 0 <= it - LAG_EXP < n_it:
                    exps(it - LAG_EXP)
                if 0 <= it - LAG_HI < n_it:
                    pt_split(it - LAG_HI)
                if it % TT == 1 and 2 <= it // TT + 1 < HEADS:
                    head_split(it // TT + 1)
                if it == TT:
                    s = split_to(s, PROJ_SLABS + RING)
                if it > LAG_PV and (it - LAG_PV) % TT == 0:
                    head_out((it - LAG_PV) // TT - 1)

            act.wait_ge(rinv_ready, 1)
            act.wait_ge(pt_lo_ready, HEADS * TT)
            act.wait_ge(pv_done, HEADS * TT // 2)
            for n in range(KD):
                k = out_tile(n)
                if n == 2:
                    act.wait_ge(sq_used, HEADS)
                    nc.scalar.activation(rnorm[:, 0, :], psum[:, SQ_BANK, :], ACT.Sqrt, bias=eps_c[:],
                                         scale=1.0 / AW).then_inc(root_ready, 1)
                if k < HEADS:
                    act.wait_ge(mixed_full, k + 1)
                    src = mixed[:, k, :]
                else:
                    src = pool_o[:, k - HEADS, :] if k < HEADS + CT else lru_o[:, k - HEADS - CT, :]
                nc.scalar.activation(m_hi[:, k, :], src, ACT.Copy).then_inc(mixed_hi, 1)
                if n % KS == KS - 1 and n >= 3:
                    s = split_to(s, s + 1)
            n0 = len(STAGES)

            def split_mlp(i, local):
                act.wait_ge(raw_landed[local % RING], i * (16 * STEP_SLABS // RING) + 16 * ((MLP0 + local) // RING + 1))
                act.wait_ge(slab_used, i * STEP_SLABS + (MLP0 + local - RING + 1))
                nc.scalar.activation(w_hi[:, local % RING, :, :], raw[:, local % RING, :, :], ACT.Copy).then_inc(hi_ready, 1)

            def x1_squares(t):
                act.wait_ge(x1_ready, t + 1)
                ch.link(squares(y1[:, t, :], slab_1[:], stat[:, 0, 4 + t:5 + t]))

            for d in range(TT):
                s = split_to(s, min(SG * (PROJ_GROUPS + d + 1) + 3, MLP0))
                if d < TT - 1:
                    done(f"out{d}")
                for t in range(TT):
                    k = TT * d + t
                    if d == TT - 1:
                        tile_finished(act, t)
                    if k:
                        act.wait_ge(out_squared, k)
                    squares(bank(STAGE[f"out{d}"], t), sq_out[:], stat[:, 3 + d, t:t + 1]).then_inc(out_squared, 1)
                    if d == TT - 1:
                        act.wait_ge(rinv_ready, 2 + t)
                        nc.scalar.activation(stat[:, 1, t:t + 1], stat[:, 0, t:t + 1], ACT.Sqrt, bias=eps_c[:],
                                             scale=1.0 / D).then_inc(root_ready, 1)
                        if t:
                            x1_squares(t - 1)
                act.wait_ge(out_squared, TT * d + TT)
                act.sem_inc(act_freed, 1)
            for local in (0, 1):
                split_mlp(0, local)
            x1_squares(TT - 1)
            nc.scalar.activation(stat[:, 1, 4:4 + TT], stat[:, 0, 4:4 + TT], ACT.Sqrt, bias=eps_c[:], scale=1.0 / D).then_inc(root_ready, 1)
            for local in (2, 3):
                split_mlp(0, local)
            act.wait_ge(mul_ready, 2)
            for k in range(KD):
                act.wait_ge(turned, k + 1)
                h_high(1, k, psum[:, 4 * TURN_HALF + k % 4, :], h2_hi)
                if k % KS == KS - 1 and k >= 3:
                    split_mlp(0, RING + (k - 3) // KS)

            def up_stage(i, u):
                act.wait_ge(slab_used, i * STEP_SLABS + (MLP0 + SG * (u + 1)))
                for b in range(4):
                    if not isinstance(i, int) or 4 * u + b >= 2:
                        act.wait_ge(up_used, i * HT + (4 * u + b - 1))
                    nc.scalar.activation(u_relu[:, b % 2, :], bank(n0 + u, b), ACT.Relu).then_inc(up_relu, 1)
                act.wait_ge(up_relu, i * HT + (4 * u + 4))
                act.sem_inc(act_freed, 1)

            def mlp_step(i, begin):
                for local in range(STEP_SLABS):
                    if local >= begin:
                        split_mlp(i, local)
                    if local in (SG + 2, 2 * SG + 2):
                        up_stage(i, (local - 2) // SG - 1)

            mlp_step(0, EARLY_SPLITS)
            with act.Fori(1, STEPS) as i:
                mlp_step(i, 0)
            for k in range(TT * DNG):
                d, t = divmod(k, TT)
                act.wait_ge(y2_done, k + 1)
                if k:
                    act.wait_ge(y2_squared, k)
                squares(y2[:, t, 512 * d:512 * d + 512], sq_out[:], stat[:, 3 + d, t:t + 1]).then_inc(y2_squared, 1)
                if d == DNG - 1:
                    act.wait_ge(rinv_ready, 6 + t)
                    nc.scalar.activation(stat[:, 1, t:t + 1], stat[:, 0, 8 + t:9 + t], ACT.Sqrt, bias=eps_c[:],
                                         scale=1.0 / D).then_inc(root_ready, 1)

        @block.vector
        def _(dve):
            ch = Chain(dve, dve_chain)
            V = nc.vector

            def done(name):
                wait_stage(dve, name)

            def free():
                ch.wait()
                dve.sem_inc(dve_freed, 1)

            def cols(table, name, n):
                tile, at_ = (col_a, at_a) if table == "a" else (col_b, at_b)
                return tile[:, at_[name]:at_[name] + n]

            def rsqrt(v_src, n, dst, scale, tmp, root=None):
                root = stat[:, 1, 0:n] if root is None else root
                v = stat[:, 7, 0:n]
                ch.link(V.tensor_scalar(v, v_src, scale, EPS, ALU.mult, ALU.add))
                ch.link(V.reciprocal(dst, root))
                ch.link(V.tensor_tensor(tmp, dst, dst, ALU.mult))
                ch.link(V.tensor_tensor(tmp, tmp, v, ALU.mult))
                ch.link(V.tensor_scalar(tmp, tmp, -0.5, 1.5, ALU.mult, ALU.add))
                ch.link(V.tensor_tensor(dst, dst, tmp, ALU.mult))

            done("c")
            ch.put(V.tensor_copy(c_col[:], bank(STAGE["c"], 0)[:, 0:KD]))
            free()
            dve.sem_inc(c_copied, 1)
            dve.wait_ge(c_tanh, 1)
            ch.link(V.scalar_tensor_tensor(c_act[:], c_tmp[:], 1.0, c_col[:], ALU.add, ALU.mult))
            ch.link(V.tensor_scalar(c_act[:], c_act[:], 0.5, None, ALU.mult))

            def mod_add(g):
                j, k = divmod(g, KD)
                acc = acc_b if j % 2 else acc_a
                slab, slot, turn = mod_slot(g)
                dve.wait_ge(mod_landed[slot], 16 * (turn + 1))
                if k == 0:
                    if j >= 2:
                        wait_stage(dve, f"mod{j - 2}")
                    V.tensor_scalar(acc[:], slab, c_act[:, k:k + 1], None, ALU.mult).then_inc(mod_step, 1)
                else:
                    dve.wait_ge(mod_step, g)
                    V.scalar_tensor_tensor(acc[:], slab, c_act[:, k:k + 1], acc[:], ALU.mult, ALU.add).then_inc(mod_step, 1)

            dve.wait_ge(pos_in, 32)
            ch.put(V.tensor_copy(pos_k[:], pos_ki[:]))
            V.tensor_copy(pos_qf[0:TT, :], pos_qi[0:TT, :]).then_inc(vec_ready, 1)
            mod_add(0)
            done("pos")
            ch.put(V.tensor_copy(pos_q[:], bank(STAGE["pos"], 0)[:, 0:TT]))
            ch.put(V.tensor_copy(start_col[:], bank(STAGE["pos"], 1)[:, 0:1]))
            free()
            for q in range(4):
                r32 = slice(32 * q, 32 * q + 32)
                ch.put(V.tensor_scalar(reach[r32, :], pos_k[r32, P * q:P * q + P], start_col[r32, :], None, ALU.subtract))
            ch.wait()
            dve.sem_inc(reach_ready, 1)

            def small_vectors():
                done("vec")
                n = STAGE["vec"]
                na, nb = sum(v.shape[0] for _, v in vec_a_rows), sum(v.shape[0] for _, v in vec_b_rows)
                ch.put(V.tensor_copy(col_a[:, 0:na], bank(n, 0)[:, 0:na]))
                ch.put(V.tensor_copy(col_b[:, 0:nb], bank(n, 1)[:, 0:nb]))
                free()
                lam = cols("b", "lam", CT)
                ch.link(V.tensor_scalar(lam_t[:, 2, :], lam, -1.0, None, ALU.mult))
                ch.link(V.tensor_tensor(lam_t[:, 0, :], lam_t[:, 2, :], lam, ALU.max))
                ch.link(V.tensor_scalar(lam_t[:, 2, :], lam_t[:, 2, :], 0.0, None, ALU.max))
                for k, name in enumerate(("r_b", "i_b")):
                    ch.put(V.tensor_scalar(half_b[:, k, :], cols("b", name, CT), 0.5, None, ALU.mult))
                ch.wait()
                dve.sem_inc(vec_ready, 1)

            e_, z, z2, sp_ = lam_t[:, 1, :], lam_t[:, 3, :], lam_t[:, 4, :], lam_t[:, 5, :]

            def softplus():
                dve.wait_ge(c_tanh, 2)
                ch.link(V.tensor_scalar(z, e_, 2.0, None, ALU.add))
                ch.link(V.reciprocal(z, z))
                ch.link(V.tensor_tensor(z, z, e_, ALU.mult))
                ch.link(V.tensor_tensor(z2, z, z, ALU.mult))
                ch.link(V.tensor_scalar(sp_, z2, 1.0 / 17, 1.0 / 15, ALU.mult, ALU.add))
                for odd in (13, 11, 9, 7, 5, 3, 1):
                    ch.link(V.tensor_tensor(sp_, sp_, z2, ALU.mult))
                    ch.link(V.tensor_scalar(sp_, sp_, 1.0 / odd, None, ALU.add))
                ch.link(V.tensor_tensor(sp_, sp_, z, ALU.mult))
                ch.link(V.scalar_tensor_tensor(sp_, sp_, 2.0, lam_t[:, 2, :], ALU.mult, ALU.add))
                ch.link(V.tensor_scalar(sp_, sp_, -LRU_C / 4, None, ALU.mult))

            def mod_out(j):
                done(f"mod{j}")
                table = "a" if f"b_mod{j}" in at_a else "b"
                ch.link(V.tensor_tensor(mod[:, j, :], bank(STAGE[f"mod{j}"], 0)[:, 0:KD], cols(table, f"b_mod{j}", KD), ALU.add))
                dve.sem_inc(dve_freed, 1)
                if j in (2, 5):
                    ch.link(V.tensor_tensor(mod[:, j, :], mod[:, j, :], cols("b", "g_post1" if j == 2 else "g_post2", KD), ALU.mult))
                    dve.sem_inc(gate_col, 1)
                if j in (0, 3):
                    k = j // 3
                    ch.link(V.scalar_tensor_tensor(mul[:, k, :], mod[:, j, :], 1.0, cols("a", f"g_pre{k + 1}", KD), ALU.add, ALU.mult))
                if j in (1, 4):
                    dve.sem_inc(mul_ready, 1)

            def evacuate(name, dst, n, banks):
                done(name)
                for b in banks:
                    ch.put(V.tensor_copy(dst[:, 4 * n + b, :], bank(STAGE[name], b)))
                free()

            def scaled_identity(first, end, at_):
                for t in range(first, end):
                    V.tensor_scalar(diag[:, t, :], ident[:], stat[:, 2, at_ + t:at_ + t + 1], None, ALU.mult).then_inc(diag_ready, 1)

            for g in range(MOD_EARLY):
                if g >= 1:
                    mod_add(g)
                if g == 6:
                    small_vectors()
                for k in range(16 * g // 3, min(16 * (g + 1) // 3, P)):
                    if not pool_makes(k):
                        if k >= 4:
                            dve.wait_ge(step_used, k - 3)
                        V.tensor_scalar(steps[:, k % 4, :], pos_k[:], reach[:, k:k + 1], None, ALU.is_le).then_inc(step_dve, 1)
                if g == 20:
                    softplus()
                if g == 25:
                    dve.wait_ge(root_ready, 1)
                    rsqrt(stat[:, 0, 0:TT], TT, stat[:, 2, 0:TT], 1.0 / D, stat[:, 2, 8:8 + TT])
                    scaled_identity(0, TT, 0)
                if g == 27:
                    mod_out(0)
                if g >= 28:
                    evacuate(f"xt{g - 28}", x_t, g - 28, (2, 3))

            def h_low(sub, k, src, hi, lo):
                ch.link(V.tensor_scalar(h_full[:, k % 2, :], src, mul[:, sub, k:k + 1], mod[:, (1, 4)[sub], k:k + 1],
                                        ALU.mult, ALU.add))
                V.tensor_tensor(lo[:, k, :], h_full[:, k % 2, :], hi[:, k, :].bitcast(F32), ALU.subtract).then_inc(h_ready, 1)

            mod_out(1)
            dve.wait_ge(act_freed, freed("A", STAGE["xt3"] + 1))
            for k in range(KD):
                dve.wait_ge(h_hi_ready, k + 1)
                h_low(0, k, x_t[:, k, :], h_hi, h_lo)

            def beside(s):
                if mod_beside(s) is not None:
                    mod_add(mod_beside(s))
                if TOPK_AT <= s < TOPK_AT + TT * ROUNDS // 2:
                    for r in (2 * (s - TOPK_AT), 2 * (s - TOPK_AT) + 1):
                        topk_round(*divmod(r, ROUNDS))

            def is_late(t):
                ch.link(V.tensor_scalar(late[:], pos_k[:], pos_q[:, t:t + 1], None, ALU.is_gt))

            def topk_round(t, r):
                ch.link(V.max(top8[:], score[:, t, :]))
                ch.link(V.match_replace(score[:, t, :], top8[:], score[:, t, :], TAKEN))
                if r == ROUNDS - 1:
                    is_late(t)
                    ch.link(V.scalar_tensor_tensor(score[:, t, :], score[:, t, :], TAKEN / 2, late[:], ALU.is_gt, ALU.max))
                    if t == 0:
                        wait_stage(dve, "igate")
                    V.tensor_scalar(mask[:, t, :], score[:, t, :], NEG, None, ALU.mult).then_inc(mask_done, 1)

            def beside_to(s, upto):
                while s < upto:
                    beside(s)
                    s += 1
                return s

            def low(dst, stage, b, hi, signal, n_hi):
                dve.wait_ge(act_hi, n_hi)
                V.tensor_tensor(dst, bank(stage, b), hi.bitcast(F32), ALU.subtract).then_inc(signal, 1)

            s = beside_to(0, SG + 3)
            done("g0")
            for k in (0, 1):
                for part in (ki_hi, ki_lo):
                    ch.put(V.memset(part[k][ID * (1 - k):ID * (1 - k) + ID, :].bitcast(F32), 0.0))
            ch.wait()
            dve.wait_ge(act_hi, 1)
            ch.link(V.tensor_tensor(ki_lo[0][0:ID, :], bank(STAGE["g0"], 0)[0:ID, :], ki_hi[0][0:ID, :].bitcast(F32), ALU.subtract))
            V.tensor_tensor(ki_lo[1][ID:P, :], bank(STAGE["g0"], 0)[ID:P, :], ki_hi[1][ID:P, :].bitcast(F32),
                            ALU.subtract).then_inc(idx_ready, 1)
            dve.wait_ge(idx_ready, 1)
            dve.sem_inc(dve_freed, 1)
            for g in (1, 2):
                s = beside_to(s, SG * (g + 1) + 3)
                done(f"g{g}")
                for b in range(4):
                    k = 4 * (g - 1) + b
                    low(qi_lo[:, k, :], STAGE[f"g{g}"], b, qi_hi[:, k, :], idx_ready, 2 + k)
                dve.wait_ge(idx_ready, 1 + 4 * g)
                dve.sem_inc(dve_freed, 1)
                if g == 1:
                    done("widx")
                    for t in range(TT):
                        ch.put(V.tensor_scalar(w_idx[:, t, :], bank(STAGE["widx"], 0)[:, IH * t:IH * t + IH], (IH * ID) ** -0.5, None,
                                               ALU.mult))
                    free()
            for k in range(TT * IH):
                t, hd = dots_of(k)
                if k % (2 * IH) == 0:
                    for u in (t, t + 1):
                        ch.put(V.tensor_scalar(score[:, u, :], pos_k[:], pos_q[:, u:u + 1], NEG, ALU.is_gt, ALU.mult))
                    ch.wait()
                dve.wait_ge(relu_ready, k + 1)
                if hd:
                    dve.wait_ge(relu_used, k - 1)
                V.scalar_tensor_tensor(score[:, t, :], relu[:, k % 2, :], w_idx[:, t, hd:hd + 1], score[:, t, :], ALU.mult,
                                       ALU.add).then_inc(relu_used, 1)
                if k % IH == IH - 1:
                    mod_add(MOD_EARLY + KD + k // IH)
            dve.wait_ge(relu_used, TT * IH)
            dve.sem_inc(score_done, 1)

            s = beside_to(s, SG * 4 + 3)
            dve.wait_ge(branch_act, 1)
            taps = cols("b", "conv_w", 4 * CT)
            for b in range(CT):
                tap = [taps[:, CT * j + b:CT * j + b + 1] for j in range(4)]
                ch.link(V.tensor_scalar(xc[:, b, :], lru_in[:, b, :], tap[3], cols("b", "conv_b", CT)[:, b:b + 1], ALU.mult, ALU.add))
                for j in (2, 1, 0):
                    w = 3 - j
                    ch.link(V.scalar_tensor_tensor(xc[:, b, w:], lru_in[:, b, :T - w], tap[j], xc[:, b, w:], ALU.mult, ALU.add))
            dve.sem_inc(branch_dve, 1)
            mod_out(2)
            s = beside_to(s, SG * 5)
            mod_out(3)
            s = beside_to(s, SG * 5 + 3)
            dve.wait_ge(branch_act, 3)
            for b in range(CT):
                ch.put(V.tensor_scalar(r_t[:, b, :], r_t[:, b, :], 1.0, sp_[:, b:b + 1], ALU.add, ALU.mult))
            ch.link(V.scalar_tensor_tensor(xc[:], i_t[:], 1.0, xc[:], ALU.add, ALU.mult))
            dve.sem_inc(branch_dve, 1)
            dve.wait_ge(branch_act, 4)
            ch.link(V.scalar_tensor_tensor(xc[:], i_t[:], 1.0, xc[:], ALU.add, ALU.mult))
            dve.wait_ge(branch_act, 5)
            ch.link(V.tensor_tensor(xc[:], xc[:], lru_in[:], ALU.mult))
            for b in range(CT):
                ch.put(V.tensor_tensor_scan(r_t[:, b, :], i_t[:, b, :], xc[:, b, :], 0.0, ALU.mult, ALU.add))
            ch.wait()
            dve.sem_inc(branch_dve, 1)
            s = beside_to(s, SG * 5 + 6)
            dve.wait_ge(branch_act, 6)
            ch.link(V.tensor_scalar(i_t[:], i_t[:], 0.044715, 1.0, ALU.mult, ALU.add))
            ch.link(V.tensor_tensor(i_t[:], i_t[:], gate_in[:], ALU.mult))
            dve.sem_inc(branch_dve, 1)
            s = beside_to(s, SG * 6)
            dve.wait_ge(branch_act, 7)
            ch.link(V.scalar_tensor_tensor(gate_in[:], lru_in[:], 1.0, gate_in[:], ALU.add, ALU.mult))
            wait_stage(dve, "mod3")
            ch.link(V.scalar_tensor_tensor(lru_o[:], r_t[:], 0.5, gate_in[:], ALU.mult, ALU.mult))
            dve.sem_inc(branch_dve, 1)
            s = beside_to(s, MOD_AGAIN + 2 * KD - TT)
            for t_ in (pool_u, pool_b, pool_c):
                ch.put(V.memset(t_[:, :, 0:PAD], 0.0))
            ch.wait()
            dve.wait_ge(branch_act, 8)
            src, dst, w = pool_u, pool_b, 1
            for b in range(CT):
                ch.link(V.tensor_tensor(dst[:, b:, PAD:], src[:, b:, PAD:], src[:, b:, PAD - w:PAD - w + T], ALU.add))
                src, dst, w = dst, (pool_c if dst is pool_b else pool_b), 2 * w
            for b in range(CT):
                win = 2 ** (b + 1)
                o = (pool_b, pool_c)[b % 2]
                ch.link(V.tensor_tensor(pool_fix[:, b, 0:win], o[:, b, PAD:PAD + win], inv_n[:, 0:win], ALU.mult))
                ch.link(V.scalar_tensor_tensor(o[:, b, PAD:], o[:, b, PAD:], 1.0 / win, pool_u[:, b, PAD:], ALU.mult, ALU.subtract))
                ch.link(V.tensor_tensor(o[:, b, PAD:PAD + win], pool_fix[:, b, 0:win], pool_u[:, b, PAD:PAD + win], ALU.subtract))
            dve.sem_inc(branch_dve, 1)
            mod_out(4)
            s = beside_to(s, TOPK_AT + TT * ROUNDS // 2)
            dve.wait_ge(branch_act, BRANCH_SQ)
            for n in (CT // 2, CT // 4):
                for sq in (pool_sq, lru_sq):
                    ch.put(V.tensor_tensor(sq[:, 0:n, :], sq[:, 0:n, :], sq[:, n:2 * n, :], ALU.add))
                ch.wait()
            dve.sem_inc(branch_dve, 1)
            def head_split(hd):
                dve.wait_ge(qk_hi, 2 * hd + 1)
                V.tensor_tensor(q_lo[:, hd, :], q_t[:, hd, :], q_hi[:, hd % 2, :].bitcast(F32), ALU.subtract).then_inc(q_lo_ready, 1)

            for g in (10, 11):
                done(f"g{g}")
                if g == 11:
                    head_split(0)
                    head_split(1)
                for b in range(TT):
                    c0 = 512 * (g - 10)
                    k = 4 * (g - 10) + b
                    low(v_lo[:, b, c0:c0 + 512], STAGE[f"g{g}"], b, v_hi[:, b, c0:c0 + 512], idx_ready, 10 + k)
                dve.wait_ge(idx_ready, 9 + 4 * (g - 9))
                dve.sem_inc(dve_freed, 1)
                if g == 10:
                    dve.wait_ge(root_ready, 2)
                    for k, (o, g) in enumerate(((pool_o, "g_pool"), (lru_o, "g_lru"))):
                        ch.link(V.reciprocal(rnorm[:, k, :], rnorm[:, k, :]))
                        for b in range(CT):
                            ch.put(V.scalar_tensor_tensor(o[:, b, :], o[:, b, :], cols("b", g, CT)[:, b:b + 1], rnorm[:, k, :],
                                                          ALU.mult, ALU.mult))
                    ch.wait()
                    dve.sem_inc(rinv_ready, 1)

            def split(s):
                dve.wait_ge(hi_ready, s + 1)
                V.tensor_tensor(w_lo[:, s % RING, :, :], raw[:, s % RING, :, :], w_hi[:, s % RING, :, :].bitcast(F32),
                                ALU.subtract).then_inc(lo_dve, 1)


            def logits(it):
                hd, t = divmod(it, TT)
                dve.wait_ge(bm_ready, it + 1)
                dve.wait_ge(s_done, it + 1)
                if it >= PROB_SLOTS:
                    dve.wait_ge(pt_done, it - PROB_SLOTS + 1)
                j = it % PROB_SLOTS
                V.tensor_tensor_reduce(out=probs[:, j, :], in0=psum[:, S_BANK + it % 3, :], in1=bm[:, it % BM_SLOTS, :], scale=-1.0,
                                       scalar=3e38, op0=ALU.add, op1=ALU.min, accum_out=nmax[:, j:j + 1]).then_inc(max_ready, 1)

            def normalise(it):
                j = it % PROB_SLOTS
                dve.wait_ge(exp_ready, it + 1)
                ch.link(V.reciprocal(arec[:, j:j + 1], asum[:, j:j + 1]))
                V.tensor_scalar(probs[:, j, :], probs[:, j, :], arec[:, j:j + 1], None, ALU.mult).then_inc(probs_ready, 1)

            def pt_split(it):
                dve.wait_ge(pt_hi_ready, it + 1)
                pair, half = divmod(it, 2)
                q = slice(P * half, P * half + P)
                V.tensor_tensor(pt_lo[:, pair % 2, :, q], psum[:, PT_BANK[it % 2], :].rearrange("p (k q) -> p k q", k=TT),
                                pt_hi[:, pair % 2, :, q].bitcast(F32), ALU.subtract).then_inc(pt_lo_ready, 1)

            n_it = HEADS * TT
            for it in range(n_it + LAG_LO):
                if it < n_it:
                    logits(it)
                if 0 <= it - LAG_NORM < n_it:
                    normalise(it - LAG_NORM)
                if 0 <= it - LAG_LO < n_it:
                    pt_split(it - LAG_LO)
                if it >= TT and it % TT == 0 and it // TT <= RING:
                    split(PROJ_SLABS + it // TT - 1)
                if it % TT == 2 and 2 <= it // TT + 1 < HEADS:
                    head_split(it // TT + 1)

            def mixed_low(n):
                k = out_tile(n)
                src = mixed[:, k, :] if k < HEADS else pool_o[:, k - HEADS, :] if k < HEADS + CT else lru_o[:, k - HEADS - CT, :]
                dve.wait_ge(mixed_hi, n + 1)
                V.tensor_tensor(m_lo[:, k, :], src, m_hi[:, k, :].bitcast(F32), ALU.subtract).then_inc(mixed_ready, 1)

            s = PROJ_SLABS + RING
            for n in range(KD + 1):
                if n == 4:
                    dve.wait_ge(root_ready, 3)
                    ch.link(V.reciprocal(rnorm[:, 0, :], rnorm[:, 0, :]))
                if n < KD and out_tile(n) < HEADS:
                    k = out_tile(n)
                    V.scalar_tensor_tensor(mixed[:, k, :], attn[:, k, :], cols("b", "g_attn", HEADS)[:, k:k + 1], rnorm[:, 0, :],
                                           ALU.mult, ALU.mult).then_inc(mixed_full, 1)
                if n >= 1:
                    if out_tile(n - 1) < HEADS:
                        dve.wait_ge(mixed_full, out_tile(n - 1) + 1)
                    mixed_low(n - 1)
                    if n % KS == 0 and n >= 4:
                        split(s)
                        s += 1

            def split_mlp(i, local):
                dve.wait_ge(hi_ready, i * STEP_SLABS + (MLP0 + local + 1))
                V.tensor_tensor(w_lo[:, local % RING, :, :], raw[:, local % RING, :, :],
                                w_hi[:, local % RING, :, :].bitcast(F32), ALU.subtract).then_inc(lo_dve, 1)

            g = 5 * KD
            for d in range(TT):
                while s < min(SG * (PROJ_GROUPS + d + 1) + 3, MLP0):
                    split(s)
                    if s >= PROJ_SLABS + SG and g < 6 * KD:
                        mod_add(g)
                        g += 1
                    s += 1
                if d < TT - 1:
                    done(f"out{d}")
                if d == 0:
                    dve.wait_ge(g_landed, 16)
                for t in range(TT):
                    dve.wait_ge(out_squared, TT * d + t + 1)
                    if d == TT - 1:
                        ch.link(V.tensor_reduce(stat[:, 0, t:t + 1], stat[:, 3:7, t:t + 1].rearrange("p d t -> p t d"), AXX, ALU.add))
                        dve.sem_inc(rinv_ready, 1)
                    ch.put(V.tensor_tensor(y1[:, t, 512 * d:512 * d + 512], bank(STAGE[f"out{d}"], t),
                                           g1_bc[:, 512 * d:512 * d + 512], ALU.mult))
                    if d == TT - 1:
                        dve.wait_ge(root_ready, 4 + t)
                        rsqrt(stat[:, 0, t:t + 1], 1, stat[:, 2, t:t + 1], 1.0 / D, stat[:, 2, 8:9], root=stat[:, 1, t:t + 1])
                        dve.wait_ge(x_again[t], 16)
                        V.scalar_tensor_tensor(y1[:, t, :], y1[:, t, :], stat[:, 2, t:t + 1], x_in[t][:], ALU.mult,
                                               ALU.add).then_inc(x1_ready, 1)
                free()
                if d == 2:
                    while g < 6 * KD:
                        mod_add(g)
                        g += 1
                    mod_out(5)
            for local in (0, 1):
                split_mlp(0, local)
            dve.wait_ge(root_ready, 8)
            rsqrt(stat[:, 0, 4:4 + TT], TT, stat[:, 2, 4:4 + TT], 1.0 / D, stat[:, 2, 12:12 + TT], root=stat[:, 1, 4:4 + TT])
            scaled_identity(0, TT, 4)
            for local in (2, 3):
                split_mlp(0, local)
            for k in range(KD):
                dve.wait_ge(h_hi_ready, KD + k + 1)
                h_low(1, k, psum[:, 4 * TURN_HALF + k % 4, :], h2_hi, h2_lo)
                dve.wait_ge(h_ready, KD + k + 1)
                dve.sem_inc(turned_used, 1)
                if k % KS == KS - 1 and k >= 3:
                    split_mlp(0, RING + (k - 3) // KS)

            n0, d0 = len(STAGES), freed("D", len(STAGES))

            c0 = ch.n

            def square_stage(i, u):
                for b in range(4):
                    k = 4 * u + b
                    dve.wait_ge(up_relu, i * HT + (k + 1))
                    if not isinstance(i, int) or k >= 2:
                        dve.wait_ge(u2_ready, i * HT + (k - 1))
                    V.tensor_tensor(u_sq[:, b % 2, :], u_relu[:, b % 2, :], u_relu[:, b % 2, :], ALU.mult).then_inc(up_used, 1)
                    dve.wait_ge(up_used, i * HT + (k + 1))
                    V.tensor_copy(u2_hi[:, k, :], u_sq[:, b % 2, :]).then_inc(dve_chain, 1)
                    dve.wait_ge(dve_chain, i * HT + (c0 + k + 1))
                    V.tensor_tensor(u2_lo[:, k, :], u_sq[:, b % 2, :], u2_hi[:, k, :].bitcast(F32), ALU.subtract).then_inc(u2_ready, 1)

            def add_stage(i, d, last_step=False):
                dve.wait_ge(slab_used, i * STEP_SLABS + (MLP0 + UPG * SG + DS * (d + 1)))
                for t in range(TT):
                    y = y2[:, t, 512 * d:512 * d + 512]
                    if isinstance(i, int) and i == 0:
                        if d == 0:
                            dve.wait_ge(turned, KD)
                            for stored in x1_stored:
                                dve.wait_ge(stored, 16)
                        last = V.tensor_copy(y, bank(n0 + UPG + d, t))
                    else:
                        last = V.tensor_tensor(y, y, bank(n0 + UPG + d, t), ALU.add)
                    if last_step:
                        last.then_inc(y2_done, 1)
                    elif t == TT - 1:
                        last.then_inc(dve_freed, 1)
                if last_step:
                    dve.wait_ge(y2_done, TT * d + TT)
                    dve.sem_inc(dve_freed, 1)

            def times_gate(d, t):
                c = slice(512 * d, 512 * d + 512)
                dve.wait_ge(y2_squared, TT * d + t + 1)
                ch.put(V.tensor_tensor(y2[:, t, c], y2[:, t, c], g2_bc[:, c], ALU.mult))

            def step(i, before, begin=0, last_step=False):
                for local in range(STEP_SLABS):
                    if local >= begin:
                        split_mlp(i, local)
                    if local == 2 and before is not None:
                        dve.wait_ge(y2_zero, 1)
                        add_stage(before, DNG - 1)
                    if local in (SG + 2, 2 * SG + 2):
                        square_stage(i, (local - 2) // SG - 1)
                    d, r = divmod(local - UPG * SG - DS - 2, DS)
                    if r == 0 and 0 <= d < DNG - 1:
                        add_stage(i, d, last_step)

            step(0, None, EARLY_SPLITS)
            with dve.Fori(1, STEPS - 1) as i:
                step(i, i - 1)
            step(STEPS - 1, STEPS - 2, last_step=True)
            ch.n = c0 + HT * STEPS
            dve.wait_ge(g_landed, 32)
            for d in range(DNG - 1):
                for t in range(TT):
                    times_gate(d, t)
            d = DNG - 1
            dve.wait_ge(x1_back, 16)
            for t in range(TT):
                dve.wait_ge(tile_done, TT - 1 + t + 1)
                y = y2[:, t, 512 * d:512 * d + 512]
                V.tensor_tensor(y, y, bank(n0 + UPG + d, t), ALU.add).then_inc(y2_done, 1)
                dve.wait_ge(y2_squared, TT * d + t + 1)
                ch.link(V.tensor_reduce(stat[:, 0, 8 + t:9 + t], stat[:, 3:7, t:t + 1].rearrange("p d t -> p t d"), AXX, ALU.add))
                dve.sem_inc(rinv_ready, 1)
                times_gate(d, t)
                dve.wait_ge(root_ready, 9 + t)
                rsqrt(stat[:, 0, 8 + t:9 + t], 1, stat[:, 2, t:t + 1], 1.0 / D, stat[:, 2, 8 + t:9 + t], root=stat[:, 1, t:t + 1])
                for half in (slice(0, D // 2), slice(D // 2, D)):
                    V.scalar_tensor_tensor(x1_in[:, t, half], y2[:, t, half], stat[:, 2, t:t + 1], x1_in[:, t, half], ALU.mult,
                                           ALU.add).then_inc(final_ready, 1)


INPUTS = ["x", "c", "positions", "rel_bias", "w_mod", "b_mod", "g_pre_mix", "g_post_mix", "g_pre_mlp", "g_post_mlp",
          "w_in", "pool_w", "pool_scale", "conv_w", "conv_b", "gate_r_w", "gate_r_b", "gate_i_w", "gate_i_b",
          "lru_lambda", "g_attn_out", "g_pool_out", "g_lru_out", "w_out", "w_mlp_up", "w_mlp_down"]


def kernel(**inputs):
    import concourse.bacc as bacc
    from concourse.bass_utils import run_bass_kernel_spmd

    nc = bacc.Bacc("TRN2", target_bir_lowering=False, num_devices=1)
    arrays, args = {}, []
    for name in INPUTS:
        a = np.ascontiguousarray(inputs[name])
        arrays[f"in_{name}"] = a
        args.append(nc.dram_tensor(f"in_{name}", a.shape, mybir.dt.from_np(a.dtype), kind="ExternalInput").ap())
    args.append(nc.dram_tensor("out_x", (1, T, D), F32, kind="ExternalOutput").ap())
    build(nc, *args)
    r = run_bass_kernel_spmd(nc, [arrays], core_ids=[0])
    return r.results[0]["out_x"]
```
